# Optimizing a Trainium2 kernel written in Bass

```python
import jax, jax.numpy as jnp
from jax import lax
import numpy as np

D_MODEL = 1024
BATCH = 1
SEQ = 128
DEPTH = 2
DEC_BATCH = 1
DEC_SEQ = 512
PAST_LEN = 128

GRID_W = 64
HEAD_DIM = 64
N_Q_HEADS = 4
N_KV_HEADS = 2
Q_PER_KV = N_Q_HEADS // N_KV_HEADS
WINDOW = 128
BLOCK = 128
ROPE_BASE = 10000.0
ATTN_WIDTH = N_Q_HEADS * HEAD_DIM
KV_WIDTH = N_KV_HEADS * HEAD_DIM
CONV_CH = 256
RWKV_HEADS = 4
RWKV_WIDTH = RWKV_HEADS * HEAD_DIM
DECAY_RANK = 32
ICLR_RANK = 32
GATE_RANK = 64
FOURIER_GROUPS = 4
FOURIER_WIDTH = FOURIER_GROUPS * HEAD_DIM
MIX_WIDTH = ATTN_WIDTH + CONV_CH + RWKV_WIDTH + FOURIER_WIDTH
IN_SPLITS = (ATTN_WIDTH, KV_WIDTH, KV_WIDTH,
             CONV_CH, CONV_CH, CONV_CH,
             RWKV_WIDTH, RWKV_WIDTH, RWKV_WIDTH, 2 * DECAY_RANK, 2 * ICLR_RANK, GATE_RANK,
             FOURIER_WIDTH)
IN_WIDTH = sum(IN_SPLITS)
D_FF = 2816
N_EXPERTS = 8
TOP_K = 2
D_FF_EXPERT = 1024
N_DENSE = (DEPTH + 1) // 2
N_MOE = DEPTH // 2
NORM_EPS = 1e-6
GN_EPS = 64e-5
NEG_INF = -1e30

kernel_name = 'hybrid_diffusion_step'

def rms_norm(x, w):
    xf = x.astype(jnp.float32)
    y = xf * lax.rsqrt(jnp.mean(xf * xf, axis=-1, keepdims=True) + NORM_EPS)
    return (y * w.astype(jnp.float32)).astype(x.dtype)

def modulate(h, shift, scale):
    return h * (1.0 + scale) + shift

def axial_rope_tables(n_tokens):
    n_rows = n_tokens // GRID_W
    row = jnp.repeat(jnp.arange(n_rows), GRID_W).astype(jnp.float32)
    col = jnp.tile(jnp.arange(GRID_W), n_rows).astype(jnp.float32)
    quarter = HEAD_DIM // 4
    inv_freq = ROPE_BASE ** (-jnp.arange(quarter, dtype=jnp.float32) / quarter)
    ang = jnp.stack([row[:, None] * inv_freq, col[:, None] * inv_freq], axis=1)
    return jnp.cos(ang), jnp.sin(ang)

def apply_rope(x, cos, sin):
    n_head_axes = x.ndim - 3
    shp = (cos.shape[0],) + (1,) * n_head_axes + cos.shape[1:]
    cos, sin = cos.reshape(shp), sin.reshape(shp)
    xr = x.reshape(x.shape[:-1] + (2, 2, HEAD_DIM // 4))
    x1, x2 = xr[..., 0, :], xr[..., 1, :]
    out = jnp.stack([x1 * cos - x2 * sin, x2 * cos + x1 * sin], axis=-2)
    return out.reshape(x.shape).astype(x.dtype)

def softmax_with_sink(logits, sink):
    s = sink.astype(jnp.float32).reshape((1, N_KV_HEADS, Q_PER_KV) + (1,) * (logits.ndim - 3))
    s = jnp.broadcast_to(s, logits.shape[:-1] + (1,))
    return jax.nn.softmax(jnp.concatenate([logits, s], axis=-1), axis=-1)[..., :-1]

def context_attention(q, k, v, sink):
    B, L = q.shape[:2]
    logits = jnp.einsum('bqhgd,bkhd->bhgqk', q, k).astype(jnp.float32) * HEAD_DIM ** -0.5
    p = softmax_with_sink(logits, sink)
    out = jnp.einsum('bhgqk,bkhd->bqhgd', p.astype(v.dtype), v)
    return out.reshape(B, L, ATTN_WIDTH)

def latent_attention(q, k, v, k_ctx, v_ctx, sink):
    B, T = q.shape[:2]
    nb = T // BLOCK
    qb = q.reshape(B, nb, BLOCK, N_KV_HEADS, Q_PER_KV, HEAD_DIM)

    def band(x):
        xp = jnp.pad(x, ((0, 0), (BLOCK, BLOCK), (0, 0), (0, 0))).reshape(B, nb + 2, BLOCK, N_KV_HEADS, HEAD_DIM)
        return jnp.concatenate([xp[:, :-2], xp[:, 1:-1], xp[:, 2:]], axis=2)

    kw, vw = band(k), band(v)
    q_pos = jnp.arange(T).reshape(nb, BLOCK)
    k_pos = (jnp.arange(nb)[:, None] - 1) * BLOCK + jnp.arange(3 * BLOCK)[None, :]
    kp = k_pos[:, None, :]
    valid = (jnp.abs(q_pos[:, :, None] - kp) <= WINDOW) & (kp >= 0) & (kp < T)
    scale = HEAD_DIM ** -0.5
    lw = jnp.einsum('bnqhgd,bnkhd->bhgnqk', qb, kw).astype(jnp.float32) * scale
    lw = jnp.where(valid, lw, NEG_INF)
    lc = jnp.einsum('bnqhgd,bchd->bhgnqc', qb, k_ctx).astype(jnp.float32) * scale
    p = softmax_with_sink(jnp.concatenate([lw, lc], axis=-1), sink)
    pw, pc = p[..., :3 * BLOCK], p[..., 3 * BLOCK:]
    out = (jnp.einsum('bhgnqk,bnkhd->bnqhgd', pw.astype(v.dtype), vw)
           + jnp.einsum('bhgnqc,bchd->bnqhgd', pc.astype(v_ctx.dtype), v_ctx))
    return out.reshape(B, T, ATTN_WIDTH)

def short_conv(x_in, b_gate, c_gate, conv_w):
    u = c_gate * x_in
    up = jnp.pad(u, ((0, 0), (1, 1), (0, 0)))
    y = conv_w[0] * up[:, :-2] + conv_w[1] * up[:, 1:-1] + conv_w[2] * up[:, 2:]
    return b_gate * y

def fourier_mix(u):
    B, T, _ = u.shape
    ug = u.reshape(B, T, FOURIER_GROUPS, HEAD_DIM).astype(jnp.float32)
    y = jnp.fft.fft2(ug, axes=(1, 3), norm='ortho').real
    return y.astype(u.dtype).reshape(B, T, FOURIER_WIDTH)

def wkv_scan(s0, r, w, k, v, z, b, reverse):
    xs = tuple(jnp.moveaxis(t, 1, 0) for t in (r, w, k, v, z, b))

    def step(S, inp):
        r_t, w_t, k_t, v_t, z_t, b_t = inp
        sz = jnp.einsum('bhvk,bhk->bhv', S, z_t)
        S = S * w_t[:, :, None, :] + sz[..., None] * b_t[:, :, None, :] + v_t[..., None] * k_t[:, :, None, :]
        return S, jnp.einsum('bhvk,bhk->bhv', S, r_t)

    s_fin, ys = lax.scan(step, s0, xs, reverse=reverse)
    return jnp.moveaxis(ys, 0, 1), s_fin

def rwkv_mixer(r, k, v, wd, ad, gd, p, s0):
    B, T, _ = r.shape
    f32 = jnp.float32

    def heads(t):
        return t.reshape(t.shape[:-1] + (RWKV_HEADS, HEAD_DIM))

    dec = p['w0'] + jnp.einsum('btjr,jrc->btjc', jnp.tanh(wd.reshape(B, T, 2, DECAY_RANK)), p['w_up'])
    w = jnp.exp(-jnp.exp(-jax.nn.softplus(-dec.astype(f32)) - 0.5))
    a = jax.nn.sigmoid((p['a0'] + jnp.einsum('btjr,jrc->btjc', ad.reshape(B, T, 2, ICLR_RANK), p['a_up'])).astype(f32))
    g = jnp.einsum('btr,rc->btc', jax.nn.sigmoid(gd), p['g_up']).astype(f32)
    rf, kf, vf = r.astype(f32), k.astype(f32), v.astype(f32)
    kk = heads(kf * p['k_k'].astype(f32))
    kk = kk / jnp.maximum(jnp.sqrt(jnp.sum(kk * kk, axis=-1, keepdims=True)), 1e-12)
    k_dir = kf[:, :, None, :] * (1.0 + (a - 1.0) * p['k_a'].astype(f32))
    b_dir = kk.reshape(B, T, 1, RWKV_WIDTH) * a
    s0 = s0.astype(f32)
    rh, vh = heads(rf), heads(vf)
    y_f, s_f = wkv_scan(s0[:, 0], rh, heads(w[:, :, 0]), heads(k_dir[:, :, 0]), vh, -kk, heads(b_dir[:, :, 0]), False)
    y_b, s_b = wkv_scan(s0[:, 1], rh, heads(w[:, :, 1]), heads(k_dir[:, :, 1]), vh, -kk, heads(b_dir[:, :, 1]), True)
    y = y_f + y_b
    mu = jnp.mean(y, axis=-1, keepdims=True)
    var = jnp.mean(jnp.square(y - mu), axis=-1, keepdims=True)
    y = (y - mu) * lax.rsqrt(var + GN_EPS) * heads(p['ln_w'].astype(f32)) + heads(p['ln_b'].astype(f32))
    bonus = jnp.sum(rh * heads(kf) * p['r_k'].astype(f32), axis=-1, keepdims=True) * vh
    out = ((y + bonus).reshape(B, T, RWKV_WIDTH) * g).astype(r.dtype)
    return out, jnp.stack([s_f, s_b], axis=1)

def token_mixers(h, p, rope=None, ctx=None):
    B, T, _ = h.shape
    proj = jnp.einsum('btd,dn->btn', h, p['w_in'])
    offsets = [int(i) for i in np.cumsum(IN_SPLITS)[:-1]]
    (aq, ak, av, bx, bb, bc, cr, ck, cv, cwd, cad, cgd, dx) = jnp.split(proj, offsets, axis=-1)
    q = rms_norm(aq.reshape(B, T, N_KV_HEADS, Q_PER_KV, HEAD_DIM), p['q_norm'])
    k = rms_norm(ak.reshape(B, T, N_KV_HEADS, HEAD_DIM), p['k_norm'])
    v = av.reshape(B, T, N_KV_HEADS, HEAD_DIM)
    if ctx is None:
        attn = context_attention(q, k, v, p['sink'])
        s0 = jnp.zeros((B, 2, RWKV_HEADS, HEAD_DIM, HEAD_DIM), jnp.float32)
    else:
        k_ctx, v_ctx, s0 = ctx
        cos, sin = rope
        attn = latent_attention(apply_rope(q, cos, sin), apply_rope(k, cos, sin), v, k_ctx, v_ctx, p['sink'])
    conv = short_conv(bx, bb, bc, p['conv_w'])
    rw, s_fin = rwkv_mixer(cr, ck, cv, cwd, cad, cgd, p, s0)
    four = fourier_mix(dx)
    out = jnp.einsum('btc,cd->btd', jnp.concatenate([attn, conv, rw, four], axis=-1), p['w_out'])
    if ctx is None:
        return out, (k, v, s_fin)
    return out, None

def swiglu(h, w1, w3, w2):
    return jnp.einsum('btf,fd->btd', jax.nn.silu(jnp.einsum('btd,df->btf', h, w1)) * jnp.einsum('btd,df->btf', h, w3), w2)

def moe_swiglu(h, router_w, w1, w3, w2):
    logits = jnp.einsum('btd,de->bte', h, router_w).astype(jnp.float32)
    probs = jax.nn.softmax(logits, axis=-1)
    top_p, top_i = lax.top_k(probs, TOP_K)
    top_p = top_p / jnp.sum(top_p, axis=-1, keepdims=True)
    gates = jnp.sum(jax.nn.one_hot(top_i, N_EXPERTS, dtype=jnp.float32) * top_p[..., None], axis=-2)
    gates = gates.astype(h.dtype)
    y = jnp.zeros_like(h)
    for e in range(N_EXPERTS):
        y = y + gates[..., e:e + 1] * swiglu(h, w1[e], w3[e], w2[e])
    return y

def setup_inputs(seed: int = 0) -> dict:
    key = jax.random.key(seed)
    ks = iter(jax.random.split(key, 48))
    D = D_MODEL

    def nrm(shape, scale=1.0):
        return jax.random.normal(next(ks), shape, jnp.float32) * scale

    return {
        'x_prompt': nrm((BATCH, SEQ, D)),
        'x_sample': nrm((DEC_BATCH, DEC_SEQ, D)),
        'cache_k': nrm((DEC_BATCH, DEPTH, PAST_LEN, N_KV_HEADS, HEAD_DIM)),
        'cache_v': nrm((DEC_BATCH, DEPTH, PAST_LEN, N_KV_HEADS, HEAD_DIM)),
        'state_wkv': nrm((DEC_BATCH, DEPTH, 2, RWKV_HEADS, HEAD_DIM, HEAD_DIM), 0.3),
        'c': nrm((DEC_BATCH, D)),
        'c_ctx': nrm((D,)),
        'mod_w': nrm((DEPTH, D, 6 * D), 0.5 * D ** -0.5),
        'mod_b': nrm((DEPTH, 6 * D), 0.02),
        'norm1_w': 1.0 + nrm((DEPTH, D), 0.05),
        'norm2_w': 1.0 + nrm((DEPTH, D), 0.05),
        'w_in': nrm((DEPTH, D, IN_WIDTH), D ** -0.5),
        'q_norm_w': 1.0 + nrm((DEPTH, HEAD_DIM), 0.05),
        'k_norm_w': 1.0 + nrm((DEPTH, HEAD_DIM), 0.05),
        'attn_sink': nrm((DEPTH, N_Q_HEADS), 0.5),
        'conv_w': nrm((DEPTH, 3, CONV_CH), 3 ** -0.5),
        'rwkv_w0': nrm((DEPTH, 2, RWKV_WIDTH)),
        'rwkv_w_up': nrm((DEPTH, 2, DECAY_RANK, RWKV_WIDTH), 0.5 * DECAY_RANK ** -0.5),
        'rwkv_a0': nrm((DEPTH, 2, RWKV_WIDTH), 0.5),
        'rwkv_a_up': nrm((DEPTH, 2, ICLR_RANK, RWKV_WIDTH), 0.5 * ICLR_RANK ** -0.5),
        'rwkv_g_up': nrm((DEPTH, GATE_RANK, RWKV_WIDTH), GATE_RANK ** -0.5),
        'rwkv_k_k': 0.85 + nrm((DEPTH, RWKV_WIDTH), 0.05),
        'rwkv_k_a': 1.0 + nrm((DEPTH, RWKV_WIDTH), 0.05),
        'rwkv_r_k': nrm((DEPTH, RWKV_HEADS, HEAD_DIM), 0.1),
        'rwkv_ln_w': 1.0 + nrm((DEPTH, RWKV_WIDTH), 0.05),
        'rwkv_ln_b': nrm((DEPTH, RWKV_WIDTH), 0.02),
        'w_out': nrm((DEPTH, MIX_WIDTH, D), MIX_WIDTH ** -0.5),
        'ffn_w1': nrm((N_DENSE, D, D_FF), D ** -0.5),
        'ffn_w3': nrm((N_DENSE, D, D_FF), D ** -0.5),
        'ffn_w2': nrm((N_DENSE, D_FF, D), D_FF ** -0.5),
        'router_w': nrm((N_MOE, D, N_EXPERTS), D ** -0.5),
        'moe_w1': nrm((N_MOE, N_EXPERTS, D, D_FF_EXPERT), D ** -0.5),
        'moe_w3': nrm((N_MOE, N_EXPERTS, D, D_FF_EXPERT), D ** -0.5),
        'moe_w2': nrm((N_MOE, N_EXPERTS, D_FF_EXPERT, D), D_FF_EXPERT ** -0.5),
    }

def reference(x_prompt, x_sample, cache_k, cache_v, state_wkv, c, c_ctx, mod_w, mod_b, norm1_w, norm2_w,
              w_in, q_norm_w, k_norm_w, attn_sink, conv_w, rwkv_w0, rwkv_w_up, rwkv_a0, rwkv_a_up, rwkv_g_up,
              rwkv_k_k, rwkv_k_a, rwkv_r_k, rwkv_ln_w, rwkv_ln_b, w_out, ffn_w1, ffn_w3, ffn_w2,
              router_w, moe_w1, moe_w3, moe_w2):
    rope = axial_rope_tables(x_sample.shape[1])
    xp, xs = x_prompt, x_sample
    new_k, new_v, new_s = [], [], []
    for l in range(DEPTH):
        p = {'w_in': w_in[l], 'q_norm': q_norm_w[l], 'k_norm': k_norm_w[l], 'sink': attn_sink[l],
             'conv_w': conv_w[l], 'w0': rwkv_w0[l], 'w_up': rwkv_w_up[l], 'a0': rwkv_a0[l],
             'a_up': rwkv_a_up[l], 'g_up': rwkv_g_up[l], 'k_k': rwkv_k_k[l], 'k_a': rwkv_k_a[l],
             'r_k': rwkv_r_k[l], 'ln_w': rwkv_ln_w[l], 'ln_b': rwkv_ln_b[l], 'w_out': w_out[l]}
        mp = jnp.split(jax.nn.silu(c_ctx) @ mod_w[l] + mod_b[l], 6, axis=-1)
        ms = jnp.split((jax.nn.silu(c) @ mod_w[l] + mod_b[l])[:, None, :], 6, axis=-1)
        out_p, (kc, vc, sc) = token_mixers(modulate(rms_norm(xp, norm1_w[l]), mp[0], mp[1]), p)
        xp = xp + mp[2] * out_p
        out_s, _ = token_mixers(modulate(rms_norm(xs, norm1_w[l]), ms[0], ms[1]), p, rope=rope,
                                ctx=(cache_k[:, l], cache_v[:, l], state_wkv[:, l]))
        xs = xs + ms[2] * out_s
        new_k.append(kc)
        new_v.append(vc)
        new_s.append(sc.astype(x_prompt.dtype))
        hp = modulate(rms_norm(xp, norm2_w[l]), mp[3], mp[4])
        hs = modulate(rms_norm(xs, norm2_w[l]), ms[3], ms[4])
        j = l // 2
        if l % 2 == 0:
            fp = swiglu(hp, ffn_w1[j], ffn_w3[j], ffn_w2[j])
            fs = swiglu(hs, ffn_w1[j], ffn_w3[j], ffn_w2[j])
        else:
            fp = moe_swiglu(hp, router_w[j], moe_w1[j], moe_w3[j], moe_w2[j])
            fs = moe_swiglu(hs, router_w[j], moe_w1[j], moe_w3[j], moe_w2[j])
        xp = xp + mp[5] * fp
        xs = xs + ms[5] * fs
    return (xp, xs, jnp.stack(new_k, axis=1), jnp.stack(new_v, axis=1), jnp.stack(new_s, axis=1))


_drawn_inputs = setup_inputs


def setup_inputs(seed=0):
    import zlib

    import numpy as np

    out = dict(_drawn_inputs(seed))
    spreads = {}
    factors = {'cache_k': 4.272,
     'cache_v': 3.135,
     'state_wkv': 6.927,
     'q_norm_w': 8.0,
     'attn_sink': 64.0,
     'rwkv_k_k': 29.562,
     'rwkv_ln_w': 5.775,
     'rwkv_ln_b': 15.745}
    for name, (base, spread) in spreads.items():
        noise = np.random.default_rng([zlib.crc32(name.encode()), seed]).standard_normal(out[name].shape)
        drawn = base * np.exp(spread * noise) if base else spread * noise
        out[name] = __import__('jax').numpy.asarray(drawn.astype(out[name].dtype))
    for name, factor in factors.items():
        out[name] = (out[name] * factor).astype(out[name].dtype)
    return out
```

```python
from contextlib import ExitStack

import numpy as np

import concourse.bass as bass
from concourse import mybir

F32 = mybir.dt.float32
ACT = mybir.ActivationFunctionType
ALU = mybir.AluOpType
AXX = mybir.AxisListType.X

P = 128
D = 1024
KT = D // P
DEPTH = 2
CTX, LAT = 128, 512
TOK = CTX + LAT
NT = TOK // P
HALF = TOK // 2
SEGS = ((0, 0, CTX), (1, CTX, TOK))
HD = 64
NQ, NKV = 4, 2
CH = 64
GRID_W = 64
IN_W = 2496
DFF = 2816
NE = 8
DFE = 1024
EPS = 1e-6
GN_EPS = 64e-5
LOG_DECAY = -float(np.exp(-0.5))
BANKS = 8

ROWS = [("mod_b", 48), ("norm1", 8), ("norm2", 8), ("conv", 6), ("w0", 4), ("a0", 4),
        ("k_k", 2), ("k_a", 2), ("r_k", 2), ("ln_w", 2), ("ln_b", 2), ("c_ctx", 8), ("c", 8)]
ROW = {}
_n = 0
for _name, _k in ROWS:
    ROW[_name] = _n
    _n += _k
NROWS = _n

CONSTS = [("ident", 128), ("ones", 128), ("blk", 128), ("band", 512), ("mzr", 512), ("m16", 256),
          ("m32", 256), ("m64", 256), ("cos", 128), ("sin", 128), ("dft64", 256), ("dft128", 256),
          ("scan", 128), ("rank", 8), ("eps", 2)]
CC = {}
_n = 0
for _name, _k in CONSTS:
    CC[_name] = _n
    _n += _k
NCONST = _n

IN_TILES = [
    (("r", 0), 0, 0), (("r", 1), 0, 128), (("k", 0), 0, 256), (("k", 1), 0, 384),
    (("v", 0), 1, 0), (("v", 1), 1, 128), (("wa", 0), 1, 256), (("gd", 0), 1, 384),
    (("bx", 0), 3, 0), (("bx", 1), 3, 128), (("bb", 0), 3, 256), (("bb", 1), 3, 384),
    (("bc", 0), 4, 0), (("bc", 1), 4, 128), (("f", 0), 4, 256), (("f", 1), 4, 384)]
RW_TILES, CF_TILES = IN_TILES[:8], IN_TILES[8:]

MOD_ITEMS = 12
SLOT = (DFF // P) * 256
MIX_ITEMS = MOD_ITEMS + 5 + 1 + 2
DENSE_UP = DFF // 256
DENSE_ITEMS = DENSE_UP + 4
EXP_UP = DFE // 256
EXP_ITEMS = EXP_UP + 2

STEPS = [("c", 0, d) for d in range(2)] + [("s", i, d) for d in range(2) for i in range(4)]


def step_tile(step):
    kind, i, d = step
    return 0 if kind == "c" else (1 + i if d == 0 else 4 - i)


def key_blocks(j):
    if j == 0:
        return [(1, 0)]
    return ([(0, j - 1)] if j > 1 else []) + [(1, j), (2, None)] + ([(3, j + 1)] if j < NT - 1 else [])


def constants():
    c = np.zeros((P, NCONST), np.float32)
    i = np.arange(P)[:, None]
    j = np.arange(P)[None, :]

    def put(name, a, at=0):
        c[:, CC[name] + at:CC[name] + at + a.shape[1]] = a

    put("ident", np.eye(P))
    put("ones", np.ones((P, P)))
    put("blk", (i // HD == j // HD).astype(np.float32))
    put("band", np.where(j >= i, 0.0, -1e30))
    put("band", np.where(j <= i, 0.0, -1e30), 384)
    for d in range(2):
        before = (i < j) if d == 0 else (i > j)
        same = lambda n: i // n == j // n
        put("mzr", (before & same(CH)).astype(np.float32), 256 * d)
        put("mzr", ((before | (i == j)) & same(CH)).astype(np.float32), 256 * d + 128)
        put("m16", (before & same(16)).astype(np.float32), 128 * d)
        put("m32", (before & same(32) & ~same(16)).astype(np.float32), 128 * d)
        put("m64", (before & same(64) & ~same(32)).astype(np.float32), 128 * d)
    inv = 10000.0 ** (-np.arange(16, dtype=np.float32) / 16)
    t = np.arange(LAT)
    ang = np.stack([(t // GRID_W)[:, None] * inv, (t % GRID_W)[:, None] * inv], 1).astype(np.float32)
    for name, fn in (("cos", np.cos), ("sin", np.sin)):
        put(name, fn(ang).reshape(4, P, 32).transpose(1, 0, 2).reshape(P, 128))
    e = np.arange(HD)
    a64 = 2 * np.pi * ((e[:, None] * e[None, :]) % HD) / HD
    for g in range(2):
        s = slice(g * HD, (g + 1) * HD)
        c[s, CC["dft64"] + g * HD:CC["dft64"] + (g + 1) * HD] = np.cos(a64) / 8
        c[s, CC["dft64"] + 128 + g * HD:CC["dft64"] + 128 + (g + 1) * HD] = -np.sin(a64) / 8
    a128 = 2 * np.pi * ((i * j) % P) / P
    put("dft128", np.cos(a128) / np.sqrt(P))
    put("dft128", np.sin(a128) / np.sqrt(P), 128)
    put("scan", np.broadcast_to((j % CH != 0), (P, P)).astype(np.float32))
    put("rank", np.broadcast_to(NE - np.arange(NE), (P, NE)).astype(np.float32))
    put("eps", np.full((P, 1), EPS), 0)
    put("eps", np.full((P, 1), GN_EPS), 1)
    u = np.arange(LAT)
    a512 = 2 * np.pi * ((u[:, None] * u[None, :]) % LAT) / LAT
    dft = np.stack([np.cos(a512), np.sin(a512)]) / np.sqrt(LAT)
    return c, dft.astype(np.float32)


class Order:

    def __init__(self, filled, emptied):
        self.filled, self.emptied = filled, emptied
        self.at, self.by, self.count = {}, [], {k: [] for k in emptied}
        self.next = 0

    def add(self, name, engine):
        self.at[name] = len(self.by)
        self.count[engine].append(len(self.by))
        self.by.append(engine)

    def bank(self, name):
        return self.at[name] % BANKS

    def wait_filled(self, eng, name):
        eng.wait_ge(self.filled, self.at[name] + 1)

    def wait_emptied(self, eng, name):
        n = self.at[name]
        e = self.by[n]
        eng.wait_ge(self.emptied[e], self.count[e].index(n) + 1)

    def open(self, pe, name):
        n = self.at[name]
        assert n == self.next, (name, n, self.next)
        self.next += 1
        if n >= BANKS:
            e = self.by[n - BANKS]
            pe.wait_ge(self.emptied[e], self.count[e].index(n - BANKS) + 1)
        return n % BANKS


class Chain:

    def __init__(self, eng, sem):
        self.eng, self.sem, self.n = eng, sem, 0

    def did(self, ins):
        ins.then_inc(self.sem, 1)
        self.n += 1

    def settle(self):
        self.eng.wait_ge(self.sem, self.n)


def list_groups(order):
    for j in range(NT):
        for q in range(2):
            order.add(("x", j, q), "AV"[q])
    for l in range(DEPTH):
        order.add(("params", l), "V")
        order.add(("mod", l), "V")
        for h in range(2):
            order.add(("ss1", l, h), "A")
        for (name, _, _) in RW_TILES:
            for h in range(2):
                order.add(("in", l, name, h), "A" if name[0] in ("wa", "gd") else "AV"[h])
        for j in range(NT):
            order.add(("qkv", l, j), "AV"[j % 2])
        for (name, _, _) in CF_TILES:
            for h in range(2):
                order.add(("in", l, name, h), "AV"[h])
        for j in range(NT):
            order.add(("vt", l, j), "A")
        for kind in range(2):
            for d in range(2):
                for ct in range(2):
                    for h in range(2):
                        order.add(("up", l, kind, d, ct, h), "A")
        for ct in range(2):
            for h in range(2):
                order.add(("kks", l, ct, h), "A")
        for ct in range(2):
            for h in range(2):
                order.add(("bonus", l, ct, h), "V")
        order.add(("ckt", l), "V")
        for j in range(NT):
            order.add(("qt", l, j), "V")
        for j in range(NT):
            for h in range(NQ):
                order.add(("qk", l, j, h), "V")
            for h in range(NQ):
                order.add(("pt", l, j, h), "AV"[h % 2])
            order.add(("pv", l, j), "V")
            order.add(("ot", l, j), "A")
        for j in range(NT):
            order.add(("f1", l, j), "AV"[j % 2])
        order.add(("f2c", l), "A")
        for ct in range(2):
            order.add(("f2", l, ct), "AV"[ct])
        for step in STEPS:
            if step[:2] == ("s", 0):
                order.add(("si", l, step[2]), "V")
            for name, engine in (("ab", "V"), ("ak", "V"), ("dd", "V"), ("tz", "A"), ("tb", "A"),
                                 ("n2", "A"), ("d2", "A"), ("akv", "V"), ("x2", "V"), ("n4", "A"), ("d4", "A"),
                                 ("x4", "V"), ("d8", "A"), ("x8", "V"), ("x8t", "A"), ("g1", "A"),
                                 ("y1", "V"), ("y1t", "A"), ("g2", "A"), ("y2", "V"), ("wp", "A"),
                                 ("rh", "V"), ("mt", "V"), ("s0", "V"), ("s1", "V"), ("yy", "V")):
                for hp in range(2):
                    order.add((name, l, step, hp), engine)
            if step[0] == "c":
                order.add(("so", l, step[2]), "V")
        for ct in range(2):
            for h in range(2):
                order.add(("mu", l, ct, h), "V")
        for ct in range(2):
            for h in range(2):
                order.add(("var", l, ct, h), "A")
        for ct in range(2):
            for h in range(2):
                order.add(("gup", l, ct, h), "V")
        for dt in range(KT):
            for h in range(2):
                order.add(("out", l, dt, h), "V")
        for h in range(2):
            order.add(("ss2", l, h), "A")
        if l == 1:
            order.add(("router", l), "V")
    for j in range(NT):
        for q in range(2):
            order.add(("y", j, q), "AV"[q])


def build(nc, a, outs):
    y_prompt, y_sample, new_k, new_v, new_s = outs
    with ExitStack() as ctx:
        def sb(name, cols):
            return ctx.enter_context(nc.sbuf_tensor(name, [P, cols], F32))

        def sem(name):
            return ctx.enter_context(nc.semaphore(name))

        def view(t, at, *dims):
            n = int(np.prod(dims))
            v = t[:, at:at + n]
            if len(dims) == 1:
                return v
            names = "abcde"[:len(dims)]
            spec = f"p ({' '.join(names)}) -> p {' '.join(names)}"
            return v.rearrange(spec, **{x: int(s) for x, s in zip(names[:-1], dims[:-1])})

        const = sb("const", NCONST)
        xT = view(sb("x_resid", KT * TOK), 0, KT, TOK)
        par_t = sb("params", NROWS + 96 + 16 + 32 + 132 + 256 + 64 + 240 + 96)
        at = [0]

        def small(*dims):
            v = view(par_t, at[0], *dims)
            at[0] += int(np.prod(dims))
            return v

        cst = lambda name, n, off=0: const[:, CC[name] + off:CC[name] + off + n]
        ident, ones, blk = cst("ident", P), cst("ones", P), cst("blk", P)

        par = small(NROWS)
        mod = small(48, 2)
        silu_c = small(KT, 2)
        amul = small(KT, 2)
        qnw = small(HD)
        knw = small(HD)
        sink = small(NQ)
        g_up = small(256)
        router_w = small(KT, NE)
        rt_l, rt_key, rt_first, rt_second, gates, rt_t = (small(NT, NE) for _ in range(6))
        stat = small(96)

        HT, GG, RING = 0, KT * TOK, KT * TOK + (DFF // P) * TOK
        SPARE = RING + 4 * SLOT
        arena = sb("arena", SPARE + 3 * TOK)
        hT = view(arena, HT, KT, TOK)
        x_tok = view(arena, HT, NT, D)
        par_rows = view(arena, GG, P)
        gT = view(arena, GG, DFF // P, TOK)
        rs = view(arena, GG + 5120, TOK)
        slot = lambda n: RING + (n % 4) * SLOT
        sil = view(arena, SPARE, 2, TOK)
        gbc = view(arena, SPARE + 2 * TOK, TOK)

        mixT = view(arena, GG, KT, TOK)
        rank_up = view(arena, GG + 4 * TOK, 4, 256)
        yT = mixT[:, 4:6, :]
        T1, T2, T3 = GG + 5120, RING + 2 * SLOT, HT
        rT = view(arena, T1, 2, TOK)
        kT_ = view(arena, T1 + 1280, 2, TOK)
        vT = view(arena, T1 + 2560, 2, TOK)
        kkT = view(arena, T1 + 3840, 2, TOK)
        v_tok = view(arena, T1 + 5120, NT, 4, HD)
        waT = view(arena, T1 + 6400, TOK)
        gdT = view(arena, T1 + 7040, TOK)
        tmp = view(arena, T1 + 7680, 2, TOK)
        bxT = view(arena, T2, 2, TOK)
        bbT = view(arena, T2 + 1280, 2, TOK)
        bcT = view(arena, T2 + 2560, 2, TOK)
        lw = view(arena, T2, 2, 2, TOK)
        aT = view(arena, T2 + 2560, 2, 2, TOK)
        T2b = T2 + 5120
        qkv = view(arena, T2b, NT, 512)
        fT = view(arena, T2b + 2560, 2, TOK)
        qT = view(arena, T3, 2, TOK)
        kT = view(arena, T3 + 1280, TOK)
        ck_tok = view(arena, T3 + 1920, P)
        cv_tok = view(arena, T3 + 2048, P)
        ckT = view(arena, T3 + 2176, P)
        sc = view(arena, T3 + 2304, NQ, 512)
        qk_sq = view(arena, T3 + 2304, NT, 384)
        qk_t = view(arena, T3 + 2304, 2, 6, HD)
        rope = view(arena, T3 + 3072, 4, 6, 2, 16)
        conv_u = view(arena, SPARE, 2, TOK + 4)
        o_tok = view(arena, T3 + 4352, 4, HD)
        v1 = view(arena, T3 + 2304, NT, 2, 256)
        pT = [view(arena, SPARE + 512 * h, 4, P) for h in range(3)] + [view(arena, T3 + 4608, 4, P)]
        s0_in = view(arena, T1 + 7680, 2, 2, P)
        s_fin = view(arena, T1 + 7680 + 512, 2, 2, P)

        free = [(T2b, T2 + 2 * SLOT), (T3, T3 + 5120), (SPARE, SPARE + 1920)]

        def wk(*dims):
            n = int(np.prod(dims))
            for i, (lo, hi) in enumerate(free):
                if hi - lo >= n:
                    free[i] = (lo + n, hi)
                    return view(arena, lo, *dims)
            raise ValueError("no room")

        AB, AK = wk(2, 2, 256), wk(2, 2, 256)
        EX = [wk(2, 3, P) for _ in range(2)]
        ST = wk(2, 3, P)
        DD, ND, D2, N2, O32, O64, XA, XB = (wk(2, 2, P) for _ in range(8))
        RR, WP = wk(2, 2, P), wk(2, 2, P)
        BP, KP = wk(2, 2, P), wk(2, 2, P)
        BM = wk(2, 2, P)
        BC, KC = wk(2, 2, P), wk(2, 2, P)
        BT, KD, RH = wk(2, P), wk(2, P), wk(2, P)
        att = view(par_t, at[0] - 96, 2, 24)
        qk_ss = view(par_t, at[0] - 48, NT * 6)
        LC = view(par_t, at[0] - 18, 2, 2, 2)
        omka = view(par_t, at[0] - 10, 2)

        psum = [ctx.enter_context(nc.psum_tensor(f"bank{i}", [P, 512], F32)) for i in range(BANKS)]

        filled = sem("bank_filled")
        emptied = {"A": sem("emptied_by_scalar"), "V": sem("emptied_by_vector")}
        order = Order(filled, emptied)
        list_groups(order)

        s_const, s_x, s_par = sem("const_in"), sem("x_in"), sem("params_in")
        s_ring = [sem(f"ring_in{i}") for i in range(4)]
        s_moditem = sem("mod_item_used")
        s_rank, s_gup_in, s_cache, s_state = sem("rank_weights_in"), sem("small_weights_in"), sem("cache_in"), sem("state_in")
        s_zero = sem("buffers_zeroed")
        s_silc, s_sq, s_hmul, s_h = sem("silu_c_ready"), sem("squares_ready"), sem("h_scaled"), sem("h_ready")
        s_kkr, s_kq, s_rk = sem("kk_raw"), sem("kk_squared"), sem("rk_ready")
        s_qsq, s_qss, s_qrt, s_qk, s_rope = (sem("qk_squares"), sem("qk_sumsq"), sem("qk_root"), sem("qk_normed"),
                                             sem("qk_roped"))
        s_max, s_exp = sem("row_max_ready"), sem("exp_done")
        s_cu, s_conv = sem("conv_gated"), sem("conv_done")
        s_sum, s_ex, s_pad, s_tri = sem("decay_sums"), sem("decay_exp"), sem("scaled_ready"), sem("triangles_ready")
        s_st0 = sem("state_zeroed")
        s_nkk = sem("kk_normed")
        s_gn, s_gsq = sem("y_centred"), sem("y_squared")
        s_kv_out, s_state_out, s_y_out = sem("kv_stored"), sem("states_stored"), sem("y_stored")
        s_fup, s_ffree, s_silu = sem("ffn_filled"), sem("ffn_emptied"), sem("silu_done")
        s_rmax, s_rexp, s_gate = sem("router_max"), sem("router_exp"), sem("gates_ready")
        s_gbc, s_gbcf = sem("gate_rows_filled"), sem("gate_rows_copied")
        s_ca, s_cv, s_cp = sem("scalar_chain"), sem("vector_chain"), sem("pool_chain")

        block = ctx.enter_context(nc.Block())

        items = []
        for l in range(DEPTH):
            for i in range(MOD_ITEMS):
                items.append(("mod", l, i))
            for i in range(5):
                items.append(("win", l, i))
            items.append(("dft", l, 0))
            for i in range(2):
                items.append(("wout", l, i))
            if l == 0:
                for i in range(DENSE_UP):
                    items.append(("up", l, 0, i))
                for i in range(4):
                    items.append(("down", l, 0, i))
            else:
                for e in range(NE):
                    for i in range(EXP_UP):
                        items.append(("up", l, e, i))
                    for i in range(2):
                        items.append(("down", l, e, i))
        number = {it: n for n, it in enumerate(items)}
        slots, loads, last = [], [], {}
        before, seen, k = [], [0] * 4, 0
        for n, it in enumerate(items):
            if it[0] in ("up", "down"):
                s = (k + 2) % 4
                k += 1
            else:
                s = (number[it] - number[("mod", it[1], 0)]) % 2
                k = 0
            slots.append(s)
            seen[s] += 32
            loads.append(seen[s])
            before.append(last.get(s))
            last[s] = n

        def item(name):
            return RING + slots[number[name]] * SLOT

        def wait_item(eng, name):
            eng.wait_ge(s_ring[slots[number[name]]], loads[number[name]])

        def ffn_shape(l, e):
            return (0, DFF // P, 2) if l == 0 else (DFF // P + 4 + e * (DFE // P + 4), DFE // P, 4)

        FFN_SETS = [ffn_shape(1, 0)[0], ffn_shape(1, NE)[0]]

        def wait_used(sp, name):
            kind, l = name[:2]
            if kind == "mod":
                if name[2] < MOD_ITEMS - 1:
                    sp.wait_ge(s_moditem, l * (MOD_ITEMS - 1) + name[2] + 1)
                else:
                    order.wait_filled(sp, ("mod", l))
            elif kind == "win":
                i = name[2]
                if i == 2:
                    order.wait_filled(sp, ("qkv", l, NT - 1))
                else:
                    order.wait_filled(sp, ("in", l, [t for t in IN_TILES if t[1] == i][-1][0], 1))
            elif kind == "dft":
                order.wait_filled(sp, ("f2", l, 1))
            elif kind == "wout":
                order.wait_filled(sp, ("out", l, 4 * name[2] + 3, 1))
            else:
                base, nf, per = ffn_shape(l, name[2])
                i = name[3]
                sp.wait_ge(s_fup, base + 2 * (i + 1) if kind == "up" else base + nf + (i + 1) * per // 2)

        @block.sync
        def _(sp):
            sp.dma_start(const[:], a["const"]).then_inc(s_const, 16)
            sp.dma_start(x_tok[:, 0, :], a["x_prompt"][0]).then_inc(s_x, 16)
            sp.dma_start(x_tok[:, 1:NT, :], a["x_sample"][0].rearrange("(j p) n -> p j n", p=P)).then_inc(s_x, 16)

            def load(name):
                n = number[name]
                if before[n] is not None:
                    wait_used(sp, items[before[n]])
                kind, l = name[:2]
                s, base = slots[n], item(name)
                if kind == "mod":
                    w = view(arena, base, KT, 512)
                    src = a["mod_w"][l].rearrange("(k p) n -> p k n", p=P)[:, :, 512 * name[2]:512 * (name[2] + 1)]
                    pieces = [(w[:, 4 * i:4 * i + 4, :], src[:, 4 * i:4 * i + 4, :]) for i in range(2)]
                elif kind == "win":
                    i = name[2]
                    src = a["w_in"][l].rearrange("(k p) n -> p k n", p=P)
                    if i < 4:
                        lo, n_ = [(1280, 512), (1792, 448), (0, 512), (512, 512)][i]
                        w = view(arena, base, KT, n_)
                        pieces = [(w[:, 4 * q:4 * q + 4, :], src[:, 4 * q:4 * q + 4, lo:lo + n_]) for q in range(2)]
                    else:
                        w = view(arena, base, KT, 512)
                        pieces = [(w[:, :, 0:256], src[:, :, 1024:1280]), (w[:, :, 256:512], src[:, :, 2240:2496])]
                elif kind == "dft":
                    w = view(arena, base, 2, 4, 512)
                    pieces = [(w[:, i], a["dft"][i].rearrange("(j p) n -> p j n", p=P)) for i in range(2)]
                elif kind == "wout":
                    i = name[2]
                    w = view(arena, base, KT, 512)
                    src = a["w_out"][l].rearrange("(k p) n -> p k n", p=P)[:, :, 512 * i:512 * (i + 1)]
                    pieces = [(w[:, 4 * q:4 * q + 4, :], src[:, 4 * q:4 * q + 4, :]) for q in range(2)]
                elif kind == "up":
                    _, _, e, i = name
                    w = view(arena, base, 2, KT, 256)
                    srcs = (a["ffn_w1"][0], a["ffn_w3"][0]) if l == 0 else (a["moe_w1"][0, e], a["moe_w3"][0, e])
                    pieces = [(w[:, q], srcs[q].rearrange("(k p) n -> p k n", p=P)[:, :, 256 * i:256 * (i + 1)])
                              for q in range(2)]
                else:
                    _, _, e, i = name
                    src = a["ffn_w2"][0] if l == 0 else a["moe_w2"][0, e]
                    nf, cols = (DFF // P, 256) if l == 0 else (DFE // P, 512)
                    w = view(arena, base, nf, cols)
                    src = src.rearrange("(k p) n -> p k n", p=P)[:, :, cols * i:cols * (i + 1)]
                    pieces = [(w[:, :nf // 2], src[:, :nf // 2]), (w[:, nf // 2:], src[:, nf // 2:])]
                for dst, src in pieces:
                    sp.dma_start(dst, src).then_inc(s_ring[s], 16)

            for l in range(DEPTH):
                if l > 0:
                    sp.wait_ge(s_fup, FFN_SETS[0])
                vec = [("mod_b", a["mod_b"][l].rearrange("(r p) -> r p", p=P)),
                       ("norm1", a["norm1_w"][l].rearrange("(r p) -> r p", p=P)),
                       ("norm2", a["norm2_w"][l].rearrange("(r p) -> r p", p=P)),
                       ("conv", a["conv_w"][l].rearrange("t (r p) -> (t r) p", p=P)),
                       ("w0", a["rwkv_w0"][l].rearrange("d (r p) -> (d r) p", p=P)),
                       ("a0", a["rwkv_a0"][l].rearrange("d (r p) -> (d r) p", p=P)),
                       ("k_k", a["rwkv_k_k"][l].rearrange("(r p) -> r p", p=P)),
                       ("k_a", a["rwkv_k_a"][l].rearrange("(r p) -> r p", p=P)),
                       ("r_k", a["rwkv_r_k"][l].rearrange("(r q) p -> r (q p)", q=2)),
                       ("ln_w", a["rwkv_ln_w"][l].rearrange("(r p) -> r p", p=P)),
                       ("ln_b", a["rwkv_ln_b"][l].rearrange("(r p) -> r p", p=P)),
                       ("c_ctx", a["c_ctx"].rearrange("(r p) -> r p", p=P)),
                       ("c", a["c"][0].rearrange("(r p) -> r p", p=P))]
                for name, src in vec:
                    n = src.shape[0]
                    sp.dma_start(par_rows[ROW[name]:ROW[name] + n, :], src).then_inc(s_par, 16)
                load(("mod", l, 0))
                load(("mod", l, 1))
                sp.wait_ge(s_zero, 2 * l + 1)
                for d in range(2):
                    sp.dma_start(rank_up[32 * d:32 * d + 32, d, :], a["rwkv_w_up"][l, d]).then_inc(s_rank, 16)
                    sp.dma_start(rank_up[64 + 32 * d:96 + 32 * d, 2 + d, :], a["rwkv_a_up"][l, d]).then_inc(s_rank, 16)
                sp.dma_start(g_up[0:64, :], a["rwkv_g_up"][l]).then_inc(s_gup_in, 16)
                sp.dma_start(qnw, a["q_norm_w"][l][None, :].broadcast_to([P, HD])).then_inc(s_gup_in, 16)
                sp.dma_start(knw, a["k_norm_w"][l][None, :].broadcast_to([P, HD])).then_inc(s_gup_in, 16)
                sp.dma_start(sink, a["attn_sink"][l][None, :].broadcast_to([P, NQ])).then_inc(s_gup_in, 16)
                sp.dma_start(router_w, a["router_w"][0].rearrange("(k p) e -> p k e", p=P)).then_inc(s_gup_in, 16)
                for i in range(2, MOD_ITEMS):
                    load(("mod", l, i))
                for i in range(5):
                    load(("win", l, i))
                order.wait_filled(sp, ("in", l, CF_TILES[-1][0], 1))
                sp.dma_start(ck_tok, a["cache_k"][0, l].rearrange("t h d -> t (h d)")).then_inc(s_cache, 16)
                sp.dma_start(cv_tok, a["cache_v"][0, l].rearrange("t h d -> t (h d)")).then_inc(s_cache, 16)
                load(("dft", l, 0))
                load(("wout", l, 0))
                load(("wout", l, 1))
                order.wait_emptied(sp, ("yy", l, STEPS[-1], 1))
                for it in items:
                    if it[1] == l and it[0] in ("up", "down"):
                        load(it)
            for j in range(NT):
                for q in range(2):
                    order.wait_emptied(sp, ("y", j, q))
                dst = y_prompt[0] if j == 0 else y_sample[0, P * (j - 1):P * j, :]
                sp.dma_start(dst, x_tok[:, j, :]).then_inc(s_y_out, 16)
            sp.wait_ge(s_y_out, 16 * NT)
            sp.wait_ge(s_kv_out, DEPTH * 2 * 16)
            sp.wait_ge(s_state_out, DEPTH * 8 * 16)

        @block.tensor
        def _(pe):
            mm, tr = nc.tensor.matmul, nc.tensor.transpose

            def end(ins):
                ins.then_inc(filled, 1)

            pe.wait_ge(s_const, 16)
            pe.wait_ge(s_x, 32)
            for j in range(NT):
                for q in range(2):
                    b = psum[order.open(pe, ("x", j, q))]
                    for k in range(4):
                        ins = tr(b[:, P * k:P * k + P], x_tok[:, j, P * (4 * q + k):P * (4 * q + k) + P], ident)
                    end(ins)

            def sum_squares(name, l, nth):
                pe.wait_ge(s_sq, nth)
                for h in range(2):
                    b = psum[order.open(pe, (name, l, h))]
                    for k in range(KT):
                        ins = mm(b[:, 0:HALF], ones, hT[:, k, HALF * h:HALF * (h + 1)], start=(k == 0), stop=(k == KT - 1))
                    end(ins)

            def in_tiles(l, tiles):
                at_item = None
                for name, it, col in tiles:
                    if it != at_item:
                        at_item = it
                        wait_item(pe, ("win", l, it))
                    width = {1: 448}.get(it, 512)
                    w = view(arena, item(("win", l, it)), KT, width)
                    m = 64 if name[0] == "gd" else P
                    for h in range(2):
                        b = psum[order.open(pe, ("in", l, name, h))]
                        for k in range(KT):
                            ins = mm(b[0:m, 0:HALF], w[:, k, col:col + m], hT[:, k, HALF * h:HALF * (h + 1)],
                                     start=(k == 0), stop=(k == KT - 1))
                        end(ins)

            def ffn(l, e, base, F, nd):
                nf = F // P
                gb = (e % 2) * (DFE // P)
                n = base
                for i in range(nf // 2):
                    wait_item(pe, ("up", l, e, i))
                    w = view(arena, item(("up", l, e, i)), 2, KT, 256)
                    for f in range(2):
                        if n >= 2:
                            pe.wait_ge(s_ffree, n - 1)
                        for q in range(2):
                            for h in range(2):
                                b = psum[4 * (n % 2) + 2 * q + h]
                                for k in range(KT):
                                    ins = mm(b[:, 0:HALF], w[:, q, k, P * f:P * f + P],
                                             hT[:, k, HALF * h:HALF * (h + 1)], start=(k == 0), stop=(k == KT - 1))
                        ins.then_inc(s_fup, 1)
                        n += 1
                pe.wait_ge(s_ffree, n)
                per = KT // nd
                for i in range(nd):
                    wait_item(pe, ("down", l, e, i))
                    w = view(arena, item(("down", l, e, i)), nf, P * per)
                    for dt in range(per):
                        if dt % 2 == 0 and n >= 2:
                            pe.wait_ge(s_ffree, n - 1)
                        for h in range(2):
                            b = psum[4 * (n % 2) + 2 * (dt % 2) + h]
                            for f in range(nf):
                                ins = mm(b[:, 0:HALF], w[:, f, P * dt:P * dt + P],
                                         gT[:, gb + f, HALF * h:HALF * (h + 1)], start=(f == 0), stop=(f == nf - 1))
                        if dt % 2 == 1:
                            ins.then_inc(s_fup, 1)
                            n += 1
                return n

            fn = 0
            for l in range(DEPTH):
                if l > 0:
                    pe.wait_ge(s_ffree, FFN_SETS[l - 1])
                pe.wait_ge(s_par, (l + 1) * 16 * len(ROWS))
                b = psum[order.open(pe, ("params", l))]
                end(tr(b[:, 0:NROWS], par_rows[0:NROWS, :], ident[0:NROWS, 0:NROWS]))
                pe.wait_ge(s_silc, l + 1)
                b = psum[order.open(pe, ("mod", l))]
                for i in range(MOD_ITEMS):
                    wait_item(pe, ("mod", l, i))
                    w = view(arena, item(("mod", l, i)), KT, 512)
                    for t in range(4):
                        c0 = 2 * (4 * i + t)
                        for k in range(KT):
                            ins = mm(b[:, c0:c0 + 2], w[:, k, P * t:P * t + P], silu_c[:, k, :],
                                     start=(k == 0), stop=(k == KT - 1))
                    if i < MOD_ITEMS - 1:
                        ins.then_inc(s_moditem, 1)
                    else:
                        end(ins)
                sum_squares("ss1", l, 2 * l + 1)
                pe.wait_ge(s_h, 2 * l + 1)
                in_tiles(l, RW_TILES)
                wait_item(pe, ("win", l, 2))
                w = view(arena, item(("win", l, 2)), KT, 512)
                for j in range(NT):
                    b = psum[order.open(pe, ("qkv", l, j))]
                    for k in range(KT):
                        ins = mm(b[:, :], hT[:, k, P * j:P * j + P], w[:, k, :], start=(k == 0), stop=(k == KT - 1))
                    end(ins)
                in_tiles(l, CF_TILES)
                for ct in range(2):
                    for h in range(2):
                        order.wait_emptied(pe, ("in", l, ("v", ct), h))
                for j in range(NT):
                    b = psum[order.open(pe, ("vt", l, j))]
                    for ct in range(2):
                        ins = tr(b[:, P * ct:P * ct + P], vT[:, ct, P * j:P * j + P], ident)
                    end(ins)
                pe.wait_ge(s_rank, 16 * 4 * (l + 1))
                for h in range(2):
                    order.wait_emptied(pe, ("in", l, ("wa", 0), h))
                for kind in range(2):
                    for d in range(2):
                        for ct in range(2):
                            for h in range(2):
                                b = psum[order.open(pe, ("up", l, kind, d, ct, h))]
                                end(mm(b[:, 0:HALF], rank_up[:, 2 * kind + d, P * ct:P * ct + P],
                                       waT[:, HALF * h:HALF * (h + 1)], start=True, stop=True))
                pe.wait_ge(s_kq, l + 1)
                for ct in range(2):
                    for h in range(2):
                        b = psum[order.open(pe, ("kks", l, ct, h))]
                        end(mm(b[:, 0:HALF], blk, tmp[:, ct, HALF * h:HALF * (h + 1)], start=True, stop=True))
                pe.wait_ge(s_rk, l + 1)
                for ct in range(2):
                    for h in range(2):
                        b = psum[order.open(pe, ("bonus", l, ct, h))]
                        end(mm(b[:, 0:HALF], blk, tmp[:, ct, HALF * h:HALF * (h + 1)], start=True, stop=True))
                pe.wait_ge(s_cache, 32 * (l + 1))
                b = psum[order.open(pe, ("ckt", l))]
                end(tr(b[:, 0:P], ck_tok, ident))
                for j in range(NT):
                    if j == 0:
                        pe.wait_ge(s_qk, l * NT + 1)
                    else:
                        pe.wait_ge(s_rope, l * (NT - 1) + j)
                    b = psum[order.open(pe, ("qt", l, j))]
                    for t in range(3):
                        ins = tr(b[:, P * t:P * t + P], qkv[:, j, P * t:P * t + P], ident)
                    end(ins)
                order.wait_emptied(pe, ("ckt", l))
                for j in range(NT):
                    order.wait_emptied(pe, ("qt", l, j))
                for j in range(NT):
                    blocks = key_blocks(j)
                    for h in range(NQ):
                        kv, g = h // 2, h % 2
                        r0 = HD * kv
                        b = psum[order.open(pe, ("qk", l, j, h))]
                        for pos, kb in blocks:
                            rhs = ckT[r0:r0 + HD, :] if kb is None else kT[r0:r0 + HD, P * kb:P * kb + P]
                            ins = mm(b[:, P * pos:P * pos + P], qT[r0:r0 + HD, g, P * j:P * j + P], rhs,
                                     start=True, stop=True)
                        end(ins)
                    pe.wait_ge(s_exp, l * NT + j + 1)
                    for h in range(NQ):
                        b = psum[order.open(pe, ("pt", l, j, h))]
                        for pos, kb in blocks:
                            ins = tr(b[:, P * pos:P * pos + P], sc[:, h, P * pos:P * pos + P], ident)
                        end(ins)
                    b = psum[order.open(pe, ("pv", l, j))]
                    for h in range(NQ):
                        order.wait_emptied(pe, ("pt", l, j, h))
                        kv = h // 2
                        for i, (pos, kb) in enumerate(blocks):
                            v = cv_tok if kb is None else qkv[:, kb, 384:512]
                            ins = mm(b[:, HD * h:HD * h + HD], pT[h][:, pos, :], v[:, HD * kv:HD * kv + HD],
                                     start=(i == 0), stop=(i == len(blocks) - 1))
                    end(ins)
                    order.wait_emptied(pe, ("pv", l, j))
                    b = psum[order.open(pe, ("ot", l, j))]
                    for t in range(2):
                        ins = tr(b[:, P * t:P * t + P], o_tok[:, 2 * t:2 * t + 2, :], ident)
                    end(ins)
                for ct in range(2):
                    for h in range(2):
                        order.wait_emptied(pe, ("in", l, ("f", ct), h))
                for j in range(NT):
                    b = psum[order.open(pe, ("f1", l, j))]
                    for ct in range(2):
                        ins = mm(b[:, 256 * ct:256 * ct + 256], fT[:, ct, P * j:P * j + P], cst("dft64", 256),
                                 start=True, stop=True)
                    end(ins)
                for j in range(NT):
                    order.wait_emptied(pe, ("f1", l, j))
                b = psum[order.open(pe, ("f2c", l))]
                for ct in range(2):
                    for cs in range(2):
                        ins = mm(b[:, P * ct:P * ct + P], v1[:, 0, ct, P * cs:P * cs + P],
                                 cst("dft128", P, P * cs), start=(cs == 0), stop=(cs == 1))
                end(ins)
                wait_item(pe, ("dft", l, 0))
                w = view(arena, item(("dft", l, 0)), 2, 4, 512)
                for ct in range(2):
                    b = psum[order.open(pe, ("f2", l, ct))]
                    for j in range(4):
                        for cs in range(2):
                            ins = mm(b[:, :], v1[:, 1 + j, ct, P * cs:P * cs + P], w[:, cs, j, :],
                                     start=(j + cs == 0), stop=(j + cs == 4))
                    end(ins)

                for j in range(NT):
                    order.wait_emptied(pe, ("vt", l, j))
                for n, step in enumerate(STEPS):
                    kind, i, d = step
                    j = step_tile(step)
                    T = lambda name, hp: (name, l, step, hp)
                    gn = l * len(STEPS) + n
                    if (kind, i) == ("s", 0):
                        pe.wait_ge(s_state, 16 * 8 * (l + 1))
                        b = psum[order.open(pe, ("si", l, d))]
                        for hp in range(2):
                            ins = tr(b[:, P * hp:P * hp + P], s0_in[:, d, hp, :], ident)
                        end(ins)
                    v0 = 2 * i if kind == "s" else 0
                    ver = lambda s: (v0 + s) % 3
                    pe.wait_ge(s_pad, gn + 1)
                    V = lambda hp, par: v_tok[:, j, 2 * hp + par, :]

                    def four(name, lhs, rhs, cols=P):
                        for hp in range(2):
                            b = psum[order.open(pe, T(name, hp))]
                            for par in range(2):
                                ins = mm(b[:, cols * par:cols * par + cols], lhs(hp, par), rhs(hp, par),
                                         start=True, stop=True)
                            end(ins)

                    E = EX[n % 2]
                    zr = lambda hp, par: E[:, hp, 0:2, :]
                    four("ab", lambda hp, par: BP[:, hp, par, :], zr, 256)
                    four("ak", lambda hp, par: KP[:, hp, par, :], zr, 256)
                    four("dd", lambda hp, par: E[:, hp, 0, :], lambda hp, par: BP[:, hp, par, :])
                    for hp in range(2):
                        b = psum[order.open(pe, T("tz", hp))]
                        end(tr(b[:, 0:P], E[:, hp, 0, :], ident))
                    for hp in range(2):
                        b = psum[order.open(pe, T("tb", hp))]
                        tr(b[:, 0:P], BT[:, hp], ident)
                        end(tr(b[:, P:2 * P], KD[:, hp], ident))
                    for hp in range(2):
                        order.wait_emptied(pe, T("dd", hp))
                    pe.wait_ge(s_tri, 2 * gn + 1)
                    sq = lambda B: (lambda hp, par: B[:, hp, par, :])
                    four("n2", sq(DD), sq(ND))
                    four("d2", sq(ND), sq(DD))
                    for hp in range(2):
                        order.wait_emptied(pe, T("ak", hp))
                    four("akv", lambda hp, par: AK[:, hp, par, 0:P], V, HD)
                    for hp in range(2):
                        order.wait_emptied(pe, T("d2", hp))
                        order.wait_emptied(pe, T("n2", hp))
                    pe.wait_ge(s_tri, 2 * gn + 2)
                    four("x2", sq(D2), sq(XA))
                    four("n4", sq(D2), sq(N2))
                    four("d4", sq(N2), sq(D2))
                    for hp in range(2):
                        order.wait_emptied(pe, T("x2", hp))
                        order.wait_emptied(pe, T("d4", hp))
                    four("x4", sq(DD), sq(XB))
                    four("d8", sq(ND), sq(DD))
                    for hp in range(2):
                        order.wait_emptied(pe, T("d8", hp))
                        order.wait_emptied(pe, T("x4", hp))
                    four("x8", sq(D2), sq(XA))

                    def flip(name, B):
                        for hp in range(2):
                            b = psum[order.open(pe, T(name, hp))]
                            for par in range(2):
                                ins = tr(b[:, P * par:P * par + P], B[:, hp, par, :], ident)
                            end(ins)

                    def emptied_pair(name):
                        for hp in range(2):
                            order.wait_emptied(pe, T(name, hp))

                    emptied_pair("x8")
                    flip("x8t", XB)
                    emptied_pair("x8t")
                    four("g1", sq(O32), sq(N2))
                    emptied_pair("g1")
                    four("y1", sq(ND), sq(XB))
                    emptied_pair("y1")
                    flip("y1t", XA)
                    emptied_pair("y1t")
                    four("g2", sq(O64), sq(N2))
                    emptied_pair("g2")
                    four("y2", sq(ND), sq(XA))
                    emptied_pair("y2")
                    emptied_pair("akv")
                    four("wp", sq(XB), sq(RR))
                    emptied_pair("wp")
                    emptied_pair("ab")
                    for hp in range(2):
                        b = psum[order.open(pe, T("rh", hp))]
                        for par in range(2):
                            ins = mm(b[HD * par:HD * par + HD, 0:P], WP[:, hp, par, 0:HD], AB[:, hp, par, P:2 * P],
                                     start=True, stop=True)
                        end(ins)
                    emptied_pair("tb")
                    for hp in range(2):
                        b = psum[order.open(pe, T("mt", hp))]
                        for par in range(2):
                            ins = mm(b[HD * par:HD * par + HD, 0:P], WP[:, hp, par, 0:HD],
                                     BC[:, hp, :, HD * par:HD * par + HD], start=True, stop=True)
                        end(ins)
                    emptied_pair("mt")
                    for s in range(2):
                        c = s if d == 0 else 1 - s
                        if s == 1:
                            emptied_pair("s0")
                        else:
                            if kind == "c":
                                pe.wait_ge(s_st0, 2 * l + d + 1)
                            elif i == 0:
                                order.wait_emptied(pe, ("si", l, d))
                            else:
                                for hp in range(2):
                                    order.wait_emptied(pe, ("s1", l, STEPS[n - 1], hp))
                        for hp in range(2):
                            b = psum[order.open(pe, T(f"s{s}", hp))]
                            mm(b[:, 0:P], BM[:, hp, c, :], ST[:, hp, ver(s), :], start=True, stop=False, skip_group_check=True)
                            for par in range(2):
                                o = b[HD * par:HD * par + HD, HD * par:HD * par + HD]
                                cols = slice(HD * par, HD * par + HD)
                                mm(o, BC[:, hp, c, cols], WP[:, hp, par, HD:P], start=False, stop=False, skip_group_check=True)
                                ins = mm(o, KC[:, hp, c, cols], V(hp, par), start=False, stop=(par == 1), skip_group_check=True)
                            end(ins)
                    emptied_pair("rh")
                    for hp in range(2):
                        b = psum[order.open(pe, T("yy", hp))]
                        for s in range(2):
                            c = s if d == 0 else 1 - s
                            mm(b[:, CH * c:CH * c + CH], ST[:, hp, ver(s), :], RH[:, hp, CH * c:CH * c + CH],
                               start=(s == 0), stop=False, skip_group_check=True)
                        for par in range(2):
                            o = b[HD * par:HD * par + HD, 0:P]
                            mm(o, WP[:, hp, par, HD:P], AB[:, hp, par, P:2 * P], start=False, stop=False, skip_group_check=True)
                            ins = mm(o, V(hp, par), AK[:, hp, par, P:2 * P], start=False, stop=(par == 1), skip_group_check=True)
                        end(ins)

                    if kind == "c":
                        emptied_pair("s1")
                        b = psum[order.open(pe, ("so", l, d))]
                        for hp in range(2):
                            ins = tr(b[:, P * hp:P * hp + P], ST[:, hp, ver(2), :], ident)
                        end(ins)

                for name in ("mu", "var"):
                    if name == "mu":
                        for hp in range(2):
                            order.wait_emptied(pe, ("yy", l, STEPS[-1], hp))
                    else:
                        pe.wait_ge(s_gsq, l + 1)
                    src = yT if name == "mu" else tmp
                    for ct in range(2):
                        for h in range(2):
                            b = psum[order.open(pe, (name, l, ct, h))]
                            end(mm(b[:, 0:HALF], blk, src[:, ct, HALF * h:HALF * (h + 1)], start=True, stop=True))
                pe.wait_ge(s_gup_in, 16 * 5 * (l + 1))
                for ct in range(2):
                    for h in range(2):
                        b = psum[order.open(pe, ("gup", l, ct, h))]
                        end(mm(b[:, 0:HALF], g_up[0:64, P * ct:P * ct + P], gdT[0:64, HALF * h:HALF * (h + 1)],
                               start=True, stop=True))
                for ct in range(2):
                    for h in range(2):
                        order.wait_emptied(pe, ("gup", l, ct, h))
                pe.wait_ge(s_conv, l + 1)
                for j in range(NT):
                    order.wait_emptied(pe, ("ot", l, j))
                order.wait_emptied(pe, ("f2c", l))
                for ct in range(2):
                    order.wait_emptied(pe, ("f2", l, ct))
                for i in range(2):
                    wait_item(pe, ("wout", l, i))
                    w = view(arena, item(("wout", l, i)), KT, 512)
                    for t in range(4):
                        for h in range(2):
                            b = psum[order.open(pe, ("out", l, 4 * i + t, h))]
                            for k in range(KT):
                                ins = mm(b[:, 0:HALF], w[:, k, P * t:P * t + P], mixT[:, k, HALF * h:HALF * (h + 1)],
                                         start=(k == 0), stop=(k == KT - 1))
                            end(ins)
                sum_squares("ss2", l, 2 * l + 2)
                pe.wait_ge(s_h, 2 * l + 2)
                if l == 1:
                    b = psum[order.open(pe, ("router", l))]
                    for j in range(NT):
                        for k in range(KT):
                            ins = mm(b[:, NE * j:NE * j + NE], hT[:, k, P * j:P * j + P], router_w[:, k, :],
                                     start=(k == 0), stop=(k == KT - 1))
                    end(ins)
                    order.wait_emptied(pe, ("router", l))
                for h in range(2):
                    order.wait_emptied(pe, ("ss2", l, h))
                if l == 0:
                    fn = ffn(l, 0, fn, DFF, 4)
                else:
                    for e in range(NE):
                        if e == 0:
                            pe.wait_ge(s_gate, 1)
                        pe.wait_ge(s_ffree, fn)
                        for h, (lo, n) in enumerate(((0, 3), (3, 2))):
                            b = psum[4 + h]
                            for j in range(lo, lo + n):
                                ins = mm(b[:, P * (j - lo):P * (j - lo) + P],
                                         gates[:, j, e:e + 1].broadcast_to([P, P]), ident, start=True, stop=True)
                        ins.then_inc(s_gbc, 1)
                        pe.wait_ge(s_gbcf, e + 1)
                        fn = ffn(l, e, fn, DFE, 2)
            pe.wait_ge(s_ffree, FFN_SETS[1])
            for j in range(NT):
                for q in range(2):
                    b = psum[order.open(pe, ("y", j, q))]
                    for k in range(4):
                        ins = tr(b[:, P * k:P * k + P], xT[:, 4 * q + k, P * j:P * j + P], ident)
                    end(ins)

        pc = lambda name, i: par[:, ROW[name] + i:ROW[name] + i + 1]
        IN_DEST = {"r": rT, "k": kT_, "v": vT, "bx": bxT, "bb": bbT, "bc": bcT, "f": fT}

        @block.scalar
        def _(act):
            chain = Chain(act, s_ca)
            ac = nc.scalar.activation

            def end(ins):
                ins.then_inc(emptied["A"], 1)

            def take(name):
                order.wait_filled(act, name)
                return psum[order.bank(name)]

            def norm(l, which):
                if which == 2:
                    order.wait_emptied(act, ("out", l, KT - 1, 1))
                elif l > 0:
                    act.wait_ge(s_ffree, FFN_SETS[l - 1])
                else:
                    for j in range(NT):
                        for q in range(2):
                            order.wait_emptied(act, ("x", j, q))
                for k in range(KT):
                    ins = ac(hT[:, k, :], xT[:, k, :], ACT.Square)
                ins.then_inc(s_sq, 1)
                for h in range(2):
                    b = take((f"ss{which}", l, h))
                    end(ac(rs[:, HALF * h:HALF * (h + 1)], b[:, 0:HALF], ACT.Sqrt, scale=1.0 / D, bias=cst("eps", 1)))
                nth = 2 * l + which - 1
                for k in range(KT):
                    act.wait_ge(s_hmul, KT * nth + k + 1)
                    for vec, lo, hi in SEGS:
                        ins = ac(hT[:, k, lo:hi], hT[:, k, lo:hi], ACT.Identity,
                                 bias=mod[:, 24 * (which - 1) + k, vec:vec + 1])
                ins.then_inc(s_h, 1)

            def in_evac(l, tiles):
                for name, _, _ in tiles:
                    for h in range(2):
                        key = ("in", l, name, h)
                        if order.by[order.at[key]] != "A":
                            continue
                        b = take(key)
                        cols = slice(HALF * h, HALF * (h + 1))
                        if name[0] == "wa":
                            chain.did(ac(waT[0:64, cols], b[0:64, 0:HALF], ACT.Tanh))
                            end(ac(waT[64:P, cols], b[64:P, 0:HALF], ACT.Copy))
                        elif name[0] == "gd":
                            end(ac(gdT[0:64, cols], b[0:64, 0:HALF], ACT.Sigmoid))
                        else:
                            end(ac(IN_DEST[name[0]][:, name[1], cols], b[:, 0:HALF], ACT.Copy))

            act.wait_ge(s_const, 16)
            for j in range(NT):
                b = take(("x", j, 0))
                end(ac(xT[:, 0:4, P * j:P * j + P], b[:, :].rearrange("p (k t) -> p k t", k=4), ACT.Copy))
            up_sets = 0
            for l in range(DEPTH):
                order.wait_emptied(act, ("params", l))
                chain.did(ac(silu_c[:, :, 0], par[:, ROW["c_ctx"]:ROW["c_ctx"] + KT], ACT.Silu))
                ac(silu_c[:, :, 1], par[:, ROW["c"]:ROW["c"] + KT], ACT.Silu).then_inc(s_silc, 1)
                norm(l, 1)
                in_evac(l, RW_TILES)
                for j in range(0, NT, 2):
                    b = take(("qkv", l, j))
                    end(ac(qkv[:, j, :], b[:, :], ACT.Copy))
                in_evac(l, CF_TILES)
                act.wait_ge(s_kkr, l + 1)
                for ct in range(2):
                    ins = ac(tmp[:, ct, :], kkT[:, ct, :], ACT.Square)
                ins.then_inc(s_kq, 1)
                order.wait_filled(act, ("in", l, CF_TILES[-1][0], 1))
                for j in range(NT):
                    order.wait_emptied(act, ("qkv", l, j))
                    ins = ac(qk_sq[:, j, :], qkv[:, j, 0:384], ACT.Square)
                ins.then_inc(s_qsq, 1)
                for j in range(NT):
                    b = take(("vt", l, j))
                    end(ac(v_tok[:, j].rearrange("p h d -> p (h d)"), b[:, 0:256], ACT.Copy))
                act.wait_ge(s_conv, l + 1)
                for kind in range(2):
                    for d in range(2):
                        for ct in range(2):
                            for h in range(2):
                                b = take(("up", l, kind, d, ct, h))
                                row = ROW["w0" if kind == 0 else "a0"] + 2 * d + ct
                                dst = (lw if kind == 0 else aT)[:, d, ct, HALF * h:HALF * (h + 1)]
                                end(ac(dst, b[:, 0:HALF], ACT.Sigmoid, bias=par[:, row:row + 1]))
                for ct in range(2):
                    for h in range(2):
                        b = take(("kks", l, ct, h))
                        end(ac(tmp[:, ct, HALF * h:HALF * (h + 1)], b[:, 0:HALF], ACT.Sqrt))
                act.wait_ge(s_qss, l + 1)
                ac(qk_ss, qk_ss, ACT.Sqrt, scale=1.0 / HD, bias=cst("eps", 1)).then_inc(s_qrt, 1)
                for j in range(NT):
                    pos = [p for p, _ in key_blocks(j)]
                    lo, hi = P * pos[0], P * (pos[-1] + 1)
                    act.wait_ge(s_max, l * NT + j + 1)
                    A = att[:, j % 2]
                    for h in range(NQ):
                        chain.did(ac(sc[:, h, lo:hi], sc[:, h, lo:hi], ACT.Exp, scale=HD ** -0.5,
                                     bias=A[:, 4 + h:5 + h], accum_out=A[:, 8 + h:9 + h]))
                    chain.settle()
                    ac(A[:, 12:16], A[:, 12:16], ACT.Exp).then_inc(s_exp, 1)
                    for h in (0, 2):
                        b = take(("pt", l, j, h))
                        end(ac(pT[h].rearrange("p a b -> p (a b)")[:, lo:hi], b[:, lo:hi], ACT.Copy))
                    b = take(("ot", l, j))
                    end(ac(mixT[:, 0:2, P * j:P * j + P], b[:, 0:256].rearrange("p (t n) -> p t n", t=2), ACT.Copy))
                for j in range(0, NT, 2):
                    b = take(("f1", l, j))
                    end(ac(v1[:, j].rearrange("p a b -> p (a b)"), b[:, :], ACT.Copy))
                b = take(("f2c", l))
                end(ac(mixT[:, 6:8, 0:CTX], b[:, 0:256].rearrange("p (t n) -> p t n", t=2), ACT.Copy))
                b = take(("f2", l, 0))
                end(ac(mixT[:, 6, CTX:TOK], b[:, :], ACT.Copy))

                act.wait_ge(s_zero, 2 * l + 2)

                def decays(n):
                    gn = l * len(STEPS) + n
                    E = EX[n % 2]
                    act.wait_ge(s_sum, gn + 1)
                    chain.did(ac(E[:, :, 2, :], E[:, :, 1, :], ACT.Exp, scale=-1.0))
                    chain.settle()
                    ac(E[:, :, 0:2, :], E[:, :, 0:2, :], ACT.Exp).then_inc(s_ex, 1)

                decays(0)
                for n, step in enumerate(STEPS):
                    T = lambda name, hp: (name, l, step, hp)

                    def copies(name, dst):
                        for hp in range(2):
                            b = take(T(name, hp))
                            end(ac(dst[:, hp], b[:, 0:256].rearrange("p (a b) -> p a b", a=2), ACT.Copy))

                    for hp in range(2):
                        b = take(T("tz", hp))
                        end(ac(RR[:, hp, :, 0:HD], b[:, 0:P].rearrange("p (a b) -> p a b", a=2), ACT.Copy))
                    for hp in range(2):
                        b = take(T("tb", hp))
                        for c in range(2):
                            rows = slice(CH * c, CH * c + CH)
                            chain.did(ac(BC[rows, hp, c, :], b[rows, 0:P], ACT.Copy, scale=-1.0))
                            ins = ac(KC[rows, hp, c, :], b[rows, P:2 * P], ACT.Copy)
                            if c == 0:
                                chain.did(ins)
                            else:
                                end(ins)
                    copies("n2", N2)
                    copies("d2", D2)
                    copies("n4", ND)
                    copies("d4", DD)
                    if n + 1 < len(STEPS):
                        decays(n + 1)
                    copies("d8", D2)
                    copies("x8t", N2)
                    copies("g1", ND)
                    copies("y1t", N2)
                    copies("g2", ND)
                    copies("wp", WP)

                act.wait_ge(s_gn, l + 1)
                act.wait_ge(s_state_out, 16 * 8 * (l + 1))
                for ct in range(2):
                    ins = ac(tmp[:, ct, :], yT[:, ct, :], ACT.Square)
                ins.then_inc(s_gsq, 1)
                for ct in range(2):
                    for h in range(2):
                        b = take(("var", l, ct, h))
                        end(ac(tmp[:, ct, HALF * h:HALF * (h + 1)], b[:, 0:HALF], ACT.Sqrt, scale=1.0 / HD,
                               bias=cst("eps", 1, 1)))
                norm(l, 2)
                if l == 1:
                    act.wait_ge(s_rmax, 1)
                    ac(rt_l, rt_l, ACT.Exp).then_inc(s_rexp, 1)
                for e in range(1 if l == 0 else NE):
                    base, nf, per = ffn_shape(l, e)
                    if l == 1:
                        act.wait_ge(s_gbc, e + 1)
                        chain.did(ac(gbc[:, 0:3 * P], psum[4][:, 0:3 * P], ACT.Copy))
                        ac(gbc[:, 3 * P:TOK], psum[5][:, 0:2 * P], ACT.Copy).then_inc(s_gbcf, 1)
                    for i in range(nf):
                        n = base + i
                        act.wait_ge(s_fup, n + 1)
                        if n >= 2:
                            act.wait_ge(s_ffree, n - 1)
                        for h in range(2):
                            ins = ac(sil[:, n % 2, HALF * h:HALF * (h + 1)], psum[4 * (n % 2) + h][:, 0:HALF], ACT.Silu)
                        ins.then_inc(s_silu, 1)
            for j in range(NT):
                b = take(("y", j, 0))
                end(ac(x_tok[:, j, 0:512], b[:, :], ACT.Copy))

        @block.vector
        def _(ve):
            chain = Chain(ve, s_cv)
            v = nc.vector

            def end(ins):
                ins.then_inc(emptied["V"], 1)

            def take(name):
                order.wait_filled(ve, name)
                return psum[order.bank(name)]

            def norm(l, which):
                t = 24 * (which - 1) + 8
                w = par[:, ROW[f"norm{which}"]:ROW[f"norm{which}"] + KT]
                if which == 1:
                    order.wait_emptied(ve, ("mod", l))
                chain.did(v.scalar_tensor_tensor(out=amul, in0=mod[:, t:t + KT, :], scalar=1.0,
                                                 in1=w[:, :, None].broadcast_to([P, KT, 2]), op0=ALU.add, op1=ALU.mult))
                for h in range(2):
                    order.wait_emptied(ve, (f"ss{which}", l, h))
                chain.did(v.reciprocal(rs, rs))
                chain.settle()
                for k in range(KT):
                    for vec, lo, hi in SEGS:
                        ins = v.scalar_tensor_tensor(out=hT[:, k, lo:hi], in0=xT[:, k, lo:hi], scalar=amul[:, k, vec:vec + 1],
                                                     in1=rs[:, lo:hi], op0=ALU.mult, op1=ALU.mult)
                        if vec == 0:
                            chain.did(ins)
                    ins.then_inc(s_hmul, 1)

            def in_evac(l, tiles):
                for name, _, _ in tiles:
                    for h in range(2):
                        key = ("in", l, name, h)
                        if order.by[order.at[key]] != "V":
                            continue
                        b = take(key)
                        end(v.tensor_copy(IN_DEST[name[0]][:, name[1], HALF * h:HALF * (h + 1)], b[:, 0:HALF]))

            def residual(b, h, dt, gate):
                parts = ((0, 0, CTX), (1, CTX, HALF)) if h == 0 else ((1, HALF, TOK),)
                for vec, lo, hi in parts:
                    off = HALF * h
                    ins = v.scalar_tensor_tensor(out=xT[:, dt, lo:hi], in0=b[:, lo - off:hi - off],
                                                 scalar=mod[:, gate + dt, vec:vec + 1], in1=xT[:, dt, lo:hi],
                                                 op0=ALU.mult, op1=ALU.add)
                    if hi < TOK and vec == 0:
                        chain.did(ins)
                return ins

            ve.wait_ge(s_const, 16)
            for j in range(NT):
                b = take(("x", j, 1))
                end(v.tensor_copy(xT[:, 4:8, P * j:P * j + P], b[:, :].rearrange("p (k t) -> p k t", k=4)))
            for l in range(DEPTH):
                b = take(("params", l))
                end(v.tensor_copy(par, b[:, 0:NROWS]))
                order.wait_emptied(ve, ("params", l))
                b = take(("mod", l))
                end(v.tensor_tensor(mod, b[:, 0:96].rearrange("p (t v) -> p t v", v=2),
                                    par[:, 0:48][:, :, None].broadcast_to([P, 48, 2]), ALU.add))
                norm(l, 1)
                in_evac(l, RW_TILES)
                for ct in range(2):
                    order.wait_emptied(ve, ("in", l, ("k", ct), 0))
                    order.wait_emptied(ve, ("in", l, ("k", ct), 1))
                    chain.did(v.tensor_scalar(omka[:, ct:ct + 1], pc("k_a", ct), -1.0, 1.0, ALU.mult, ALU.add))
                    ins = v.tensor_scalar(kkT[:, ct, :], kT_[:, ct, :], pc("k_k", ct), None, ALU.mult)
                ins.then_inc(s_kkr, 1)
                for j in range(1, NT, 2):
                    b = take(("qkv", l, j))
                    end(v.tensor_copy(qkv[:, j, :], b[:, :]))
                in_evac(l, CF_TILES)
                ve.wait_ge(s_cu, l + 1)
                for h in range(2):
                    for ct in range(2):
                        order.wait_emptied(ve, ("in", l, ("bb", ct), h))
                for ct in range(2):
                    for at0, (_, lo, hi) in ((0, SEGS[0]), (2, SEGS[1])):
                        n = hi - lo
                        u = lambda s: conv_u[:, ct, at0 + lo + s:at0 + hi + s]
                        o = mixT[:, 2 + ct, lo:hi]
                        chain.did(v.tensor_scalar(o, u(0), pc("conv", ct), None, ALU.mult))
                        for s in (1, 2):
                            chain.settle()
                            chain.did(v.scalar_tensor_tensor(out=o, in0=u(s), scalar=pc("conv", 2 * s + ct), in1=o,
                                                             op0=ALU.mult, op1=ALU.add))
                        chain.settle()
                        ins = v.tensor_tensor(o, o, bbT[:, ct, lo:hi], ALU.mult)
                        if (ct, lo) != (1, CTX):
                            chain.did(ins)
                        else:
                            ins.then_inc(s_conv, 1)
                ve.wait_ge(s_qsq, l + 1)
                v.tensor_reduce(out=qk_ss, in_=qk_sq.rearrange("p j (h d) -> p (j h) d", d=HD), axis=AXX,
                                op=ALU.add).then_inc(s_qss, 1)
                for ct in range(2):
                    for h in range(2):
                        order.wait_emptied(ve, ("kks", l, ct, h))
                chain.did(v.tensor_scalar(tmp, tmp, 1e-12, None, ALU.max))
                chain.settle()
                chain.did(v.reciprocal(tmp, tmp))
                chain.settle()
                v.scalar_tensor_tensor(out=kkT, in0=kkT, scalar=-1.0, in1=tmp, op0=ALU.mult, op1=ALU.mult).then_inc(s_nkk, 1)
                ve.wait_ge(s_nkk, l + 1)
                for ct in range(2):
                    for h in range(2):
                        order.wait_emptied(ve, ("in", l, ("r", ct), h))
                    ins = v.scalar_tensor_tensor(out=tmp[:, ct, :], in0=rT[:, ct, :], scalar=pc("r_k", ct), in1=kT_[:, ct, :],
                                                 op0=ALU.mult, op1=ALU.mult)
                    if ct == 0:
                        chain.did(ins)
                ins.then_inc(s_rk, 1)
                for ct in range(2):
                    for h in range(2):
                        b = take(("bonus", l, ct, h))
                        for c2 in range(2):
                            order.wait_emptied(ve, ("in", l, ("v", ct), c2))
                        cols = slice(HALF * h, HALF * (h + 1))
                        end(v.tensor_tensor(vT[:, ct, cols], b[:, 0:HALF], vT[:, ct, cols], ALU.mult))
                b = take(("ckt", l))
                end(v.tensor_copy(ckT, b[:, 0:P]))
                ve.wait_ge(s_qrt, l + 1)
                ve.wait_ge(s_gup_in, 16 * 5 * (l + 1))
                chain.did(v.reciprocal(qk_ss, qk_ss))
                for j in range(NT):
                    q_in = qkv[:, j, 0:384].rearrange("p (h d) -> p h d", d=HD)
                    t = qk_t[:, j % 2]
                    chain.settle()
                    if j == 0:
                        for jj in range(NT):
                            order.wait_emptied(ve, ("qkv", l, jj))
                    chain.did(v.tensor_tensor(t, q_in, qk_ss[:, 6 * j:6 * j + 6][:, :, None].broadcast_to([P, 6, HD]), ALU.mult))
                    chain.settle()
                    chain.did(v.tensor_tensor(
                        qkv[:, j, 0:256].rearrange("p (g k d) -> p k g d", g=2, k=2),
                        t[:, 0:4, :].rearrange("p (k g) d -> p k g d", k=2),
                        qnw[:, None, None, :].broadcast_to([P, 2, 2, HD]), ALU.mult))
                    v.tensor_tensor(qkv[:, j, 256:384].rearrange("p (k d) -> p k d", k=2), t[:, 4:6, :],
                                    knw[:, None, :].broadcast_to([P, 2, HD]), ALU.mult).then_inc(s_qk, 1)
                for j in range(NT):
                    b = take(("qt", l, j))
                    chain.did(v.tensor_copy(qT[:, :, P * j:P * j + P], b[:, 0:256].rearrange("p (t n) -> p t n", t=2)))
                    end(v.tensor_copy(kT[:, P * j:P * j + P], b[:, 256:384]))
                for j in range(NT):
                    pos = [p for p, _ in key_blocks(j)]
                    lo, hi = P * pos[0], P * (pos[-1] + 1)
                    A = att[:, j % 2]
                    for h in range(NQ):
                        b = take(("qk", l, j, h))
                        if j == 0:
                            end(v.tensor_copy(sc[:, h, lo:hi], b[:, lo:hi]))
                        else:
                            end(v.tensor_tensor(sc[:, h, lo:hi], b[:, lo:hi], cst("band", 512)[:, lo:hi], ALU.add))
                    order.wait_emptied(ve, ("qk", l, j, NQ - 1))
                    chain.did(v.tensor_reduce(out=A[:, 0:4], in_=sc[:, :, lo:hi], axis=AXX, op=ALU.max))
                    chain.settle()
                    chain.did(v.scalar_tensor_tensor(out=A[:, 0:4], in0=A[:, 0:4], scalar=HD ** -0.5, in1=sink,
                                                     op0=ALU.mult, op1=ALU.max))
                    chain.settle()
                    chain.did(v.tensor_scalar(A[:, 4:8], A[:, 0:4], -1.0, None, ALU.mult))
                    v.tensor_tensor(A[:, 12:16], sink, A[:, 0:4], ALU.subtract).then_inc(s_max, 1)
                    for h in (1, 3):
                        b = take(("pt", l, j, h))
                        end(v.tensor_copy(pT[h].rearrange("p a b -> p (a b)")[:, lo:hi], b[:, lo:hi]))
                    ve.wait_ge(s_exp, l * NT + j + 1)
                    chain.did(v.tensor_tensor(A[:, 16:20], A[:, 8:12], A[:, 12:16], ALU.add))
                    chain.settle()
                    chain.did(v.reciprocal(A[:, 16:20], A[:, 16:20]))
                    chain.settle()
                    b = take(("pv", l, j))
                    end(v.tensor_tensor(o_tok, b[:, 0:256].rearrange("p (h d) -> p h d", h=NQ),
                                        A[:, 16:20][:, :, None].broadcast_to([P, NQ, HD]), ALU.mult))
                for j in range(1, NT, 2):
                    b = take(("f1", l, j))
                    end(v.tensor_copy(v1[:, j].rearrange("p a b -> p (a b)"), b[:, :]))
                b = take(("f2", l, 1))
                end(v.tensor_copy(mixT[:, 7, CTX:TOK], b[:, :]))

                ve.wait_ge(s_zero, 2 * l + 2)

                def sums(n):
                    _, _, d = STEPS[n]
                    j = step_tile(STEPS[n])
                    E = EX[n % 2]
                    x = lw[:, d, :, P * j:P * j + P]
                    if n >= 2:
                        for hp in range(2):
                            order.wait_emptied(ve, ("rh", l, STEPS[n - 2], hp))
                    for hp in range(2):
                        chain.did(v.tensor_tensor_scan(out=E[:, hp, 1, :], data0=cst("scan", P), data1=x[:, hp, :],
                                                       initial=0.0, op0=ALU.mult, op1=ALU.add))
                    chain.settle()
                    if d == 0:
                        chain.did(v.tensor_tensor(E[:, :, 0, :], E[:, :, 1, :], x, ALU.subtract))
                        chain.settle()
                    else:
                        for c in range(2):
                            tot = E[:, :, 1, CH * c + CH - 1:CH * c + CH].broadcast_to([P, 2, CH])
                            chain.did(v.tensor_tensor(E[:, :, 0, CH * c:CH * c + CH], tot, E[:, :, 1, CH * c:CH * c + CH],
                                                      ALU.subtract))
                        chain.settle()
                        chain.did(v.tensor_tensor(E[:, :, 1, :], E[:, :, 0, :], x, ALU.add))
                        chain.settle()
                    v.tensor_scalar(E[:, :, 0:2, :], E[:, :, 0:2, :], LOG_DECAY, None, ALU.mult).then_inc(s_sum, 1)

                sums(0)
                for n, step in enumerate(STEPS):
                    kind, i, d = step
                    j = step_tile(step)
                    gn = l * len(STEPS) + n
                    T = lambda name, hp: (name, l, step, hp)
                    E = EX[n % 2]
                    v0 = 2 * i if kind == "s" else 0
                    if (kind, i) == ("s", 0):
                        b = take(("si", l, d))
                        end(v.tensor_copy(ST[:, :, 0, :], b[:, 0:256].rearrange("p (a b) -> p a b", a=2)))
                    elif kind == "c":
                        if d == 1:
                            order.wait_emptied(ve, ("so", l, 0))
                        v.memset(ST[:, :, 0, :], 0.0).then_inc(s_st0, 1)
                    pair = lambda b: b[:, 0:256].rearrange("p (a b) -> p a b", a=2)
                    for hp in range(2):
                        b = take(T("ab", hp))
                        end(v.scalar_tensor_tensor(out=AB[:, hp], in0=b[:, :].rearrange("p (a b) -> p a b", a=2), scalar=-1.0,
                                                   in1=cst("mzr", 256, 256 * d)[:, None, :].broadcast_to([P, 2, 256]),
                                                   op0=ALU.mult, op1=ALU.mult))
                    for hp in range(2):
                        b = take(T("ak", hp))
                        end(v.tensor_tensor(AK[:, hp], b[:, :].rearrange("p (a b) -> p a b", a=2),
                                            cst("mzr", 256, 256 * d)[:, None, :].broadcast_to([P, 2, 256]), ALU.mult))
                    for hp in range(2):
                        b = take(T("dd", hp))
                        end(v.scalar_tensor_tensor(out=DD[:, hp], in0=pair(b), scalar=-1.0,
                                                   in1=cst("m16", P, P * (1 - d))[:, None, :].broadcast_to([P, 2, P]),
                                                   op0=ALU.mult, op1=ALU.mult))
                    for hp in range(2):
                        b = take(T("akv", hp))
                        end(v.tensor_copy(RR[:, hp, :, HD:P], b[:, 0:P].rearrange("p (a b) -> p a b", a=2)))

                    def plus(name, dst, src):
                        for hp in range(2):
                            b = take(T(name, hp))
                            end(v.tensor_tensor(dst[:, hp], pair(b), src[:, hp], ALU.add))

                    def done(name):
                        for hp in range(2):
                            order.wait_emptied(ve, T(name, hp))

                    plus("x2", XB, XA)
                    if n + 1 < len(STEPS):
                        sums(n + 1)
                    done("x2")
                    plus("x4", XA, XB)
                    done("x4")
                    plus("x8", XB, XA)
                    done("x8")
                    plus("y1", XA, XB)
                    done("y1")
                    plus("y2", XB, XA)
                    for hp in range(2):
                        b = take(T("rh", hp))
                        end(v.tensor_tensor(RH[:, hp], b[:, 0:P], E[:, hp, 1, :], ALU.add))
                    for hp in range(2):
                        b = take(T("mt", hp))
                        for par_ in range(2):
                            r = slice(HD * par_, HD * par_ + HD)
                            ins = v.tensor_tensor(BM[r, hp, :, r], b[r, 0:P].rearrange("p (c k) -> p c k", c=2),
                                                  ident[r, r][:, None, :].broadcast_to([HD, 2, HD]), ALU.add)
                            if par_ == 0:
                                chain.did(ins)
                        end(ins)
                    for s in range(2):
                        c = s if d == 0 else 1 - s
                        for hp in range(2):
                            b = take(T(f"s{s}", hp))
                            end(v.tensor_scalar(ST[:, hp, (v0 + s + 1) % 3, :], b[:, 0:P], LC[:, n % 2, hp, c:c + 1], None,
                                                ALU.mult))
                    for hp in range(2):
                        b = take(T("yy", hp))
                        o = yT[:, hp, P * j:P * j + P]
                        if d == 0:
                            end(v.tensor_copy(o, b[:, 0:P]))
                        else:
                            end(v.tensor_tensor(o, b[:, 0:P], o, ALU.add))
                    if kind == "c":
                        b = take(("so", l, d))
                        end(v.tensor_copy(s_fin[:, d], pair(b)))

                order.wait_emptied(ve, ("yy", l, STEPS[-1], 1))
                for ct in range(2):
                    for h in range(2):
                        b = take(("mu", l, ct, h))
                        cols = slice(HALF * h, HALF * (h + 1))
                        end(v.scalar_tensor_tensor(out=yT[:, ct, cols], in0=b[:, 0:HALF], scalar=-1.0 / HD, in1=yT[:, ct, cols],
                                                   op0=ALU.mult, op1=ALU.add))
                order.wait_emptied(ve, ("mu", l, 1, 1))
                ve.sem_inc(s_gn, 1)
                for ct in range(2):
                    for h in range(2):
                        order.wait_emptied(ve, ("var", l, ct, h))
                chain.did(v.reciprocal(tmp, tmp))
                chain.settle()
                chain.did(v.tensor_tensor(yT, yT, tmp, ALU.mult))
                for ct in range(2):
                    chain.settle()
                    chain.did(v.tensor_scalar(yT[:, ct, :], yT[:, ct, :], pc("ln_w", ct), pc("ln_b", ct), ALU.mult, ALU.add))
                chain.settle()
                chain.did(v.tensor_tensor(yT, yT, vT, ALU.add))
                chain.settle()
                for ct in range(2):
                    for h in range(2):
                        b = take(("gup", l, ct, h))
                        cols = slice(HALF * h, HALF * (h + 1))
                        end(v.tensor_tensor(yT[:, ct, cols], b[:, 0:HALF], yT[:, ct, cols], ALU.mult))
                for dt in range(KT):
                    for h in range(2):
                        end(residual(take(("out", l, dt, h)), h, dt, 16))
                norm(l, 2)
                if l == 1:
                    three = lambda x: x[:, :, None].broadcast_to([P, NT, NE])
                    b = take(("router", l))
                    m = view(par_t, at[0] - 96, 3, NT)
                    end(v.tensor_copy(rt_t, b[:, 0:NT * NE].rearrange("p (j e) -> p j e", e=NE)))
                    order.wait_emptied(ve, ("router", l))
                    rank = cst("rank", NE)[:, None, :].broadcast_to([P, NT, NE])

                    def pick(dst, mx):
                        chain.did(v.tensor_reduce(out=mx, in_=rt_t, axis=AXX, op=ALU.max))
                        chain.settle()
                        chain.did(v.tensor_tensor(rt_key, rt_t, three(mx), ALU.is_equal))
                        chain.settle()
                        chain.did(v.tensor_tensor(rt_key, rt_key, rank, ALU.mult))
                        chain.settle()
                        chain.did(v.tensor_reduce(out=m[:, 2], in_=rt_key, axis=AXX, op=ALU.max))
                        chain.settle()
                        chain.did(v.tensor_tensor(dst, rt_key, three(m[:, 2]), ALU.is_equal))
                        chain.settle()

                    pick(rt_first, m[:, 0])
                    chain.did(v.tensor_tensor(rt_l, rt_t, three(m[:, 0]), ALU.subtract))
                    chain.did(v.scalar_tensor_tensor(out=rt_t, in0=rt_first, scalar=-3e38, in1=rt_t, op0=ALU.mult, op1=ALU.add))
                    chain.settle()
                    pick(rt_second, m[:, 1])
                    v.tensor_tensor(rt_first, rt_first, rt_second, ALU.add).then_inc(s_rmax, 1)
                    ve.wait_ge(s_rexp, 1)
                    chain.did(v.tensor_tensor(gates, rt_l, rt_first, ALU.mult))
                    chain.settle()
                    chain.did(v.tensor_reduce(out=m[:, 0], in_=gates, axis=AXX, op=ALU.add))
                    chain.settle()
                    chain.did(v.reciprocal(m[:, 0], m[:, 0]))
                    chain.settle()
                    v.tensor_tensor(gates, gates, three(m[:, 0]), ALU.mult).then_inc(s_gate, 1)
                ups = 0 if l == 0 else DFF // P
                for e in range(1 if l == 0 else NE):
                    base, nf, per = ffn_shape(l, e)
                    gb = (e % 2) * (DFE // P)
                    if l == 1:
                        ve.wait_ge(s_gbcf, e + 1)
                    for i in range(nf):
                        n = base + i
                        ve.wait_ge(s_silu, ups + e * nf + i + 1)
                        if l == 1:
                            chain.did(v.tensor_tensor(sil[:, n % 2, :], sil[:, n % 2, :], gbc, ALU.mult))
                            chain.settle()
                        for h in range(2):
                            cols = slice(HALF * h, HALF * (h + 1))
                            ins = v.tensor_tensor(gT[:, gb + i, cols], psum[4 * (n % 2) + 2 + h][:, 0:HALF],
                                                  sil[:, n % 2, cols], ALU.mult)
                            if h == 0:
                                chain.did(ins)
                        ins.then_inc(s_ffree, 1)
                    for i in range(4):
                        n = base + nf + i
                        ve.wait_ge(s_fup, n + 1)
                        for t in range(2):
                            for h in range(2):
                                ins = residual(psum[4 * (n % 2) + 2 * t + h], h, 2 * i + t, 40)
                                if (t, h) != (1, 1):
                                    chain.did(ins)
                        ins.then_inc(s_ffree, 1)
                        ve.wait_ge(s_ffree, n + 1)
            for j in range(NT):
                b = take(("y", j, 1))
                end(v.tensor_copy(x_tok[:, j, 512:1024], b[:, :]))

        @block.gpsimd
        def _(pool):
            chain = Chain(pool, s_cp)
            g = nc.gpsimd
            pool.wait_ge(s_const, 16)
            for l in range(DEPTH):
                if l > 0:
                    pool.wait_ge(s_ffree, FFN_SETS[l - 1])
                g.memset(rank_up, 0.0).then_inc(s_zero, 1)
                for name in ("bx", "bc"):
                    for ct in range(2):
                        for h in range(2):
                            order.wait_emptied(pool, ("in", l, (name, ct), h))
                chain.did(g.memset(conv_u, 0.0))
                chain.settle()
                chain.did(g.tensor_tensor(conv_u[:, :, 1:1 + CTX], bcT[:, :, 0:CTX], bxT[:, :, 0:CTX], ALU.mult))
                g.tensor_tensor(conv_u[:, :, 3 + CTX:3 + TOK], bcT[:, :, CTX:TOK], bxT[:, :, CTX:TOK], ALU.mult).then_inc(s_cu, 1)
                pool.wait_ge(s_qk, l * NT + 1)
                g.dma_start(new_k[0, l].rearrange("t h d -> t (h d)"), qkv[:, 0, 256:384]).then_inc(s_kv_out, 16)
                g.dma_start(new_v[0, l].rearrange("t h d -> t (h d)"), qkv[:, 0, 384:512]).then_inc(s_kv_out, 16)
                for j in range(1, NT):
                    pool.wait_ge(s_qk, l * NT + j + 1)
                    x = qkv[:, j, 0:384].rearrange("p (h s d) -> p h s d", s=4, d=16)
                    x1, x2 = x[:, :, 0::2, :], x[:, :, 1::2, :]
                    tab = lambda name: cst(name, 32, 32 * (j - 1)).rearrange("p (s d) -> p s d", s=2)[:, None, :, :] \
                        .broadcast_to([P, 6, 2, 16])
                    r = [rope[:, i] for i in range(4)]
                    chain.settle()
                    for t, xx, name in ((0, x1, "cos"), (1, x2, "sin"), (2, x2, "cos"), (3, x1, "sin")):
                        chain.did(g.tensor_tensor(r[t], xx, tab(name), ALU.mult))
                    chain.settle()
                    chain.did(g.tensor_tensor(x1, r[0], r[1], ALU.subtract))
                    g.tensor_tensor(x2, r[2], r[3], ALU.add).then_inc(s_rope, 1)
                    pool.wait_ge(s_rope, l * (NT - 1) + j)
                order.wait_filled(pool, ("f2", l, 1))
                pool.wait_ge(s_kv_out, 32 * (l + 1))
                for buf in (BP, KP, BM, BC, KC, s0_in):
                    chain.did(g.memset(buf, 0.0))
                chain.settle()
                pool.sem_inc(s_zero, 1)
                for d in range(2):
                    for h in range(4):
                        r = slice(HD * (h % 2), HD * (h % 2) + HD)
                        g.dma_start(s0_in[r, d, h // 2, r], a["state_wkv"][0, l, d, h]).then_inc(s_state, 16)
                pool.wait_ge(s_nkk, l + 1)
                for n, step in enumerate(STEPS):
                    kind, i, d = step
                    j = step_tile(step)
                    gn = l * len(STEPS) + n
                    cols = slice(P * j, P * j + P)
                    E = EX[n % 2]
                    pool.wait_ge(s_ex, gn + 1)
                    if n > 0:
                        order.wait_filled(pool, ("tb", l, STEPS[n - 1], 1))
                        if n > 1:
                            order.wait_emptied(pool, ("s1", l, STEPS[n - 2], 1))
                    e0 = CH - 1 if d == 0 else 0
                    chain.did(g.tensor_copy(LC[:, n % 2], E[:, :, 1, e0::CH]))
                    chain.did(g.tensor_tensor(BT, kkT[:, :, cols], aT[:, d, :, cols], ALU.mult))
                    for ct in range(2):
                        chain.did(g.tensor_scalar(KD[:, ct], aT[:, d, ct, cols], pc("k_a", ct), omka[:, ct:ct + 1],
                                                  ALU.mult, ALU.add))
                    chain.did(g.tensor_tensor(E[:, :, 0, :], E[:, :, 0, :], kkT[:, :, cols], ALU.mult))
                    chain.settle()
                    chain.did(g.tensor_tensor(E[:, :, 1, :], E[:, :, 1, :], rT[:, :, cols], ALU.mult))
                    chain.did(g.tensor_tensor(KD, KD, kT_[:, :, cols], ALU.mult))
                    chain.did(g.tensor_tensor(BT, BT, E[:, :, 2, :], ALU.mult))
                    chain.settle()
                    chain.did(g.tensor_tensor(KD, KD, E[:, :, 2, :], ALU.mult))
                    chain.settle()
                    for q in range(2):
                        r = slice(HD * q, HD * q + HD)
                        chain.did(g.tensor_copy(BP[r, :, q, :], BT[r, :, :]))
                        chain.did(g.tensor_copy(KP[r, :, q, :], KD[r, :, :]))
                    chain.settle()
                    pool.sem_inc(s_pad, 1)
                    for hp in range(2):
                        order.wait_emptied(pool, ("ab", l, step, hp))
                    z = lambda B: B[:, :, :, 0:P]
                    four = lambda B: B.rearrange("p a b c -> p (a b) c")
                    N = AB.rearrange("p a b c -> p (a b) c")[:, :, 0:P]
                    mask = lambda name: cst(name, P, P * d)[:, None, :].broadcast_to([P, 4, P])
                    g.tensor_tensor(four(ND), N, mask("m16"), ALU.mult).then_inc(s_tri, 1)
                    pool.wait_ge(s_tri, 2 * gn + 1)
                    chain.did(g.tensor_tensor(four(XA), four(ND), ident[:, None, :].broadcast_to([P, 4, P]), ALU.add))
                    chain.did(g.tensor_tensor(four(O32), N, mask("m32"), ALU.mult))
                    chain.did(g.tensor_tensor(four(O64), N, mask("m64"), ALU.mult))
                    chain.settle()
                    pool.sem_inc(s_tri, 1)
                    if n == 2:
                        for dd in range(2):
                            order.wait_emptied(pool, ("so", l, dd))
                            for h in range(4):
                                r = slice(HD * (h % 2), HD * (h % 2) + HD)
                                g.dma_start(new_s[0, l, dd, h], s_fin[r, dd, h // 2, r]).then_inc(s_state_out, 16)


def kernel(**inputs):
    from concourse import bacc
    from concourse.bass_utils import run_bass_kernel_spmd

    nc = bacc.Bacc("TRN2", target_bir_lowering=False, num_devices=1)
    const, dft = constants()
    arrays = {name: np.ascontiguousarray(x) for name, x in inputs.items()}
    arrays["const"], arrays["dft"] = const, dft
    aps = {name: nc.dram_tensor(f"in_{name}", x.shape, F32, kind="ExternalInput").ap() for name, x in arrays.items()}
    shapes = [(1, CTX, D), (1, LAT, D), (1, DEPTH, CTX, NKV, HD), (1, DEPTH, CTX, NKV, HD), (1, DEPTH, 2, 4, HD, HD)]
    outs = [nc.dram_tensor(f"out_{i}", s, F32, kind="ExternalOutput").ap() for i, s in enumerate(shapes)]
    build(nc, aps, outs)
    r = run_bass_kernel_spmd(nc, [{f"in_{name}": x for name, x in arrays.items()}], core_ids=[0])
    return tuple(r.results[0][f"out_{i}"] for i in range(len(shapes)))
```

```python
from contextlib import ExitStack

import numpy as np

import concourse.bass as bass
from concourse import mybir

F32 = mybir.dt.float32
F32R = mybir.dt.float32r
ACT = mybir.ActivationFunctionType
ALU = mybir.AluOpType
AXX = mybir.AxisListType.X

P = 128
D = 1024
KT = D // P
DEPTH = 2
CTX, LAT = 128, 512
TOK = CTX + LAT
NT = TOK // P
HALF = TOK // 2
SEGS = ((0, 0, CTX), (1, CTX, TOK))
HD = 64
NQ, NKV = 4, 2
CH = 64
GRID_W = 64
IN_W = 2496
DFF = 2816
NE = 8
DFE = 1024
EPS = 1e-6
GN_EPS = 64e-5
LOG_DECAY = -float(np.exp(-0.5))
BANKS = 8

ROWS = [("mod_b", 48), ("norm1", 8), ("norm2", 8), ("conv", 6), ("w0", 4), ("a0", 4),
        ("k_k", 2), ("k_a", 2), ("r_k", 2), ("ln_w", 2), ("ln_b", 2), ("c_ctx", 8), ("c", 8)]
ROW = {}
_n = 0
for _name, _k in ROWS:
    ROW[_name] = _n
    _n += _k
NROWS = _n

CONSTS = [("ident", 128), ("ones", 128), ("blk", 128), ("band", 512), ("mzr", 512), ("m16", 256),
          ("m32", 256), ("m64", 256), ("cos", 128), ("sin", 128), ("dft64", 256), ("dft128", 256),
          ("scan", 128), ("rank", 8), ("eps", 2), ("upper", 128), ("slots", 256), ("slot", 2)]
CC = {}
_n = 0
for _name, _k in CONSTS:
    CC[_name] = _n
    _n += _k
NCONST = _n

IN_TILES = [
    (("r", 0), 0, 0), (("r", 1), 0, 128), (("k", 0), 0, 256), (("k", 1), 0, 384),
    (("v", 0), 1, 0), (("v", 1), 1, 128), (("wa", 0), 1, 256), (("gd", 0), 1, 384),
    (("bx", 0), 3, 0), (("bx", 1), 3, 128), (("bb", 0), 3, 256), (("bb", 1), 3, 384),
    (("bc", 0), 4, 0), (("bc", 1), 4, 128), (("f", 0), 4, 256), (("f", 1), 4, 384)]
RW_TILES, CF_TILES = IN_TILES[:8], IN_TILES[8:]

MOD_ITEMS = 12
MOD_FIRST = 4
MIX_ITEMS = MOD_ITEMS + 5 + 1 + 2
SLOT = KT * 512
CHUNK = KT * 256
CAP = 256
MAX_ROUNDS = -(-TOK // CAP)
DENSE_PARTS = ((0, 8), (8, 8), (16, 6))
EXP_F = DFE // P
EXP_CHUNKS = EXP_F + 4
PAIR_ITEMS = 2 * EXP_CHUNKS // 2

STEPS = [("c", 0, d) for d in range(2)] + [("s", i, d) for d in range(2) for i in range(4)]


def step_tile(step):
    kind, i, d = step
    return 0 if kind == "c" else (1 + i if d == 0 else 4 - i)


def key_blocks(j):
    if j == 0:
        return [(1, 0)]
    return ([(0, j - 1)] if j > 1 else []) + [(1, j), (2, None)] + ([(3, j + 1)] if j < NT - 1 else [])


def constants():
    c = np.zeros((P, NCONST), np.float32)
    i = np.arange(P)[:, None]
    j = np.arange(P)[None, :]

    def put(name, a, at=0):
        c[:, CC[name] + at:CC[name] + at + a.shape[1]] = a

    put("ident", np.eye(P))
    put("ones", np.ones((P, P)))
    put("blk", (i // HD == j // HD).astype(np.float32))
    put("band", np.where(j >= i, 0.0, -1e30))
    put("band", np.where(j <= i, 0.0, -1e30), 384)
    for d in range(2):
        before = (i < j) if d == 0 else (i > j)
        same = lambda n: i // n == j // n
        put("mzr", (before & same(CH)).astype(np.float32), 256 * d)
        put("mzr", ((before | (i == j)) & same(CH)).astype(np.float32), 256 * d + 128)
        put("m16", (before & same(16)).astype(np.float32), 128 * d)
        put("m32", (before & same(32) & ~same(16)).astype(np.float32), 128 * d)
        put("m64", (before & same(64) & ~same(32)).astype(np.float32), 128 * d)
    inv = 10000.0 ** (-np.arange(16, dtype=np.float32) / 16)
    t = np.arange(LAT)
    ang = np.stack([(t // GRID_W)[:, None] * inv, (t % GRID_W)[:, None] * inv], 1).astype(np.float32)
    for name, fn in (("cos", np.cos), ("sin", np.sin)):
        put(name, fn(ang).reshape(4, P, 32).transpose(1, 0, 2).reshape(P, 128))
    e = np.arange(HD)
    a64 = 2 * np.pi * ((e[:, None] * e[None, :]) % HD) / HD
    for g in range(2):
        s = slice(g * HD, (g + 1) * HD)
        c[s, CC["dft64"] + g * HD:CC["dft64"] + (g + 1) * HD] = np.cos(a64) / 8
        c[s, CC["dft64"] + 128 + g * HD:CC["dft64"] + 128 + (g + 1) * HD] = -np.sin(a64) / 8
    a128 = 2 * np.pi * ((i * j) % P) / P
    put("dft128", np.cos(a128) / np.sqrt(P))
    put("dft128", np.sin(a128) / np.sqrt(P), 128)
    put("scan", np.broadcast_to((j % CH != 0), (P, P)).astype(np.float32))
    put("rank", np.broadcast_to(NE - np.arange(NE), (P, NE)).astype(np.float32))
    put("eps", np.full((P, 1), EPS), 0)
    put("eps", np.full((P, 1), GN_EPS), 1)
    put("upper", (i < j).astype(np.float32))
    put("slots", np.broadcast_to(np.arange(CAP), (P, CAP)).astype(np.float32))
    put("slot", i + P * np.arange(2)[None, :])
    u = np.arange(LAT)
    a512 = 2 * np.pi * ((u[:, None] * u[None, :]) % LAT) / LAT
    dft = np.stack([np.cos(a512), np.sin(a512)]) / np.sqrt(LAT)
    return c, dft.astype(np.float32)


class Order:

    def __init__(self, filled, emptied):
        self.filled, self.emptied = filled, emptied
        self.at, self.by, self.count = {}, [], {k: [] for k in emptied}
        self.next = 0

    def add(self, name, engine):
        self.at[name] = len(self.by)
        self.count[engine].append(len(self.by))
        self.by.append(engine)

    def bank(self, name):
        return self.at[name] % BANKS

    def wait_filled(self, eng, name):
        eng.wait_ge(self.filled, self.at[name] + 1)

    def wait_emptied(self, eng, name):
        n = self.at[name]
        e = self.by[n]
        eng.wait_ge(self.emptied[e], self.count[e].index(n) + 1)

    def open(self, pe, name):
        n = self.at[name]
        assert n == self.next, (name, n, self.next)
        self.next += 1
        if n >= BANKS:
            e = self.by[n - BANKS]
            pe.wait_ge(self.emptied[e], self.count[e].index(n - BANKS) + 1)
        return n % BANKS


class Chain:

    def __init__(self, eng, sem):
        self.eng, self.sem, self.n = eng, sem, 0

    def did(self, ins):
        ins.then_inc(self.sem, 1)
        self.n += 1

    def settle(self):
        self.eng.wait_ge(self.sem, self.n)


class PairOrder(Order):

    def wait_filled(self, eng, name, it, back=0):
        eng.wait_ge(self.filled, (it + 1 - back) * len(self.by) + self.at[name] + 1)

    def wait_emptied(self, eng, name, it):
        eng.wait_ge(self.emptied["V"], (it + 1) * len(self.by) + self.at[name] + 1)

    def open(self, pe, name, it):
        n = self.at[name]
        assert n == self.next % len(self.by), (name, n, self.next)
        self.next += 1
        pe.wait_ge(self.emptied["V"], (it + 1) * len(self.by) + n - BANKS + 1)
        return n % BANKS


def list_pair_groups(order):
    def gather(k):
        for b in range(4):
            order.add(("ga", k, b), "V")

    def scatter(k):
        for dt in range(KT):
            for h in range(2):
                order.add(("sc", k, dt, h), "V")

    for k in range(2):
        for b in range(4):
            order.add(("bc", k, b), "V")
        if k == 0:
            gather(0)
        for f in range(EXP_F):
            order.add(("up", k, f), "V")
        for i in range(2):
            for q in range(2):
                order.add(("dw", k, i, q), "V")
        if k == 0:
            gather(1)
        scatter(k)
    assert len(order.by) % BANKS == 0


def list_groups(order):
    for j in range(NT):
        for q in range(2):
            order.add(("x", j, q), "AV"[q])
    for l in range(DEPTH):
        order.add(("params", l), "V")
        order.add(("mod", l), "V")
        for h in range(2):
            order.add(("ss1", l, h), "A")
        for (name, _, _) in RW_TILES:
            for h in range(2):
                order.add(("in", l, name, h), "A" if name[0] in ("wa", "gd") else "AV"[h])
        for j in range(NT):
            order.add(("qkv", l, j), "AV"[j % 2])
        for (name, _, _) in CF_TILES:
            for h in range(2):
                order.add(("in", l, name, h), "AV"[h])
        for j in range(NT):
            order.add(("vt", l, j), "A")
        for kind in range(2):
            for d in range(2):
                for ct in range(2):
                    for h in range(2):
                        order.add(("up", l, kind, d, ct, h), "A")
        for ct in range(2):
            for h in range(2):
                order.add(("kks", l, ct, h), "A")
        for ct in range(2):
            for h in range(2):
                order.add(("bonus", l, ct, h), "V")
        order.add(("ckt", l), "V")
        for j in range(NT):
            order.add(("qt", l, j), "V")
        for j in range(NT):
            for h in range(NQ):
                order.add(("qk", l, j, h), "V")
            if MOD_FIRST + 2 * j < MOD_ITEMS:
                order.add(("mod", l, MOD_FIRST + 2 * j), "A")
            for h in range(NQ):
                order.add(("pt", l, j, h), "AV"[h % 2])
            if MOD_FIRST + 2 * j < MOD_ITEMS:
                order.add(("mod", l, MOD_FIRST + 2 * j + 1), "A")
            order.add(("pv", l, j), "V")
            order.add(("ot", l, j), "A")
        for j in range(NT):
            order.add(("f1", l, j), "AV"[j % 2])
        order.add(("f2c", l), "A")
        for ct in range(2):
            order.add(("f2", l, ct), "AV"[ct])
        for step in STEPS:
            if step[:2] == ("s", 0):
                order.add(("si", l, step[2]), "V")
            for name, engine in (("ab", "V"), ("ak", "V"), ("dd", "V"), ("tz", "A"), ("tb", "A"),
                                 ("n2", "A"), ("d2", "A"), ("akv", "V"), ("x2", "V"), ("n4", "A"), ("d4", "A"),
                                 ("x4", "V"), ("d8", "A"), ("x8", "V"), ("x8t", "A"), ("g1", "A"),
                                 ("y1", "V"), ("y1t", "A"), ("g2", "A"), ("y2", "V"), ("wp", "A"),
                                 ("rh", "V"), ("mt", "V"), ("s0", "V"), ("s1", "V"), ("yy", "V")):
                for hp in range(2):
                    order.add((name, l, step, hp), engine)
            if step[0] == "c":
                order.add(("so", l, step[2]), "V")
        for ct in range(2):
            for h in range(2):
                order.add(("mu", l, ct, h), "V")
        for ct in range(2):
            for h in range(2):
                order.add(("var", l, ct, h), "A")
        for ct in range(2):
            for h in range(2):
                order.add(("gup", l, ct, h), "V")
        for dt in range(KT):
            for h in range(2):
                order.add(("out", l, dt, h), "V")
        for h in range(2):
            order.add(("ss2", l, h), "A")
        if l == 0:
            for p, (_, nf) in enumerate(DENSE_PARTS):
                for f in range(nf):
                    for q in range(2):
                        for h in range(2):
                            order.add(("du", p, f, q, h), "AV"[q])
                for c in range(4):
                    for t in range(2):
                        for h in range(2):
                            order.add(("dn", p, c, t, h), "V")
        else:
            order.add(("router", l), "V")
            order.add(("pos", l), "V")
            for j in range(NT):
                for q in range(2):
                    order.add(("ht", j, q), "V")
    for j in range(NT):
        for q in range(2):
            order.add(("y", j, q), "AV"[q])


def build(nc, a, outs):
    y_prompt, y_sample, new_k, new_v, new_s = outs
    with ExitStack() as ctx:
        def sb(name, cols):
            return ctx.enter_context(nc.sbuf_tensor(name, [P, cols], F32))

        def sem(name):
            return ctx.enter_context(nc.semaphore(name))

        def view(t, at, *dims):
            n = int(np.prod(dims))
            v = t[:, at:at + n]
            if len(dims) == 1:
                return v
            names = "abcde"[:len(dims)]
            spec = f"p ({' '.join(names)}) -> p {' '.join(names)}"
            return v.rearrange(spec, **{x: int(s) for x, s in zip(names[:-1], dims[:-1])})

        const = sb("const", NCONST)
        xT = view(sb("x_resid", KT * TOK), 0, KT, TOK)
        ring = sb("ring", 2 * SLOT)
        rs = sb("rms", TOK)[:, :]
        par_rows = rs[:, 0:P]
        par_t = sb("params", NROWS + 96 + 16 + 16 + 132 + 256 + 64 + 280 + 58 + 96)
        at = [0]

        def small(*dims):
            v = view(par_t, at[0], *dims)
            at[0] += int(np.prod(dims))
            return v

        cst = lambda name, n, off=0: const[:, CC[name] + off:CC[name] + off + n]
        ident, ones, blk = cst("ident", P), cst("ones", P), cst("blk", P)

        par = small(NROWS)
        mod = small(48, 2)
        silu_c = small(KT, 2)
        amul = small(KT, 2)
        qnw = small(HD)
        knw = small(HD)
        sink = small(NQ)
        g_up = small(256)
        router_w = small(KT, NE)
        rt_l, rt_key, rt_first, rt_second, gates, rt_t, posm = (small(NT, NE) for _ in range(7))
        cur_pos, cur_gate = small(2, NT), small(2, NT)
        gs_part, gslot = small(2, 2, 2), small(2, 2)
        rt_cnt, rt_m = small(NE), small(4)
        stat = small(96)

        HT, MIX = 0, KT * TOK
        T1 = MIX + KT * TOK
        T2 = T1 + 8960
        SPARE = T2 + 11264
        guard = nc.sbuf_tensor("arena", [P, SPARE + 3 * TOK], F32)
        arena = guard.__enter__()
        guard.__exit__(None, None, None)
        hT = view(arena, HT, KT, TOK)
        x_tok = view(arena, HT, NT, D)

        mixT = view(arena, MIX, KT, TOK)
        rank_up = view(arena, MIX + 4 * TOK, 4, 256)
        yT = mixT[:, 4:6, :]
        T3 = HT
        rT = view(arena, T1, 2, TOK)
        kT_ = view(arena, T1 + 1280, 2, TOK)
        vT = view(arena, T1 + 2560, 2, TOK)
        kkT = view(arena, T1 + 3840, 2, TOK)
        v_tok = view(arena, T1 + 5120, NT, 4, HD)
        waT = view(arena, T1 + 6400, TOK)
        gdT = view(arena, T1 + 7040, TOK)
        tmp = view(arena, T1 + 7680, 2, TOK)
        bxT = view(arena, T2, 2, TOK)
        bbT = view(arena, T2 + 1280, 2, TOK)
        bcT = view(arena, T2 + 2560, 2, TOK)
        lw = view(arena, T2, 2, 2, TOK)
        aT = view(arena, T2 + 2560, 2, 2, TOK)
        T2b = T2 + 5120
        qkv = view(arena, T2b, NT, 512)
        fT = view(arena, T2b + 2560, 2, TOK)
        qT = view(arena, T3, 2, TOK)
        kT = view(arena, T3 + 1280, TOK)
        ck_tok = view(arena, T3 + 1920, P)
        cv_tok = view(arena, T3 + 2048, P)
        ckT = view(arena, T3 + 2176, P)
        sc = view(arena, T3 + 2304, NQ, 512)
        qk_sq = view(arena, T3 + 2304, NT, 384)
        qk_t = view(arena, T3 + 2304, 2, 6, HD)
        rope = view(arena, T3 + 3072, 4, 6, 2, 16)
        conv_u = view(arena, SPARE, 2, TOK + 4)
        o_tok = view(arena, T3 + 4352, 4, HD)
        v1 = view(arena, T3 + 2304, NT, 2, 256)
        pT = [view(arena, SPARE + 512 * h, 4, P) for h in range(3)] + [view(arena, T3 + 4608, 4, P)]
        s0_in = view(arena, T1 + 7680, 2, 2, P)
        s_fin = view(arena, T1 + 7680 + 512, 2, 2, P)

        free = [(T2b, SPARE), (T3, T3 + 5120), (SPARE, SPARE + 1920)]

        def wk(*dims):
            n = int(np.prod(dims))
            for i, (lo, hi) in enumerate(free):
                if hi - lo >= n:
                    free[i] = (lo + n, hi)
                    return view(arena, lo, *dims)
            raise ValueError("no room")

        AB, AK = wk(2, 2, 256), wk(2, 2, 256)
        EX = [wk(2, 3, P) for _ in range(2)]
        ST = wk(2, 3, P)
        DD, ND, D2, N2, O32, O64, XA, XB = (wk(2, 2, P) for _ in range(8))
        RR, WP = wk(2, 2, P), wk(2, 2, P)
        BP, KP = wk(2, 2, P), wk(2, 2, P)
        BM = wk(2, 2, P)
        BC, KC = wk(2, 2, P), wk(2, 2, P)
        BT, KD, RH = wk(2, P), wk(2, P), wk(2, P)
        att = view(par_t, at[0] - 96, 2, 24)
        qk_ss = view(par_t, at[0] - 48, NT * 6)
        LC = view(par_t, at[0] - 18, 2, 2, 2)
        omka = view(par_t, at[0] - 10, 2)

        def sbr(name, cols):
            return ctx.enter_context(nc.sbuf_tensor(name, [P, cols], F32R))

        GW = 6144
        g_hi, g_lo = sbr("g_hi", GW), sbr("g_lo", GW)
        h_hi, h_lo = sbr("h_hi", KT * TOK), sbr("h_lo", KT * TOK)
        w_hi, w_lo = sbr("w_hi", 2 * CHUNK), sbr("w_lo", 2 * CHUNK)
        sel_t = sbr("select", NT * CAP + 2 * TOK)
        silt = sb("silu", 2 * TOK)
        f32 = lambda x: x.bitcast(F32)
        sil = view(silt, 0, 2, TOK)
        sel = view(sel_t, 0, NT, CAP)
        selT = view(sel_t, NT * CAP, 2, TOK)
        e_sil = view(silt, 0, 2, CAP)
        junk = view(silt, 2 * CAP, 2, 3 * P)
        xg = [view(t, 0, KT, CAP) for t in (g_hi, g_lo)]
        eg = [view(t, KT * CAP, EXP_F, CAP) for t in (g_hi, g_lo)]
        yg = [view(t, 2 * KT * CAP, 2, D) for t in (g_hi, g_lo)]
        dg = [view(t, 0, 8, TOK) for t in (g_hi, g_lo)]
        hc = [view(t, 0, KT, TOK) for t in (h_hi, h_lo)]
        ht = [view(t, 0, NT, D) for t in (h_hi, h_lo)]
        rounds_t = ctx.enter_context(nc.sbuf_tensor("rounds", [P, 2], mybir.dt.int32))

        psum = [ctx.enter_context(nc.psum_tensor(f"bank{i}", [P, 512], F32)) for i in range(BANKS)]

        filled = sem("bank_filled")
        emptied = {"A": sem("emptied_by_scalar"), "V": sem("emptied_by_vector")}
        order = Order(filled, emptied)
        list_groups(order)
        order2 = PairOrder(sem("pair_filled"), {"V": sem("pair_emptied")})
        list_pair_groups(order2)

        s_const, s_x, s_par = sem("const_in"), sem("x_in"), sem("params_in")
        s_ring = [sem(f"ring_in{i}") for i in range(2)]
        s_moditem = sem("mod_item_used")
        s_rank, s_gup_in, s_cache, s_state = sem("rank_weights_in"), sem("small_weights_in"), sem("cache_in"), sem("state_in")
        s_zero = sem("buffers_zeroed")
        s_silc, s_sq, s_hmul, s_h = sem("silu_c_ready"), sem("squares_ready"), sem("h_scaled"), sem("h_ready")
        s_kkr, s_kq, s_rk = sem("kk_raw"), sem("kk_squared"), sem("rk_ready")
        s_qsq, s_qss, s_qrt, s_qk, s_rope = (sem("qk_squares"), sem("qk_sumsq"), sem("qk_root"), sem("qk_normed"),
                                             sem("qk_roped"))
        s_max, s_exp = sem("row_max_ready"), sem("exp_done")
        s_cu, s_conv = sem("conv_gated"), sem("conv_done")
        s_sum, s_ex, s_pad, s_tri = sem("decay_sums"), sem("decay_exp"), sem("scaled_ready"), sem("triangles_ready")
        s_st0 = sem("state_zeroed")
        s_nkk = sem("kk_normed")
        s_gn, s_gsq = sem("y_centred"), sem("y_squared")
        s_kv_out, s_state_out, s_y_out = sem("kv_stored"), sem("states_stored"), sem("y_stored")
        s_hi, s_lo, s_sil, s_ghi = sem("weights_hi"), sem("weights_lo"), sem("silu_done"), sem("g_hi_done")
        s_glo = sem("g_lo_done")
        s_hhi, s_hlo = sem("h_hi_done"), sem("h_lo_done")
        s_rmax, s_rexp, s_rounds = sem("router_max"), sem("router_exp"), sem("rounds_ready")
        s_moe_done = sem("experts_done")
        s_ring2 = [sem(f"pair_ring_in{i}") for i in range(2)]
        s_hi2, s_lo2, s_sil2, s_ghi2, s_glo2 = (sem("pair_weights_hi"), sem("pair_weights_lo"), sem("pair_silu"),
                                               sem("pair_g_hi"), sem("pair_g_lo"))
        s_sel, s_xhi, s_gs, s_yhi, s_half = (sem("select_ready"), sem("gathered_hi"), sem("slot_gates"),
                                             sem("expert_out_hi"), sem("down_half_used"))
        s_ca, s_cv, s_cp = sem("scalar_chain"), sem("vector_chain"), sem("pool_chain")

        block = ctx.enter_context(nc.Block())

        items = []
        for l in range(DEPTH):
            for i in range(MOD_FIRST):
                items.append(("mod", l, i))
            for i in range(5):
                items.append(("win", l, i))
            for i in range(MOD_FIRST, MOD_ITEMS):
                items.append(("mod", l, i))
            items.append(("dft", l, 0))
            for i in range(2):
                items.append(("wout", l, i))
            if l == 0:
                for p, (_, nf) in enumerate(DENSE_PARTS):
                    for i in range(nf // 2):
                        items.append(("up", l, p, i))
                    for i in range(2):
                        items.append(("down", l, p, i))
        number = {it: n for n, it in enumerate(items)}

        def load_count(name):
            return 32 * (number[name] // 2 + 1)

        chunks = [(p, kind, i) for p, (_, nf) in enumerate(DENSE_PARTS)
                  for kind, n in (("up", nf), ("down", 4)) for i in range(n)]
        chunk_no = {c: n for n, c in enumerate(chunks)}

        def item(name):
            return (number[name] % 2) * SLOT

        def wait_item(eng, name):
            eng.wait_ge(s_ring[number[name] % 2], load_count(name))

        def wait_used(sp, name):
            kind, l = name[:2]
            if kind == "mod":
                if name[2] < MOD_FIRST - 1:
                    sp.wait_ge(s_moditem, l * (MOD_FIRST - 1) + name[2] + 1)
                elif name[2] == MOD_FIRST - 1:
                    order.wait_filled(sp, ("mod", l))
                else:
                    order.wait_filled(sp, ("mod", l, name[2]))
            elif kind == "win":
                i = name[2]
                if i == 2:
                    order.wait_filled(sp, ("qkv", l, NT - 1))
                else:
                    order.wait_filled(sp, ("in", l, [t for t in IN_TILES if t[1] == i][-1][0], 1))
            elif kind == "dft":
                order.wait_filled(sp, ("f2", l, 1))
            elif kind == "wout":
                order.wait_filled(sp, ("out", l, 4 * name[2] + 3, 1))
            else:
                sp.wait_ge(s_lo, chunk_no[(name[2], kind, 2 * name[3] + 1)] + 1)

        @block.sync
        def _(sp):
            sp.dma_start(const[:], a["const"]).then_inc(s_const, 16)
            sp.dma_start(x_tok[:, 0, :], a["x_prompt"][0]).then_inc(s_x, 16)
            sp.dma_start(x_tok[:, 1:NT, :], a["x_sample"][0].rearrange("(j p) n -> p j n", p=P)).then_inc(s_x, 16)

            def load(name):
                n = number[name]
                if n >= 2:
                    wait_used(sp, items[n - 2])
                kind, l = name[:2]
                s, base = n % 2, item(name)
                if kind == "mod":
                    w = view(ring, base, KT, 512)
                    src = a["mod_w"][l].rearrange("(k p) n -> p k n", p=P)[:, :, 512 * name[2]:512 * (name[2] + 1)]
                    pieces = [(w[:, 4 * i:4 * i + 4, :], src[:, 4 * i:4 * i + 4, :]) for i in range(2)]
                elif kind == "win":
                    i = name[2]
                    src = a["w_in"][l].rearrange("(k p) n -> p k n", p=P)
                    if i < 4:
                        lo, n_ = [(1280, 512), (1792, 448), (0, 512), (512, 512)][i]
                        w = view(ring, base, KT, n_)
                        pieces = [(w[:, 4 * q:4 * q + 4, :], src[:, 4 * q:4 * q + 4, lo:lo + n_]) for q in range(2)]
                    else:
                        w = view(ring, base, KT, 512)
                        pieces = [(w[:, :, 0:256], src[:, :, 1024:1280]), (w[:, :, 256:512], src[:, :, 2240:2496])]
                elif kind == "dft":
                    w = view(ring, base, 2, 4, 512)
                    pieces = [(w[:, i], a["dft"][i].rearrange("(j p) n -> p j n", p=P)) for i in range(2)]
                elif kind == "wout":
                    i = name[2]
                    w = view(ring, base, KT, 512)
                    src = a["w_out"][l].rearrange("(k p) n -> p k n", p=P)[:, :, 512 * i:512 * (i + 1)]
                    pieces = [(w[:, 4 * q:4 * q + 4, :], src[:, 4 * q:4 * q + 4, :]) for q in range(2)]
                elif kind == "up":
                    _, _, p, i = name
                    w = view(ring, base, 2, KT, 256)
                    f0 = P * (DENSE_PARTS[p][0] + 2 * i)
                    pieces = [(w[:, q], a[nm][0].rearrange("(k p) n -> p k n", p=P)[:, :, f0:f0 + 256])
                              for q, nm in enumerate(("ffn_w1", "ffn_w3"))]
                else:
                    _, _, p, i = name
                    f0, nf = DENSE_PARTS[p]
                    w = view(ring, base, nf, 512)
                    src = a["ffn_w2"][0].rearrange("(k p) n -> p k n", p=P)[:, f0:f0 + nf, 512 * i:512 * (i + 1)]
                    pieces = [(w[:, :nf // 2], src[:, :nf // 2]), (w[:, nf // 2:], src[:, nf // 2:])]
                for dst, src in pieces:
                    sp.dma_start(dst, src).then_inc(s_ring[s], 16)

            for l in range(DEPTH):
                if l > 0:
                    sp.wait_ge(s_h, 2 * l)
                vec = [("mod_b", a["mod_b"][l].rearrange("(r p) -> r p", p=P)),
                       ("norm1", a["norm1_w"][l].rearrange("(r p) -> r p", p=P)),
                       ("norm2", a["norm2_w"][l].rearrange("(r p) -> r p", p=P)),
                       ("conv", a["conv_w"][l].rearrange("t (r p) -> (t r) p", p=P)),
                       ("w0", a["rwkv_w0"][l].rearrange("d (r p) -> (d r) p", p=P)),
                       ("a0", a["rwkv_a0"][l].rearrange("d (r p) -> (d r) p", p=P)),
                       ("k_k", a["rwkv_k_k"][l].rearrange("(r p) -> r p", p=P)),
                       ("k_a", a["rwkv_k_a"][l].rearrange("(r p) -> r p", p=P)),
                       ("r_k", a["rwkv_r_k"][l].rearrange("(r q) p -> r (q p)", q=2)),
                       ("ln_w", a["rwkv_ln_w"][l].rearrange("(r p) -> r p", p=P)),
                       ("ln_b", a["rwkv_ln_b"][l].rearrange("(r p) -> r p", p=P)),
                       ("c_ctx", a["c_ctx"].rearrange("(r p) -> r p", p=P)),
                       ("c", a["c"][0].rearrange("(r p) -> r p", p=P))]
                for name, src in vec:
                    n = src.shape[0]
                    sp.dma_start(par_rows[ROW[name]:ROW[name] + n, :], src).then_inc(s_par, 16)
                for i in range(MOD_FIRST):
                    load(("mod", l, i))
                sp.wait_ge(s_zero, 2 * l + 1)
                for d in range(2):
                    sp.dma_start(rank_up[32 * d:32 * d + 32, d, :], a["rwkv_w_up"][l, d]).then_inc(s_rank, 16)
                    sp.dma_start(rank_up[64 + 32 * d:96 + 32 * d, 2 + d, :], a["rwkv_a_up"][l, d]).then_inc(s_rank, 16)
                sp.dma_start(g_up[0:64, :], a["rwkv_g_up"][l]).then_inc(s_gup_in, 16)
                sp.dma_start(qnw, a["q_norm_w"][l][None, :].broadcast_to([P, HD])).then_inc(s_gup_in, 16)
                sp.dma_start(knw, a["k_norm_w"][l][None, :].broadcast_to([P, HD])).then_inc(s_gup_in, 16)
                sp.dma_start(sink, a["attn_sink"][l][None, :].broadcast_to([P, NQ])).then_inc(s_gup_in, 16)
                sp.dma_start(router_w, a["router_w"][0].rearrange("(k p) e -> p k e", p=P)).then_inc(s_gup_in, 16)
                for i in range(5):
                    load(("win", l, i))
                order.wait_filled(sp, ("in", l, CF_TILES[-1][0], 1))
                sp.dma_start(ck_tok, a["cache_k"][0, l].rearrange("t h d -> t (h d)")).then_inc(s_cache, 16)
                sp.dma_start(cv_tok, a["cache_v"][0, l].rearrange("t h d -> t (h d)")).then_inc(s_cache, 16)
                for i in range(MOD_FIRST, MOD_ITEMS):
                    load(("mod", l, i))
                load(("dft", l, 0))
                load(("wout", l, 0))
                load(("wout", l, 1))
                for it in items:
                    if it[1] == l and it[0] in ("up", "down"):
                        load(it)
            for it in items[-2:]:
                wait_used(sp, it)
            sp.wait_ge(s_rounds, 1)
            rounds = sp.value_load(rounds_t[0:1, 0:1], min_val=1, max_val=MAX_ROUNDS)
            with sp.Fori(0, rounds) as r:
                with sp.Fori(0, NE // 2) as pair:
                    it = r * (NE // 2) + pair
                    for n in range(PAIR_ITEMS):
                        k, i = n // (PAIR_ITEMS // 2), n % (PAIR_ITEMS // 2)
                        e = 2 * pair + k
                        sp.wait_ge(s_lo2, (it + 1) * 2 * EXP_CHUNKS + 2 * (n - 1))
                        if i < EXP_F // 2:
                            w = view(ring, ((n + len(items)) % 2) * SLOT, 2, KT, 256)
                            pieces = [(w[:, q], a[nm][0, bass.ds(e, 1)].rearrange("e (k p) n -> p (e k) n", p=P)
                                       [:, :, 256 * i:256 * (i + 1)]) for q, nm in enumerate(("moe_w1", "moe_w3"))]
                        else:
                            i -= EXP_F // 2
                            w = view(ring, ((n + len(items)) % 2) * SLOT, EXP_F, 512)
                            src = a["moe_w2"][0, bass.ds(e, 1)].rearrange("e (k p) n -> p (e k) n", p=P)
                            pieces = [(w[:, q:q + 4], src[:, q:q + 4, 512 * i:512 * (i + 1)]) for q in (0, 4)]
                        for dst, src in pieces:
                            sp.dma_start(dst, src).then_inc(s_ring2[n % 2], 16)
            for j in range(NT):
                for q in range(2):
                    order.wait_emptied(sp, ("y", j, q))
                dst = y_prompt[0] if j == 0 else y_sample[0, P * (j - 1):P * j, :]
                sp.dma_start(dst, x_tok[:, j, :]).then_inc(s_y_out, 16)
            sp.wait_ge(s_y_out, 16 * NT)
            sp.wait_ge(s_kv_out, DEPTH * 2 * 16)
            sp.wait_ge(s_state_out, DEPTH * 8 * 16)

        @block.tensor
        def _(pe):
            mm, tr = nc.tensor.matmul, nc.tensor.transpose

            def end(ins):
                ins.then_inc(filled, 1)

            pe.wait_ge(s_const, 16)
            pe.wait_ge(s_x, 32)
            for j in range(NT):
                for q in range(2):
                    b = psum[order.open(pe, ("x", j, q))]
                    for k in range(4):
                        ins = tr(b[:, P * k:P * k + P], x_tok[:, j, P * (4 * q + k):P * (4 * q + k) + P], ident)
                    end(ins)

            def sum_squares(name, l, nth):
                pe.wait_ge(s_sq, nth)
                for h in range(2):
                    b = psum[order.open(pe, (name, l, h))]
                    for k in range(KT):
                        ins = mm(b[:, 0:HALF], ones, hT[:, k, HALF * h:HALF * (h + 1)], start=(k == 0), stop=(k == KT - 1))
                    end(ins)

            def in_tiles(l, tiles):
                at_item = None
                for name, it, col in tiles:
                    if it != at_item:
                        at_item = it
                        wait_item(pe, ("win", l, it))
                    width = {1: 448}.get(it, 512)
                    w = view(ring, item(("win", l, it)), KT, width)
                    m = 64 if name[0] == "gd" else P
                    for h in range(2):
                        b = psum[order.open(pe, ("in", l, name, h))]
                        for k in range(KT):
                            ins = mm(b[0:m, 0:HALF], w[:, k, col:col + m], hT[:, k, HALF * h:HALF * (h + 1)],
                                     start=(k == 0), stop=(k == KT - 1))
                        end(ins)

            def split3(out, lhs, rhs, first, last):
                for i, (x, y) in enumerate(((0, 0), (0, 1), (1, 0))):
                    ins = mm(out, lhs[x], rhs[y], start=(first and i == 0), stop=(last and i == 2))
                return ins

            def weights(n, *dims):
                return [view(t, (n % 2) * CHUNK, *dims) for t in (w_hi, w_lo)]

            def dense():
                pe.wait_ge(s_hlo, KT)
                for p, (_, nf) in enumerate(DENSE_PARTS):
                    for f in range(nf):
                        n = chunk_no[(p, "up", f)]
                        pe.wait_ge(s_lo, n + 1)
                        w = weights(n, 2, KT, P)
                        for q in range(2):
                            for h in range(2):
                                b = psum[order.open(pe, ("du", p, f, q, h))]
                                cols = slice(HALF * h, HALF * (h + 1))
                                for k in range(KT):
                                    ins = split3(b[:, 0:HALF], [x[:, q, k, :] for x in w], [x[:, k, cols] for x in hc],
                                                 k == 0, k == KT - 1)
                                end(ins)
                    pe.wait_ge(s_glo, sum(x[1] for x in DENSE_PARTS[:p + 1]))
                    for c in range(4):
                        n = chunk_no[(p, "down", c)]
                        pe.wait_ge(s_lo, n + 1)
                        w = weights(n, nf, 256)
                        for t in range(2):
                            for h in range(2):
                                b = psum[order.open(pe, ("dn", p, c, t, h))]
                                cols = slice(HALF * h, HALF * (h + 1))
                                for f in range(nf):
                                    ins = split3(b[:, 0:HALF], [x[:, f, P * t:P * t + P] for x in w],
                                                 [x[:, f, cols] for x in dg], f == 0, f == nf - 1)
                                end(ins)

            def experts():
                o = order2
                pe.sem_inc(o.filled, len(o.by))
                pe.sem_inc(s_half, 4)
                pe.wait_ge(s_rounds, 1)
                rounds = pe.value_load(rounds_t[0:1, 0:1], min_val=1, max_val=MAX_ROUNDS)
                with pe.Fori(0, rounds) as r:
                    with pe.Fori(0, NE // 2) as pair:
                        it = r * (NE // 2) + pair

                        def end2(ins):
                            ins.then_inc(o.filled, 1)

                        def spread(k):
                            pe.wait_ge(s_sel, 2 * it + k + 1)
                            for b4 in range(4):
                                b = psum[o.open(pe, ("bc", k, b4), it)]
                                src = cur_pos if b4 < 2 else cur_gate
                                lo, n = ((0, 3), (3, 2))[b4 % 2]
                                for j in range(n):
                                    ins = mm(b[:, P * j:P * j + P], src[:, k, lo + j:lo + j + 1].broadcast_to([P, P]),
                                             ident, start=True, stop=True)
                                end2(ins)

                        def gather(k):
                            pe.wait_ge(s_sel, 2 * it + k + 1)
                            for b4 in range(4):
                                b = psum[o.open(pe, ("ga", k, b4), it)]
                                for t in range(2):
                                    d = 2 * b4 + t
                                    for j in range(NT):
                                        for x in range(2):
                                            ins = mm(b[:, CAP * t:CAP * t + CAP], ht[x][:, j, P * d:P * d + P], sel[:, j, :],
                                                     start=(j + x == 0), stop=(j == NT - 1 and x == 1))
                                end2(ins)

                        def scatter(k):
                            o.wait_emptied(pe, ("dw", k, 1, 1), it)
                            o.wait_emptied(pe, ("bc", k, 1), it)
                            for dt in range(KT):
                                for h in range(2):
                                    b = psum[o.open(pe, ("sc", k, dt, h), it)]
                                    for q in range(2):
                                        for x in range(2):
                                            ins = mm(b[:, 0:HALF], yg[x][:, q, P * dt:P * dt + P],
                                                     selT[:, q, HALF * h:HALF * (h + 1)],
                                                     start=(q + x == 0), stop=(q + x == 2))
                                    end2(ins)

                        for k in range(2):
                            spread(k)
                            if k == 0:
                                gather(0)
                            o.wait_emptied(pe, ("ga", k, 3), it)
                            for f in range(EXP_F):
                                n = EXP_CHUNKS * k + f
                                pe.wait_ge(s_lo2, (it + 1) * 2 * EXP_CHUNKS + n + 1)
                                w = weights(n, 2, KT, P)
                                b = psum[o.open(pe, ("up", k, f), it)]
                                for q in range(2):
                                    for kt in range(KT):
                                        ins = split3(b[:, CAP * q:CAP * q + CAP], [x[:, q, kt, :] for x in w],
                                                     [x[:, kt, :] for x in xg], kt == 0, kt == KT - 1)
                                end2(ins)
                            pe.wait_ge(s_glo2, (2 * it + k + 1) * EXP_F)
                            for i in range(2):
                                banks = [psum[o.open(pe, ("dw", k, i, q), it)] for q in range(2)]
                                for c in range(2):
                                    n = EXP_CHUNKS * k + EXP_F + 2 * i + c
                                    pe.wait_ge(s_lo2, (it + 1) * 2 * EXP_CHUNKS + n + 1)
                                    w = weights(n, 4, 512)
                                    for q in range(2):
                                        for f in range(4):
                                            ins = split3(banks[q][:, :], [x[:, 4 * c + f, P * q:P * q + P] for x in eg],
                                                         [x[:, f, :] for x in w], c + f == 0, c + f == 4)
                                        if c == 1:
                                            end2(ins)
                                    if c == 0:
                                        ins.then_inc(s_half, 1)
                            if k == 0:
                                gather(1)
                            scatter(k)

            for l in range(DEPTH):
                pe.wait_ge(s_par, (l + 1) * 16 * len(ROWS))
                b = psum[order.open(pe, ("params", l))]
                end(tr(b[:, 0:NROWS], par_rows[0:NROWS, :], ident[0:NROWS, 0:NROWS]))
                pe.wait_ge(s_silc, l + 1)
                b = psum[order.open(pe, ("mod", l))]
                for i in range(MOD_FIRST):
                    wait_item(pe, ("mod", l, i))
                    w = view(ring, item(("mod", l, i)), KT, 512)
                    for t in range(4):
                        c0 = 2 * (4 * i + t)
                        for k in range(KT):
                            ins = mm(b[:, c0:c0 + 2], w[:, k, P * t:P * t + P], silu_c[:, k, :],
                                     start=(k == 0), stop=(k == KT - 1))
                    if i < MOD_FIRST - 1:
                        ins.then_inc(s_moditem, 1)
                    else:
                        end(ins)
                sum_squares("ss1", l, 2 * l + 1)
                pe.wait_ge(s_h, 2 * l + 1)
                in_tiles(l, RW_TILES)
                wait_item(pe, ("win", l, 2))
                w = view(ring, item(("win", l, 2)), KT, 512)
                for j in range(NT):
                    b = psum[order.open(pe, ("qkv", l, j))]
                    for k in range(KT):
                        ins = mm(b[:, :], hT[:, k, P * j:P * j + P], w[:, k, :], start=(k == 0), stop=(k == KT - 1))
                    end(ins)
                in_tiles(l, CF_TILES)
                for ct in range(2):
                    for h in range(2):
                        order.wait_emptied(pe, ("in", l, ("v", ct), h))
                for j in range(NT):
                    b = psum[order.open(pe, ("vt", l, j))]
                    for ct in range(2):
                        ins = tr(b[:, P * ct:P * ct + P], vT[:, ct, P * j:P * j + P], ident)
                    end(ins)
                pe.wait_ge(s_rank, 16 * 4 * (l + 1))
                for h in range(2):
                    order.wait_emptied(pe, ("in", l, ("wa", 0), h))
                for kind in range(2):
                    for d in range(2):
                        for ct in range(2):
                            for h in range(2):
                                b = psum[order.open(pe, ("up", l, kind, d, ct, h))]
                                end(mm(b[:, 0:HALF], rank_up[:, 2 * kind + d, P * ct:P * ct + P],
                                       waT[:, HALF * h:HALF * (h + 1)], start=True, stop=True))
                pe.wait_ge(s_kq, l + 1)
                for ct in range(2):
                    for h in range(2):
                        b = psum[order.open(pe, ("kks", l, ct, h))]
                        end(mm(b[:, 0:HALF], blk, tmp[:, ct, HALF * h:HALF * (h + 1)], start=True, stop=True))
                pe.wait_ge(s_rk, l + 1)
                for ct in range(2):
                    for h in range(2):
                        b = psum[order.open(pe, ("bonus", l, ct, h))]
                        end(mm(b[:, 0:HALF], blk, tmp[:, ct, HALF * h:HALF * (h + 1)], start=True, stop=True))
                def modulation(i):
                    if i >= MOD_ITEMS:
                        return
                    wait_item(pe, ("mod", l, i))
                    w = view(ring, item(("mod", l, i)), KT, 512)
                    b = psum[order.open(pe, ("mod", l, i))]
                    for t in range(4):
                        for k in range(KT):
                            ins = mm(b[:, 2 * t:2 * t + 2], w[:, k, P * t:P * t + P], silu_c[:, k, :],
                                     start=(k == 0), stop=(k == KT - 1))
                    end(ins)

                pe.wait_ge(s_cache, 32 * (l + 1))
                b = psum[order.open(pe, ("ckt", l))]
                end(tr(b[:, 0:P], ck_tok, ident))
                for j in range(NT):
                    if j == 0:
                        pe.wait_ge(s_qk, l * NT + 1)
                    else:
                        pe.wait_ge(s_rope, l * (NT - 1) + j)
                    b = psum[order.open(pe, ("qt", l, j))]
                    for t in range(3):
                        ins = tr(b[:, P * t:P * t + P], qkv[:, j, P * t:P * t + P], ident)
                    end(ins)
                order.wait_emptied(pe, ("ckt", l))
                for j in range(NT):
                    order.wait_emptied(pe, ("qt", l, j))
                for j in range(NT):
                    blocks = key_blocks(j)
                    for h in range(NQ):
                        kv, g = h // 2, h % 2
                        r0 = HD * kv
                        b = psum[order.open(pe, ("qk", l, j, h))]
                        for pos, kb in blocks:
                            rhs = ckT[r0:r0 + HD, :] if kb is None else kT[r0:r0 + HD, P * kb:P * kb + P]
                            ins = mm(b[:, P * pos:P * pos + P], qT[r0:r0 + HD, g, P * j:P * j + P], rhs,
                                     start=True, stop=True)
                        end(ins)
                    modulation(MOD_FIRST + 2 * j)
                    pe.wait_ge(s_exp, l * NT + j + 1)
                    for h in range(NQ):
                        b = psum[order.open(pe, ("pt", l, j, h))]
                        for pos, kb in blocks:
                            ins = tr(b[:, P * pos:P * pos + P], sc[:, h, P * pos:P * pos + P], ident)
                        end(ins)
                    modulation(MOD_FIRST + 2 * j + 1)
                    b = psum[order.open(pe, ("pv", l, j))]
                    for h in range(NQ):
                        order.wait_emptied(pe, ("pt", l, j, h))
                        kv = h // 2
                        for i, (pos, kb) in enumerate(blocks):
                            v = cv_tok if kb is None else qkv[:, kb, 384:512]
                            ins = mm(b[:, HD * h:HD * h + HD], pT[h][:, pos, :], v[:, HD * kv:HD * kv + HD],
                                     start=(i == 0), stop=(i == len(blocks) - 1))
                    end(ins)
                    order.wait_emptied(pe, ("pv", l, j))
                    b = psum[order.open(pe, ("ot", l, j))]
                    for t in range(2):
                        ins = tr(b[:, P * t:P * t + P], o_tok[:, 2 * t:2 * t + 2, :], ident)
                    end(ins)
                for ct in range(2):
                    for h in range(2):
                        order.wait_emptied(pe, ("in", l, ("f", ct), h))
                for j in range(NT):
                    b = psum[order.open(pe, ("f1", l, j))]
                    for ct in range(2):
                        ins = mm(b[:, 256 * ct:256 * ct + 256], fT[:, ct, P * j:P * j + P], cst("dft64", 256),
                                 start=True, stop=True)
                    end(ins)
                for j in range(NT):
                    order.wait_emptied(pe, ("f1", l, j))
                b = psum[order.open(pe, ("f2c", l))]
                for ct in range(2):
                    for cs in range(2):
                        ins = mm(b[:, P * ct:P * ct + P], v1[:, 0, ct, P * cs:P * cs + P],
                                 cst("dft128", P, P * cs), start=(cs == 0), stop=(cs == 1))
                end(ins)
                wait_item(pe, ("dft", l, 0))
                w = view(ring, item(("dft", l, 0)), 2, 4, 512)
                for ct in range(2):
                    b = psum[order.open(pe, ("f2", l, ct))]
                    for j in range(4):
                        for cs in range(2):
                            ins = mm(b[:, :], v1[:, 1 + j, ct, P * cs:P * cs + P], w[:, cs, j, :],
                                     start=(j + cs == 0), stop=(j + cs == 4))
                    end(ins)

                for j in range(NT):
                    order.wait_emptied(pe, ("vt", l, j))
                for n, step in enumerate(STEPS):
                    kind, i, d = step
                    j = step_tile(step)
                    T = lambda name, hp: (name, l, step, hp)
                    gn = l * len(STEPS) + n
                    if (kind, i) == ("s", 0):
                        pe.wait_ge(s_state, 16 * 8 * (l + 1))
                        b = psum[order.open(pe, ("si", l, d))]
                        for hp in range(2):
                            ins = tr(b[:, P * hp:P * hp + P], s0_in[:, d, hp, :], ident)
                        end(ins)
                    v0 = 2 * i if kind == "s" else 0
                    ver = lambda s: (v0 + s) % 3
                    pe.wait_ge(s_pad, gn + 1)
                    V = lambda hp, par: v_tok[:, j, 2 * hp + par, :]

                    def four(name, lhs, rhs, cols=P):
                        for hp in range(2):
                            b = psum[order.open(pe, T(name, hp))]
                            for par in range(2):
                                ins = mm(b[:, cols * par:cols * par + cols], lhs(hp, par), rhs(hp, par),
                                         start=True, stop=True)
                            end(ins)

                    E = EX[n % 2]
                    zr = lambda hp, par: E[:, hp, 0:2, :]
                    four("ab", lambda hp, par: BP[:, hp, par, :], zr, 256)
                    four("ak", lambda hp, par: KP[:, hp, par, :], zr, 256)
                    four("dd", lambda hp, par: E[:, hp, 0, :], lambda hp, par: BP[:, hp, par, :])
                    for hp in range(2):
                        b = psum[order.open(pe, T("tz", hp))]
                        end(tr(b[:, 0:P], E[:, hp, 0, :], ident))
                    for hp in range(2):
                        b = psum[order.open(pe, T("tb", hp))]
                        tr(b[:, 0:P], BT[:, hp], ident)
                        end(tr(b[:, P:2 * P], KD[:, hp], ident))
                    for hp in range(2):
                        order.wait_emptied(pe, T("dd", hp))
                    pe.wait_ge(s_tri, 2 * gn + 1)
                    sq = lambda B: (lambda hp, par: B[:, hp, par, :])
                    four("n2", sq(DD), sq(ND))
                    four("d2", sq(ND), sq(DD))
                    for hp in range(2):
                        order.wait_emptied(pe, T("ak", hp))
                    four("akv", lambda hp, par: AK[:, hp, par, 0:P], V, HD)
                    for hp in range(2):
                        order.wait_emptied(pe, T("d2", hp))
                        order.wait_emptied(pe, T("n2", hp))
                    pe.wait_ge(s_tri, 2 * gn + 2)
                    four("x2", sq(D2), sq(XA))
                    four("n4", sq(D2), sq(N2))
                    four("d4", sq(N2), sq(D2))
                    for hp in range(2):
                        order.wait_emptied(pe, T("x2", hp))
                        order.wait_emptied(pe, T("d4", hp))
                    four("x4", sq(DD), sq(XB))
                    four("d8", sq(ND), sq(DD))
                    for hp in range(2):
                        order.wait_emptied(pe, T("d8", hp))
                        order.wait_emptied(pe, T("x4", hp))
                    four("x8", sq(D2), sq(XA))

                    def flip(name, B):
                        for hp in range(2):
                            b = psum[order.open(pe, T(name, hp))]
                            for par in range(2):
                                ins = tr(b[:, P * par:P * par + P], B[:, hp, par, :], ident)
                            end(ins)

                    def emptied_pair(name):
                        for hp in range(2):
                            order.wait_emptied(pe, T(name, hp))

                    emptied_pair("x8")
                    flip("x8t", XB)
                    emptied_pair("x8t")
                    four("g1", sq(O32), sq(N2))
                    emptied_pair("g1")
                    four("y1", sq(ND), sq(XB))
                    emptied_pair("y1")
                    flip("y1t", XA)
                    emptied_pair("y1t")
                    four("g2", sq(O64), sq(N2))
                    emptied_pair("g2")
                    four("y2", sq(ND), sq(XA))
                    emptied_pair("y2")
                    emptied_pair("akv")
                    four("wp", sq(XB), sq(RR))
                    emptied_pair("wp")
                    emptied_pair("ab")
                    for hp in range(2):
                        b = psum[order.open(pe, T("rh", hp))]
                        for par in range(2):
                            ins = mm(b[HD * par:HD * par + HD, 0:P], WP[:, hp, par, 0:HD], AB[:, hp, par, P:2 * P],
                                     start=True, stop=True)
                        end(ins)
                    emptied_pair("tb")
                    for hp in range(2):
                        b = psum[order.open(pe, T("mt", hp))]
                        for par in range(2):
                            ins = mm(b[HD * par:HD * par + HD, 0:P], WP[:, hp, par, 0:HD],
                                     BC[:, hp, :, HD * par:HD * par + HD], start=True, stop=True)
                        end(ins)
                    emptied_pair("mt")
                    for s in range(2):
                        c = s if d == 0 else 1 - s
                        if s == 1:
                            emptied_pair("s0")
                        else:
                            if kind == "c":
                                pe.wait_ge(s_st0, 2 * l + d + 1)
                            elif i == 0:
                                order.wait_emptied(pe, ("si", l, d))
                            else:
                                for hp in range(2):
                                    order.wait_emptied(pe, ("s1", l, STEPS[n - 1], hp))
                        for hp in range(2):
                            b = psum[order.open(pe, T(f"s{s}", hp))]
                            mm(b[:, 0:P], BM[:, hp, c, :], ST[:, hp, ver(s), :], start=True, stop=False, skip_group_check=True)
                            for par in range(2):
                                o = b[HD * par:HD * par + HD, HD * par:HD * par + HD]
                                cols = slice(HD * par, HD * par + HD)
                                mm(o, BC[:, hp, c, cols], WP[:, hp, par, HD:P], start=False, stop=False, skip_group_check=True)
                                ins = mm(o, KC[:, hp, c, cols], V(hp, par), start=False, stop=(par == 1), skip_group_check=True)
                            end(ins)
                    emptied_pair("rh")
                    for hp in range(2):
                        b = psum[order.open(pe, T("yy", hp))]
                        for s in range(2):
                            c = s if d == 0 else 1 - s
                            mm(b[:, CH * c:CH * c + CH], ST[:, hp, ver(s), :], RH[:, hp, CH * c:CH * c + CH],
                               start=(s == 0), stop=False, skip_group_check=True)
                        for par in range(2):
                            o = b[HD * par:HD * par + HD, 0:P]
                            mm(o, WP[:, hp, par, HD:P], AB[:, hp, par, P:2 * P], start=False, stop=False, skip_group_check=True)
                            ins = mm(o, V(hp, par), AK[:, hp, par, P:2 * P], start=False, stop=(par == 1), skip_group_check=True)
                        end(ins)

                    if kind == "c":
                        emptied_pair("s1")
                        b = psum[order.open(pe, ("so", l, d))]
                        for hp in range(2):
                            ins = tr(b[:, P * hp:P * hp + P], ST[:, hp, ver(2), :], ident)
                        end(ins)

                for name in ("mu", "var"):
                    if name == "mu":
                        for hp in range(2):
                            order.wait_emptied(pe, ("yy", l, STEPS[-1], hp))
                    else:
                        pe.wait_ge(s_gsq, l + 1)
                    src = yT if name == "mu" else tmp
                    for ct in range(2):
                        for h in range(2):
                            b = psum[order.open(pe, (name, l, ct, h))]
                            end(mm(b[:, 0:HALF], blk, src[:, ct, HALF * h:HALF * (h + 1)], start=True, stop=True))
                pe.wait_ge(s_gup_in, 16 * 5 * (l + 1))
                for ct in range(2):
                    for h in range(2):
                        b = psum[order.open(pe, ("gup", l, ct, h))]
                        end(mm(b[:, 0:HALF], g_up[0:64, P * ct:P * ct + P], gdT[0:64, HALF * h:HALF * (h + 1)],
                               start=True, stop=True))
                for ct in range(2):
                    for h in range(2):
                        order.wait_emptied(pe, ("gup", l, ct, h))
                pe.wait_ge(s_conv, l + 1)
                for j in range(NT):
                    order.wait_emptied(pe, ("ot", l, j))
                order.wait_emptied(pe, ("f2c", l))
                for ct in range(2):
                    order.wait_emptied(pe, ("f2", l, ct))
                for i in range(2):
                    wait_item(pe, ("wout", l, i))
                    w = view(ring, item(("wout", l, i)), KT, 512)
                    for t in range(4):
                        for h in range(2):
                            b = psum[order.open(pe, ("out", l, 4 * i + t, h))]
                            for k in range(KT):
                                ins = mm(b[:, 0:HALF], w[:, k, P * t:P * t + P], mixT[:, k, HALF * h:HALF * (h + 1)],
                                         start=(k == 0), stop=(k == KT - 1))
                            end(ins)
                sum_squares("ss2", l, 2 * l + 2)
                pe.wait_ge(s_h, 2 * l + 2)
                if l == 1:
                    b = psum[order.open(pe, ("router", l))]
                    for j in range(NT):
                        for k in range(KT):
                            ins = mm(b[:, NE * j:NE * j + NE], hT[:, k, P * j:P * j + P], router_w[:, k, :],
                                     start=(k == 0), stop=(k == KT - 1))
                    end(ins)
                    pe.wait_ge(s_rmax, 1)
                    b = psum[order.open(pe, ("pos", l))]
                    for j in range(NT + 1):
                        for i in range(min(j + 1, NT)):
                            ins = mm(b[:, NE * j:NE * j + NE], cst("upper", P) if i == j else ones, rt_first[:, i, :],
                                     start=(i == 0), stop=(i == min(j, NT - 1)))
                    end(ins)
                    for j in range(NT):
                        for q in range(2):
                            b = psum[order.open(pe, ("ht", j, q))]
                            for k in range(4):
                                ins = tr(b[:, P * k:P * k + P], hT[:, 4 * q + k, P * j:P * j + P], ident)
                            end(ins)
                    for j in range(NT):
                        for q in range(2):
                            order.wait_emptied(pe, ("ht", j, q))
                for h in range(2):
                    order.wait_emptied(pe, ("ss2", l, h))
                if l == 0:
                    dense()
                else:
                    experts()
                    pe.wait_ge(s_moe_done, 1)
            for j in range(NT):
                for q in range(2):
                    b = psum[order.open(pe, ("y", j, q))]
                    for k in range(4):
                        ins = tr(b[:, P * k:P * k + P], xT[:, 4 * q + k, P * j:P * j + P], ident)
                    end(ins)

        pc = lambda name, i: par[:, ROW[name] + i:ROW[name] + i + 1]
        def chunk_item(n):
            p, kind, i = chunks[n]
            return (kind, 0, p, i // 2)

        def dense_chunk(n):
            p, kind, i = chunks[n]
            base = item(chunk_item(n))
            if kind == "up":
                dims, src = (2, KT, P), view(ring, base, 2, KT, 256)[:, :, :, P * (i % 2):P * (i % 2) + P]
            else:
                nf = DENSE_PARTS[p][1]
                dims, src = (nf, 256), view(ring, base, nf, 512)[:, :, 256 * (i % 2):256 * (i % 2) + 256]
            return [view(t, (n % 2) * CHUNK, *dims) for t in (w_hi, w_lo)], src

        def wait_chunk_used(eng, n):
            if n < 2:
                return
            p, kind, i = chunks[n - 2]
            order.wait_filled(eng, ("du", p, i, 1, 1) if kind == "up" else ("dn", p, i, 1, 1))

        def pair_chunk(n):
            c = n % EXP_CHUNKS
            base = ((n // 2 + len(items)) % 2) * SLOT
            if c < EXP_F:
                dims, src = (2, KT, P), view(ring, base, 2, KT, 256)[:, :, :, P * (c % 2):P * (c % 2) + P]
            else:
                dims, src = (4, 512), view(ring, base, EXP_F, 512)[:, 4 * (c % 2):4 * (c % 2) + 4, :]
            return [view(t, (n % 2) * CHUNK, *dims) for t in (w_hi, w_lo)], src

        def wait_pair_chunk_used(eng, n, it):
            back = 1 if n < 2 else 0
            n = (n - 2) % (2 * EXP_CHUNKS)
            k, c = divmod(n, EXP_CHUNKS)
            if c < EXP_F:
                order2.wait_filled(eng, ("up", k, c), it, back)
            elif (c - EXP_F) % 2 == 1:
                order2.wait_filled(eng, ("dw", k, (c - EXP_F) // 2, 1), it, back)
            elif back:
                eng.wait_ge(s_half, 4 * it + 4 - 4 + (2 * k + (c - EXP_F) // 2) + 1)
            else:
                eng.wait_ge(s_half, 4 * it + 4 + (2 * k + (c - EXP_F) // 2) + 1)

        IN_DEST = {"r": rT, "k": kT_, "v": vT, "bx": bxT, "bb": bbT, "bc": bcT, "f": fT}

        @block.scalar
        def _(act):
            chain = Chain(act, s_ca)
            ac = nc.scalar.activation

            def end(ins):
                ins.then_inc(emptied["A"], 1)

            def take(name):
                order.wait_filled(act, name)
                return psum[order.bank(name)]

            def norm(l, which):
                if which == 2:
                    order.wait_emptied(act, ("out", l, KT - 1, 1))
                elif l > 0:
                    order.wait_emptied(act, ("dn", len(DENSE_PARTS) - 1, 3, 1, 1))
                else:
                    for j in range(NT):
                        for q in range(2):
                            order.wait_emptied(act, ("x", j, q))
                for k in range(KT):
                    ins = ac(hT[:, k, :], xT[:, k, :], ACT.Square)
                ins.then_inc(s_sq, 1)
                for h in range(2):
                    b = take((f"ss{which}", l, h))
                    end(ac(rs[:, HALF * h:HALF * (h + 1)], b[:, 0:HALF], ACT.Sqrt, scale=1.0 / D, bias=cst("eps", 1)))
                nth = 2 * l + which - 1
                for k in range(KT):
                    act.wait_ge(s_hmul, KT * nth + k + 1)
                    for vec, lo, hi in SEGS:
                        ins = ac(hT[:, k, lo:hi], hT[:, k, lo:hi], ACT.Identity,
                                 bias=mod[:, 24 * (which - 1) + k, vec:vec + 1])
                ins.then_inc(s_h, 1)

            def in_evac(l, tiles):
                for name, _, _ in tiles:
                    for h in range(2):
                        key = ("in", l, name, h)
                        if order.by[order.at[key]] != "A":
                            continue
                        b = take(key)
                        cols = slice(HALF * h, HALF * (h + 1))
                        if name[0] == "wa":
                            chain.did(ac(waT[0:64, cols], b[0:64, 0:HALF], ACT.Tanh))
                            end(ac(waT[64:P, cols], b[64:P, 0:HALF], ACT.Copy))
                        elif name[0] == "gd":
                            end(ac(gdT[0:64, cols], b[0:64, 0:HALF], ACT.Sigmoid))
                        else:
                            end(ac(IN_DEST[name[0]][:, name[1], cols], b[:, 0:HALF], ACT.Copy))

            def dense_split(n):
                wait_item(act, chunk_item(n))
                wait_chunk_used(act, n)
                dst, src = dense_chunk(n)
                ac(dst[0], src, ACT.Copy).then_inc(s_hi, 1)

            act.wait_ge(s_const, 16)
            for j in range(NT):
                b = take(("x", j, 0))
                end(ac(xT[:, 0:4, P * j:P * j + P], b[:, :].rearrange("p (k t) -> p k t", k=4), ACT.Copy))
            for l in range(DEPTH):
                order.wait_emptied(act, ("params", l))
                chain.did(ac(silu_c[:, :, 0], par[:, ROW["c_ctx"]:ROW["c_ctx"] + KT], ACT.Silu))
                ac(silu_c[:, :, 1], par[:, ROW["c"]:ROW["c"] + KT], ACT.Silu).then_inc(s_silc, 1)
                norm(l, 1)
                in_evac(l, RW_TILES)
                for j in range(0, NT, 2):
                    b = take(("qkv", l, j))
                    end(ac(qkv[:, j, :], b[:, :], ACT.Copy))
                in_evac(l, CF_TILES)
                act.wait_ge(s_kkr, l + 1)
                for ct in range(2):
                    ins = ac(tmp[:, ct, :], kkT[:, ct, :], ACT.Square)
                ins.then_inc(s_kq, 1)
                order.wait_filled(act, ("in", l, CF_TILES[-1][0], 1))
                for j in range(NT):
                    order.wait_emptied(act, ("qkv", l, j))
                    ins = ac(qk_sq[:, j, :], qkv[:, j, 0:384], ACT.Square)
                ins.then_inc(s_qsq, 1)
                for j in range(NT):
                    b = take(("vt", l, j))
                    end(ac(v_tok[:, j].rearrange("p h d -> p (h d)"), b[:, 0:256], ACT.Copy))
                act.wait_ge(s_conv, l + 1)
                for kind in range(2):
                    for d in range(2):
                        for ct in range(2):
                            for h in range(2):
                                b = take(("up", l, kind, d, ct, h))
                                row = ROW["w0" if kind == 0 else "a0"] + 2 * d + ct
                                dst = (lw if kind == 0 else aT)[:, d, ct, HALF * h:HALF * (h + 1)]
                                end(ac(dst, b[:, 0:HALF], ACT.Sigmoid, bias=par[:, row:row + 1]))
                for ct in range(2):
                    for h in range(2):
                        b = take(("kks", l, ct, h))
                        end(ac(tmp[:, ct, HALF * h:HALF * (h + 1)], b[:, 0:HALF], ACT.Sqrt))
                act.wait_ge(s_qss, l + 1)
                ac(qk_ss, qk_ss, ACT.Sqrt, scale=1.0 / HD, bias=cst("eps", 1)).then_inc(s_qrt, 1)
                def modulation(i):
                    if i >= MOD_ITEMS:
                        return
                    b = take(("mod", l, i))
                    for t in range(4):
                        ins = ac(mod[:, 4 * i + t, :], b[:, 2 * t:2 * t + 2], ACT.Identity, bias=pc("mod_b", 4 * i + t))
                        if t < 3:
                            chain.did(ins)
                    end(ins)

                for j in range(NT):
                    pos = [p for p, _ in key_blocks(j)]
                    lo, hi = P * pos[0], P * (pos[-1] + 1)
                    act.wait_ge(s_max, l * NT + j + 1)
                    A = att[:, j % 2]
                    for h in range(NQ):
                        chain.did(ac(sc[:, h, lo:hi], sc[:, h, lo:hi], ACT.Exp, scale=HD ** -0.5,
                                     bias=A[:, 4 + h:5 + h], accum_out=A[:, 8 + h:9 + h]))
                    chain.settle()
                    ac(A[:, 12:16], A[:, 12:16], ACT.Exp).then_inc(s_exp, 1)
                    modulation(MOD_FIRST + 2 * j)
                    for h in (0, 2):
                        b = take(("pt", l, j, h))
                        end(ac(pT[h].rearrange("p a b -> p (a b)")[:, lo:hi], b[:, lo:hi], ACT.Copy))
                    modulation(MOD_FIRST + 2 * j + 1)
                    b = take(("ot", l, j))
                    end(ac(mixT[:, 0:2, P * j:P * j + P], b[:, 0:256].rearrange("p (t n) -> p t n", t=2), ACT.Copy))
                for j in range(0, NT, 2):
                    b = take(("f1", l, j))
                    end(ac(v1[:, j].rearrange("p a b -> p (a b)"), b[:, :], ACT.Copy))
                b = take(("f2c", l))
                end(ac(mixT[:, 6:8, 0:CTX], b[:, 0:256].rearrange("p (t n) -> p t n", t=2), ACT.Copy))
                b = take(("f2", l, 0))
                end(ac(mixT[:, 6, CTX:TOK], b[:, :], ACT.Copy))

                act.wait_ge(s_zero, 2 * l + 2)

                def decays(n):
                    gn = l * len(STEPS) + n
                    E = EX[n % 2]
                    act.wait_ge(s_sum, gn + 1)
                    chain.did(ac(E[:, :, 2, :], E[:, :, 1, :], ACT.Exp, scale=-1.0))
                    chain.settle()
                    ac(E[:, :, 0:2, :], E[:, :, 0:2, :], ACT.Exp).then_inc(s_ex, 1)

                decays(0)
                for n, step in enumerate(STEPS):
                    T = lambda name, hp: (name, l, step, hp)

                    def copies(name, dst):
                        for hp in range(2):
                            b = take(T(name, hp))
                            end(ac(dst[:, hp], b[:, 0:256].rearrange("p (a b) -> p a b", a=2), ACT.Copy))

                    for hp in range(2):
                        b = take(T("tz", hp))
                        end(ac(RR[:, hp, :, 0:HD], b[:, 0:P].rearrange("p (a b) -> p a b", a=2), ACT.Copy))
                    for hp in range(2):
                        b = take(T("tb", hp))
                        for c in range(2):
                            rows = slice(CH * c, CH * c + CH)
                            chain.did(ac(BC[rows, hp, c, :], b[rows, 0:P], ACT.Copy, scale=-1.0))
                            ins = ac(KC[rows, hp, c, :], b[rows, P:2 * P], ACT.Copy)
                            if c == 0:
                                chain.did(ins)
                            else:
                                end(ins)
                    copies("n2", N2)
                    copies("d2", D2)
                    copies("n4", ND)
                    copies("d4", DD)
                    if n + 1 < len(STEPS):
                        decays(n + 1)
                    copies("d8", D2)
                    copies("x8t", N2)
                    copies("g1", ND)
                    copies("y1t", N2)
                    copies("g2", ND)
                    copies("wp", WP)

                act.wait_ge(s_gn, l + 1)
                act.wait_ge(s_state_out, 16 * 8 * (l + 1))
                for ct in range(2):
                    ins = ac(tmp[:, ct, :], yT[:, ct, :], ACT.Square)
                ins.then_inc(s_gsq, 1)
                for ct in range(2):
                    for h in range(2):
                        b = take(("var", l, ct, h))
                        end(ac(tmp[:, ct, HALF * h:HALF * (h + 1)], b[:, 0:HALF], ACT.Sqrt, scale=1.0 / HD,
                               bias=cst("eps", 1, 1)))
                norm(l, 2)
                if l == 0:
                    for k in range(KT):
                        if k == 0:
                            act.wait_ge(s_h, 2)
                        ac(hc[0][:, k, :], hT[:, k, :], ACT.Copy).then_inc(s_hhi, 1)
                    dense_split(0)
                    for n, (p, kind, i) in enumerate(chunks):
                        if n + 1 < len(chunks):
                            dense_split(n + 1)
                        if kind == "up":
                            u = DENSE_PARTS[p][0] + i
                            if u >= 2:
                                act.wait_ge(s_glo, u - 1)
                            for h in range(2):
                                b = take(("du", p, i, 0, h))
                                end(ac(sil[:, u % 2, HALF * h:HALF * (h + 1)], b[:, 0:HALF], ACT.Silu))
                            if i == 0 and p > 0:
                                order.wait_filled(act, ("dn", p - 1, 3, 1, 1))
                            order.wait_emptied(act, ("du", p, i, 1, 1))
                            ac(dg[0][:, i, :], sil[:, u % 2, :], ACT.Copy).then_inc(s_ghi, 1)
                else:
                    act.wait_ge(s_rmax, 1)
                    ac(rt_l, rt_l, ACT.Exp).then_inc(s_rexp, 1)
                    for j in range(NT):
                        for q in range(2):
                            order.wait_filled(act, ("ht", j, q))
                            b = psum[order.bank(("ht", j, q))]
                            ac(ht[0][:, j, 512 * q:512 * (q + 1)], b[:, :], ACT.Copy).then_inc(s_hhi, 1)
                    o = order2
                    act.sem_inc(s_hi2, 2 * EXP_CHUNKS)
                    act.wait_ge(s_rounds, 1)
                    rounds = act.value_load(rounds_t[0:1, 0:1], min_val=1, max_val=MAX_ROUNDS)
                    with act.Fori(0, rounds) as r:
                        with act.Fori(0, NE // 2) as pair:
                            it = r * (NE // 2) + pair
                            take2 = lambda name: (o.wait_filled(act, name, it), psum[o.bank(name)])[1]

                            def split(n):
                                act.wait_ge(s_ring2[n // 2 % 2], it * 32 * (PAIR_ITEMS // 2) + 32 * (n // 4 + 1))
                                wait_pair_chunk_used(act, n, it)
                                dst, src = pair_chunk(n)
                                ac(dst[0], src, ACT.Copy).then_inc(s_hi2, 1)

                            for k in range(2):
                                n0 = EXP_CHUNKS * k
                                split(n0)
                                for b4 in range(4):
                                    b = take2(("ga", k, b4))
                                    ac(xg[0][:, 2 * b4:2 * b4 + 2, :], b[:, :].rearrange("p (t n) -> p t n", t=2),
                                       ACT.Copy).then_inc(s_xhi, 1)
                                for c in range(EXP_CHUNKS):
                                    if c + 1 < EXP_CHUNKS:
                                        split(n0 + c + 1)
                                    if c < EXP_F:
                                        u = (2 * it + k) * EXP_F + c
                                        b = take2(("up", k, c))
                                        if c >= 2:
                                            act.wait_ge(s_glo2, u - 1)
                                        ac(e_sil[:, c % 2, :], b[:, 0:CAP], ACT.Silu).then_inc(s_sil2, 1)
                                        o.wait_emptied(act, ("up", k, c), it)
                                        ac(eg[0][:, c, :], e_sil[:, c % 2, :], ACT.Copy).then_inc(s_ghi2, 1)
                                    elif (c - EXP_F) % 2 == 1:
                                        i = (c - EXP_F) // 2
                                        act.wait_ge(s_gs, 2 * it + k + 1)
                                        for q in range(2):
                                            b = take2(("dw", k, i, q))
                                            ac(yg[0][:, q, 512 * i:512 * (i + 1)], b[:, :], ACT.Copy,
                                               scale=gslot[:, k, q:q + 1]).then_inc(s_yhi, 1)
            for j in range(NT):
                b = take(("y", j, 0))
                end(ac(x_tok[:, j, 0:512], b[:, :], ACT.Copy))

        @block.vector
        def _(ve):
            chain = Chain(ve, s_cv)
            v = nc.vector

            def end(ins):
                ins.then_inc(emptied["V"], 1)

            def take(name):
                order.wait_filled(ve, name)
                return psum[order.bank(name)]

            def norm(l, which):
                t = 24 * (which - 1) + 8
                w = par[:, ROW[f"norm{which}"]:ROW[f"norm{which}"] + KT]
                if which == 1:
                    order.wait_emptied(ve, ("mod", l))
                chain.did(v.scalar_tensor_tensor(out=amul, in0=mod[:, t:t + KT, :], scalar=1.0,
                                                 in1=w[:, :, None].broadcast_to([P, KT, 2]), op0=ALU.add, op1=ALU.mult))
                for h in range(2):
                    order.wait_emptied(ve, (f"ss{which}", l, h))
                chain.did(v.reciprocal(rs, rs))
                chain.settle()
                for k in range(KT):
                    for vec, lo, hi in SEGS:
                        ins = v.scalar_tensor_tensor(out=hT[:, k, lo:hi], in0=xT[:, k, lo:hi], scalar=amul[:, k, vec:vec + 1],
                                                     in1=rs[:, lo:hi], op0=ALU.mult, op1=ALU.mult)
                        if vec == 0:
                            chain.did(ins)
                    ins.then_inc(s_hmul, 1)

            def in_evac(l, tiles):
                for name, _, _ in tiles:
                    for h in range(2):
                        key = ("in", l, name, h)
                        if order.by[order.at[key]] != "V":
                            continue
                        b = take(key)
                        end(v.tensor_copy(IN_DEST[name[0]][:, name[1], HALF * h:HALF * (h + 1)], b[:, 0:HALF]))

            def residual(b, h, dt, gate, drain=False):
                parts = ((0, 0, CTX), (1, CTX, HALF)) if h == 0 else ((1, HALF, TOK),)
                for vec, lo, hi in parts:
                    off = HALF * h
                    ins = v.scalar_tensor_tensor(out=xT[:, dt, lo:hi], in0=b[:, lo - off:hi - off],
                                                 scalar=mod[:, gate + dt, vec:vec + 1], in1=xT[:, dt, lo:hi],
                                                 op0=ALU.mult, op1=ALU.add)
                    if hi < TOK and vec == 0 and not drain:
                        chain.did(ins)
                return ins

            def dense_split(n):
                ve.wait_ge(s_hi, n + 1)
                dst, src = dense_chunk(n)
                v.tensor_tensor(dst[1], src, f32(dst[0]), ALU.subtract).then_inc(s_lo, 1)

            def experts():
                o = order2
                ve.sem_inc(o.emptied["V"], len(o.by))
                ve.sem_inc(s_lo2, 2 * EXP_CHUNKS)
                rounds = ve.value_load(rounds_t[0:1, 0:1], min_val=1, max_val=MAX_ROUNDS)
                with ve.Fori(0, rounds) as r:
                    with ve.Fori(0, NE // 2) as pair:
                        it = r * (NE // 2) + pair

                        def end2(ins):
                            ins.then_inc(o.emptied["V"], 1)

                        def take2(name):
                            o.wait_filled(ve, name, it)
                            return psum[o.bank(name)]

                        def settle():
                            ve.drain()

                        def split(n):
                            ve.wait_ge(s_hi2, (it + 1) * 2 * EXP_CHUNKS + n + 1)
                            dst, src = pair_chunk(n)
                            v.tensor_tensor(dst[1], src, f32(dst[0]), ALU.subtract).then_inc(s_lo2, 1)

                        def select(k):
                            e = 2 * pair + k
                            settle()
                            if k == 1:
                                o.wait_filled(ve, ("ga", 0, 3), it)
                            v.tensor_copy(cur_pos[:, k, :], posm[:, :, bass.ds(e, 1)].rearrange("p j e -> p (j e)"))
                            v.tensor_copy(cur_gate[:, k, :], gates[:, :, bass.ds(e, 1)].rearrange("p j e -> p (j e)"))
                            settle()
                            for j in range(NT):
                                ins = v.tensor_scalar(sel[:, j, :], cst("slots", CAP), cur_pos[:, k, j:j + 1], None, ALU.is_equal)
                            ins.then_inc(s_sel, 1)

                        def spread(k):
                            for b2 in range(2):
                                b = take2(("bc", k, b2))
                                lo, n = ((0, 384), (384, 256))[b2]
                                for q in range(2):
                                    ins = v.tensor_scalar(selT[:, q, lo:lo + n], b[:, 0:n], cst("slot", 1, q), None, ALU.is_equal)
                                end2(ins)
                            settle()
                            for b2 in range(2):
                                b = take2(("bc", k, 2 + b2))
                                lo, n = ((0, 384), (384, 256))[b2]
                                for q in range(2):
                                    v.tensor_tensor(junk[:, q, 0:n], b[:, 0:n], f32(selT[:, q, lo:lo + n]), ALU.mult)
                                settle()
                                for q in range(2):
                                    ins = v.tensor_reduce(out=gs_part[:, k, q, b2:b2 + 1], in_=junk[:, q, 0:n], axis=AXX, op=ALU.add)
                                end2(ins)
                                settle()
                            v.tensor_tensor(gslot[:, k, :], gs_part[:, k, :, 0], gs_part[:, k, :, 1], ALU.add).then_inc(s_gs, 1)
                            ve.wait_ge(s_gs, 2 * it + k + 1)

                        def gathered(k):
                            for b4 in range(4):
                                b = take2(("ga", k, b4))
                                ve.wait_ge(s_xhi, 4 * (2 * it + k) + b4 + 1)
                                end2(v.tensor_tensor(xg[1][:, 2 * b4:2 * b4 + 2, :], b[:, :].rearrange("p (t n) -> p t n", t=2),
                                                     f32(xg[0][:, 2 * b4:2 * b4 + 2, :]), ALU.subtract))

                        def scattered(k):
                            for dt in range(KT):
                                for h in range(2):
                                    end2(residual(take2(("sc", k, dt, h)), h, dt, 40, drain=True))

                        select(0)
                        for k in range(2):
                            n0 = EXP_CHUNKS * k
                            if k == 0:
                                spread(0)
                                split(n0)
                                gathered(0)
                            for c in range(EXP_CHUNKS):
                                if c + 1 < EXP_CHUNKS:
                                    split(n0 + c + 1)
                                if c < EXP_F:
                                    u = (2 * it + k) * EXP_F + c
                                    b = take2(("up", k, c))
                                    ve.wait_ge(s_sil2, u + 1)
                                    end2(v.tensor_tensor(e_sil[:, c % 2, :], b[:, CAP:2 * CAP], e_sil[:, c % 2, :], ALU.mult))
                                    ve.wait_ge(s_ghi2, u + 1)
                                    v.tensor_tensor(eg[1][:, c, :], e_sil[:, c % 2, :], f32(eg[0][:, c, :]),
                                                    ALU.subtract).then_inc(s_glo2, 1)
                                elif (c - EXP_F) % 2 == 1:
                                    i = (c - EXP_F) // 2
                                    cols = slice(512 * i, 512 * (i + 1))
                                    for q in range(2):
                                        b = take2(("dw", k, i, q))
                                        ve.wait_ge(s_yhi, 4 * (2 * it + k) + 2 * i + q + 1)
                                        end2(v.scalar_tensor_tensor(out=yg[1][:, q, cols], in0=b[:, :], scalar=gslot[:, k, q:q + 1],
                                                                    in1=f32(yg[0][:, q, cols]), op0=ALU.mult, op1=ALU.subtract))
                                if k == 0 and c == EXP_F:
                                    select(1)
                            if k == 0:
                                split(EXP_CHUNKS)
                                gathered(1)
                            scattered(k)
                            if k == 0:
                                spread(1)
                    ve.drain()
                    v.tensor_scalar(posm, posm, -float(CAP), None, ALU.add)
                    ve.drain()
                ve.sem_inc(s_moe_done, 1)

            ve.wait_ge(s_const, 16)
            for j in range(NT):
                b = take(("x", j, 1))
                end(v.tensor_copy(xT[:, 4:8, P * j:P * j + P], b[:, :].rearrange("p (k t) -> p k t", k=4)))
            for l in range(DEPTH):
                b = take(("params", l))
                end(v.tensor_copy(par, b[:, 0:NROWS]))
                order.wait_emptied(ve, ("params", l))
                b = take(("mod", l))
                m = 4 * MOD_FIRST
                end(v.tensor_tensor(mod[:, 0:m, :], b[:, 0:2 * m].rearrange("p (t v) -> p t v", v=2),
                                    par[:, 0:m][:, :, None].broadcast_to([P, m, 2]), ALU.add))
                norm(l, 1)
                in_evac(l, RW_TILES)
                for ct in range(2):
                    order.wait_emptied(ve, ("in", l, ("k", ct), 0))
                    order.wait_emptied(ve, ("in", l, ("k", ct), 1))
                    chain.did(v.tensor_scalar(omka[:, ct:ct + 1], pc("k_a", ct), -1.0, 1.0, ALU.mult, ALU.add))
                    ins = v.tensor_scalar(kkT[:, ct, :], kT_[:, ct, :], pc("k_k", ct), None, ALU.mult)
                ins.then_inc(s_kkr, 1)
                for j in range(1, NT, 2):
                    b = take(("qkv", l, j))
                    end(v.tensor_copy(qkv[:, j, :], b[:, :]))
                in_evac(l, CF_TILES)
                ve.wait_ge(s_cu, l + 1)
                for h in range(2):
                    for ct in range(2):
                        order.wait_emptied(ve, ("in", l, ("bb", ct), h))
                for ct in range(2):
                    for at0, (_, lo, hi) in ((0, SEGS[0]), (2, SEGS[1])):
                        n = hi - lo
                        u = lambda s: conv_u[:, ct, at0 + lo + s:at0 + hi + s]
                        o = mixT[:, 2 + ct, lo:hi]
                        chain.did(v.tensor_scalar(o, u(0), pc("conv", ct), None, ALU.mult))
                        for s in (1, 2):
                            chain.settle()
                            chain.did(v.scalar_tensor_tensor(out=o, in0=u(s), scalar=pc("conv", 2 * s + ct), in1=o,
                                                             op0=ALU.mult, op1=ALU.add))
                        chain.settle()
                        ins = v.tensor_tensor(o, o, bbT[:, ct, lo:hi], ALU.mult)
                        if (ct, lo) != (1, CTX):
                            chain.did(ins)
                        else:
                            ins.then_inc(s_conv, 1)
                ve.wait_ge(s_qsq, l + 1)
                v.tensor_reduce(out=qk_ss, in_=qk_sq.rearrange("p j (h d) -> p (j h) d", d=HD), axis=AXX,
                                op=ALU.add).then_inc(s_qss, 1)
                for ct in range(2):
                    for h in range(2):
                        order.wait_emptied(ve, ("kks", l, ct, h))
                chain.did(v.tensor_scalar(tmp, tmp, 1e-12, None, ALU.max))
                chain.settle()
                chain.did(v.reciprocal(tmp, tmp))
                chain.settle()
                v.scalar_tensor_tensor(out=kkT, in0=kkT, scalar=-1.0, in1=tmp, op0=ALU.mult, op1=ALU.mult).then_inc(s_nkk, 1)
                ve.wait_ge(s_nkk, l + 1)
                for ct in range(2):
                    for h in range(2):
                        order.wait_emptied(ve, ("in", l, ("r", ct), h))
                    ins = v.scalar_tensor_tensor(out=tmp[:, ct, :], in0=rT[:, ct, :], scalar=pc("r_k", ct), in1=kT_[:, ct, :],
                                                 op0=ALU.mult, op1=ALU.mult)
                    if ct == 0:
                        chain.did(ins)
                ins.then_inc(s_rk, 1)
                for ct in range(2):
                    for h in range(2):
                        b = take(("bonus", l, ct, h))
                        for c2 in range(2):
                            order.wait_emptied(ve, ("in", l, ("v", ct), c2))
                        cols = slice(HALF * h, HALF * (h + 1))
                        end(v.tensor_tensor(vT[:, ct, cols], b[:, 0:HALF], vT[:, ct, cols], ALU.mult))
                b = take(("ckt", l))
                end(v.tensor_copy(ckT, b[:, 0:P]))
                ve.wait_ge(s_qrt, l + 1)
                ve.wait_ge(s_gup_in, 16 * 5 * (l + 1))
                chain.did(v.reciprocal(qk_ss, qk_ss))
                for j in range(NT):
                    q_in = qkv[:, j, 0:384].rearrange("p (h d) -> p h d", d=HD)
                    t = qk_t[:, j % 2]
                    chain.settle()
                    if j == 0:
                        for jj in range(NT):
                            order.wait_emptied(ve, ("qkv", l, jj))
                    chain.did(v.tensor_tensor(t, q_in, qk_ss[:, 6 * j:6 * j + 6][:, :, None].broadcast_to([P, 6, HD]), ALU.mult))
                    chain.settle()
                    chain.did(v.tensor_tensor(
                        qkv[:, j, 0:256].rearrange("p (g k d) -> p k g d", g=2, k=2),
                        t[:, 0:4, :].rearrange("p (k g) d -> p k g d", k=2),
                        qnw[:, None, None, :].broadcast_to([P, 2, 2, HD]), ALU.mult))
                    v.tensor_tensor(qkv[:, j, 256:384].rearrange("p (k d) -> p k d", k=2), t[:, 4:6, :],
                                    knw[:, None, :].broadcast_to([P, 2, HD]), ALU.mult).then_inc(s_qk, 1)
                for j in range(NT):
                    b = take(("qt", l, j))
                    chain.did(v.tensor_copy(qT[:, :, P * j:P * j + P], b[:, 0:256].rearrange("p (t n) -> p t n", t=2)))
                    end(v.tensor_copy(kT[:, P * j:P * j + P], b[:, 256:384]))
                for j in range(NT):
                    pos = [p for p, _ in key_blocks(j)]
                    lo, hi = P * pos[0], P * (pos[-1] + 1)
                    A = att[:, j % 2]
                    for h in range(NQ):
                        b = take(("qk", l, j, h))
                        if j == 0:
                            end(v.tensor_copy(sc[:, h, lo:hi], b[:, lo:hi]))
                        else:
                            end(v.tensor_tensor(sc[:, h, lo:hi], b[:, lo:hi], cst("band", 512)[:, lo:hi], ALU.add))
                    order.wait_emptied(ve, ("qk", l, j, NQ - 1))
                    chain.did(v.tensor_reduce(out=A[:, 0:4], in_=sc[:, :, lo:hi], axis=AXX, op=ALU.max))
                    chain.settle()
                    chain.did(v.scalar_tensor_tensor(out=A[:, 0:4], in0=A[:, 0:4], scalar=HD ** -0.5, in1=sink,
                                                     op0=ALU.mult, op1=ALU.max))
                    chain.settle()
                    chain.did(v.tensor_scalar(A[:, 4:8], A[:, 0:4], -1.0, None, ALU.mult))
                    v.tensor_tensor(A[:, 12:16], sink, A[:, 0:4], ALU.subtract).then_inc(s_max, 1)
                    for h in (1, 3):
                        b = take(("pt", l, j, h))
                        end(v.tensor_copy(pT[h].rearrange("p a b -> p (a b)")[:, lo:hi], b[:, lo:hi]))
                    ve.wait_ge(s_exp, l * NT + j + 1)
                    chain.did(v.tensor_tensor(A[:, 16:20], A[:, 8:12], A[:, 12:16], ALU.add))
                    chain.settle()
                    chain.did(v.reciprocal(A[:, 16:20], A[:, 16:20]))
                    chain.settle()
                    b = take(("pv", l, j))
                    end(v.tensor_tensor(o_tok, b[:, 0:256].rearrange("p (h d) -> p h d", h=NQ),
                                        A[:, 16:20][:, :, None].broadcast_to([P, NQ, HD]), ALU.mult))
                for j in range(1, NT, 2):
                    b = take(("f1", l, j))
                    end(v.tensor_copy(v1[:, j].rearrange("p a b -> p (a b)"), b[:, :]))
                b = take(("f2", l, 1))
                end(v.tensor_copy(mixT[:, 7, CTX:TOK], b[:, :]))

                ve.wait_ge(s_zero, 2 * l + 2)

                def sums(n):
                    _, _, d = STEPS[n]
                    j = step_tile(STEPS[n])
                    E = EX[n % 2]
                    x = lw[:, d, :, P * j:P * j + P]
                    if n >= 2:
                        for hp in range(2):
                            order.wait_emptied(ve, ("rh", l, STEPS[n - 2], hp))
                    for hp in range(2):
                        chain.did(v.tensor_tensor_scan(out=E[:, hp, 1, :], data0=cst("scan", P), data1=x[:, hp, :],
                                                       initial=0.0, op0=ALU.mult, op1=ALU.add))
                    chain.settle()
                    if d == 0:
                        chain.did(v.tensor_tensor(E[:, :, 0, :], E[:, :, 1, :], x, ALU.subtract))
                        chain.settle()
                    else:
                        for c in range(2):
                            tot = E[:, :, 1, CH * c + CH - 1:CH * c + CH].broadcast_to([P, 2, CH])
                            chain.did(v.tensor_tensor(E[:, :, 0, CH * c:CH * c + CH], tot, E[:, :, 1, CH * c:CH * c + CH],
                                                      ALU.subtract))
                        chain.settle()
                        chain.did(v.tensor_tensor(E[:, :, 1, :], E[:, :, 0, :], x, ALU.add))
                        chain.settle()
                    v.tensor_scalar(E[:, :, 0:2, :], E[:, :, 0:2, :], LOG_DECAY, None, ALU.mult).then_inc(s_sum, 1)

                sums(0)
                for n, step in enumerate(STEPS):
                    kind, i, d = step
                    j = step_tile(step)
                    gn = l * len(STEPS) + n
                    T = lambda name, hp: (name, l, step, hp)
                    E = EX[n % 2]
                    v0 = 2 * i if kind == "s" else 0
                    if (kind, i) == ("s", 0):
                        b = take(("si", l, d))
                        end(v.tensor_copy(ST[:, :, 0, :], b[:, 0:256].rearrange("p (a b) -> p a b", a=2)))
                    elif kind == "c":
                        if d == 1:
                            order.wait_emptied(ve, ("so", l, 0))
                        v.memset(ST[:, :, 0, :], 0.0).then_inc(s_st0, 1)
                    pair = lambda b: b[:, 0:256].rearrange("p (a b) -> p a b", a=2)
                    for hp in range(2):
                        b = take(T("ab", hp))
                        end(v.scalar_tensor_tensor(out=AB[:, hp], in0=b[:, :].rearrange("p (a b) -> p a b", a=2), scalar=-1.0,
                                                   in1=cst("mzr", 256, 256 * d)[:, None, :].broadcast_to([P, 2, 256]),
                                                   op0=ALU.mult, op1=ALU.mult))
                    for hp in range(2):
                        b = take(T("ak", hp))
                        end(v.tensor_tensor(AK[:, hp], b[:, :].rearrange("p (a b) -> p a b", a=2),
                                            cst("mzr", 256, 256 * d)[:, None, :].broadcast_to([P, 2, 256]), ALU.mult))
                    for hp in range(2):
                        b = take(T("dd", hp))
                        end(v.scalar_tensor_tensor(out=DD[:, hp], in0=pair(b), scalar=-1.0,
                                                   in1=cst("m16", P, P * (1 - d))[:, None, :].broadcast_to([P, 2, P]),
                                                   op0=ALU.mult, op1=ALU.mult))
                    for hp in range(2):
                        b = take(T("akv", hp))
                        end(v.tensor_copy(RR[:, hp, :, HD:P], b[:, 0:P].rearrange("p (a b) -> p a b", a=2)))

                    def plus(name, dst, src):
                        for hp in range(2):
                            b = take(T(name, hp))
                            end(v.tensor_tensor(dst[:, hp], pair(b), src[:, hp], ALU.add))

                    def done(name):
                        for hp in range(2):
                            order.wait_emptied(ve, T(name, hp))

                    plus("x2", XB, XA)
                    if n + 1 < len(STEPS):
                        sums(n + 1)
                    done("x2")
                    plus("x4", XA, XB)
                    done("x4")
                    plus("x8", XB, XA)
                    done("x8")
                    plus("y1", XA, XB)
                    done("y1")
                    plus("y2", XB, XA)
                    for hp in range(2):
                        b = take(T("rh", hp))
                        end(v.tensor_tensor(RH[:, hp], b[:, 0:P], E[:, hp, 1, :], ALU.add))
                    for hp in range(2):
                        b = take(T("mt", hp))
                        for par_ in range(2):
                            r = slice(HD * par_, HD * par_ + HD)
                            ins = v.tensor_tensor(BM[r, hp, :, r], b[r, 0:P].rearrange("p (c k) -> p c k", c=2),
                                                  ident[r, r][:, None, :].broadcast_to([HD, 2, HD]), ALU.add)
                            if par_ == 0:
                                chain.did(ins)
                        end(ins)
                    for s in range(2):
                        c = s if d == 0 else 1 - s
                        for hp in range(2):
                            b = take(T(f"s{s}", hp))
                            end(v.tensor_scalar(ST[:, hp, (v0 + s + 1) % 3, :], b[:, 0:P], LC[:, n % 2, hp, c:c + 1], None,
                                                ALU.mult))
                    for hp in range(2):
                        b = take(T("yy", hp))
                        o = yT[:, hp, P * j:P * j + P]
                        if d == 0:
                            end(v.tensor_copy(o, b[:, 0:P]))
                        else:
                            end(v.tensor_tensor(o, b[:, 0:P], o, ALU.add))
                    if kind == "c":
                        b = take(("so", l, d))
                        end(v.tensor_copy(s_fin[:, d], pair(b)))

                order.wait_emptied(ve, ("yy", l, STEPS[-1], 1))
                for ct in range(2):
                    for h in range(2):
                        b = take(("mu", l, ct, h))
                        cols = slice(HALF * h, HALF * (h + 1))
                        end(v.scalar_tensor_tensor(out=yT[:, ct, cols], in0=b[:, 0:HALF], scalar=-1.0 / HD, in1=yT[:, ct, cols],
                                                   op0=ALU.mult, op1=ALU.add))
                order.wait_emptied(ve, ("mu", l, 1, 1))
                ve.sem_inc(s_gn, 1)
                for ct in range(2):
                    for h in range(2):
                        order.wait_emptied(ve, ("var", l, ct, h))
                chain.did(v.reciprocal(tmp, tmp))
                chain.settle()
                chain.did(v.tensor_tensor(yT, yT, tmp, ALU.mult))
                for ct in range(2):
                    chain.settle()
                    chain.did(v.tensor_scalar(yT[:, ct, :], yT[:, ct, :], pc("ln_w", ct), pc("ln_b", ct), ALU.mult, ALU.add))
                chain.settle()
                chain.did(v.tensor_tensor(yT, yT, vT, ALU.add))
                chain.settle()
                for ct in range(2):
                    for h in range(2):
                        b = take(("gup", l, ct, h))
                        cols = slice(HALF * h, HALF * (h + 1))
                        end(v.tensor_tensor(yT[:, ct, cols], b[:, 0:HALF], yT[:, ct, cols], ALU.mult))
                for dt in range(KT):
                    for h in range(2):
                        end(residual(take(("out", l, dt, h)), h, dt, 16))
                norm(l, 2)
                if l == 1:
                    three = lambda x: x[:, :, None].broadcast_to([P, NT, NE])
                    b = take(("router", l))
                    m = view(par_t, at[0] - 96, 3, NT)
                    end(v.tensor_copy(rt_t, b[:, 0:NT * NE].rearrange("p (j e) -> p j e", e=NE)))
                    order.wait_emptied(ve, ("router", l))
                    rank = cst("rank", NE)[:, None, :].broadcast_to([P, NT, NE])

                    def pick(dst, mx):
                        chain.did(v.tensor_reduce(out=mx, in_=rt_t, axis=AXX, op=ALU.max))
                        chain.settle()
                        chain.did(v.tensor_tensor(rt_key, rt_t, three(mx), ALU.is_equal))
                        chain.settle()
                        chain.did(v.tensor_tensor(rt_key, rt_key, rank, ALU.mult))
                        chain.settle()
                        chain.did(v.tensor_reduce(out=m[:, 2], in_=rt_key, axis=AXX, op=ALU.max))
                        chain.settle()
                        chain.did(v.tensor_tensor(dst, rt_key, three(m[:, 2]), ALU.is_equal))
                        chain.settle()

                    pick(rt_first, m[:, 0])
                    chain.did(v.tensor_tensor(rt_l, rt_t, three(m[:, 0]), ALU.subtract))
                    chain.did(v.scalar_tensor_tensor(out=rt_t, in0=rt_first, scalar=-3e38, in1=rt_t, op0=ALU.mult, op1=ALU.add))
                    chain.settle()
                    pick(rt_second, m[:, 1])
                    v.tensor_tensor(rt_first, rt_first, rt_second, ALU.add).then_inc(s_rmax, 1)
                    ve.wait_ge(s_rmax, 1)
                    ve.wait_ge(s_rexp, 1)
                    chain.did(v.tensor_tensor(gates, rt_l, rt_first, ALU.mult))
                    chain.settle()
                    chain.did(v.tensor_reduce(out=m[:, 0], in_=gates, axis=AXX, op=ALU.add))
                    chain.settle()
                    chain.did(v.reciprocal(m[:, 0], m[:, 0]))
                    chain.settle()
                    chain.did(v.tensor_tensor(gates, gates, three(m[:, 0]), ALU.mult))
                    b = take(("pos", l))
                    chain.did(v.scalar_tensor_tensor(out=posm, in0=b[:, 0:NT * NE].rearrange("p (j e) -> p j e", e=NE),
                                                     scalar=1.0, in1=rt_first, op0=ALU.add, op1=ALU.mult))
                    end(v.tensor_reduce(out=rt_m[:, 0:1], in_=b[:, NT * NE:(NT + 1) * NE], axis=AXX, op=ALU.max))
                    order.wait_emptied(ve, ("pos", l))
                    chain.did(v.tensor_scalar(posm, posm, -1.0, None, ALU.add))
                    for i in range(1, MAX_ROUNDS):
                        chain.did(v.tensor_scalar(rt_m[:, i:i + 1], rt_m[:, 0:1], float(CAP * i), 1.0 if i == 1 else 0.0,
                                                  ALU.is_gt, ALU.add))
                    for i in range(2, MAX_ROUNDS):
                        chain.settle()
                        chain.did(v.tensor_tensor(rt_m[:, 1:2], rt_m[:, 1:2], rt_m[:, i:i + 1], ALU.add))
                    chain.settle()
                    v.tensor_copy(rounds_t[:, 0:1], rt_m[:, 1:2]).then_inc(s_rounds, 1)
                    for j in range(NT):
                        for q in range(2):
                            b = take(("ht", j, q))
                            cols = slice(512 * q, 512 * (q + 1))
                            ve.wait_ge(s_hhi, KT + 2 * j + q + 1)
                            end(v.tensor_tensor(ht[1][:, j, cols], b[:, :], f32(ht[0][:, j, cols]), ALU.subtract))
                    experts()
                else:
                    for k in range(KT):
                        ve.wait_ge(s_hhi, k + 1)
                        v.tensor_tensor(hc[1][:, k, :], hT[:, k, :], f32(hc[0][:, k, :]), ALU.subtract).then_inc(s_hlo, 1)
                    dense_split(0)
                    for n, (p, kind, i) in enumerate(chunks):
                        if n + 1 < len(chunks):
                            dense_split(n + 1)
                        if kind == "up":
                            u = DENSE_PARTS[p][0] + i
                            for h in range(2):
                                cols = slice(HALF * h, HALF * (h + 1))
                                order.wait_emptied(ve, ("du", p, i, 0, h))
                                b = take(("du", p, i, 1, h))
                                end(v.tensor_tensor(sil[:, u % 2, cols], b[:, 0:HALF], sil[:, u % 2, cols], ALU.mult))
                            ve.wait_ge(s_ghi, u + 1)
                            v.tensor_tensor(dg[1][:, i, :], sil[:, u % 2, :], f32(dg[0][:, i, :]), ALU.subtract).then_inc(s_glo, 1)
                        else:
                            for t in range(2):
                                for h in range(2):
                                    end(residual(take(("dn", p, i, t, h)), h, 2 * i + t, 40))
            for j in range(NT):
                b = take(("y", j, 1))
                end(v.tensor_copy(x_tok[:, j, 512:1024], b[:, :]))

        @block.gpsimd
        def _(pool):
            chain = Chain(pool, s_cp)
            g = nc.gpsimd
            pool.wait_ge(s_const, 16)
            for l in range(DEPTH):
                if l > 0:
                    order.wait_emptied(pool, ("dn", len(DENSE_PARTS) - 1, 3, 1, 1))
                g.memset(rank_up, 0.0).then_inc(s_zero, 1)
                for name in ("bx", "bc"):
                    for ct in range(2):
                        for h in range(2):
                            order.wait_emptied(pool, ("in", l, (name, ct), h))
                chain.did(g.memset(conv_u, 0.0))
                chain.settle()
                chain.did(g.tensor_tensor(conv_u[:, :, 1:1 + CTX], bcT[:, :, 0:CTX], bxT[:, :, 0:CTX], ALU.mult))
                g.tensor_tensor(conv_u[:, :, 3 + CTX:3 + TOK], bcT[:, :, CTX:TOK], bxT[:, :, CTX:TOK], ALU.mult).then_inc(s_cu, 1)
                pool.wait_ge(s_qk, l * NT + 1)
                g.dma_start(new_k[0, l].rearrange("t h d -> t (h d)"), qkv[:, 0, 256:384]).then_inc(s_kv_out, 16)
                g.dma_start(new_v[0, l].rearrange("t h d -> t (h d)"), qkv[:, 0, 384:512]).then_inc(s_kv_out, 16)
                for j in range(1, NT):
                    pool.wait_ge(s_qk, l * NT + j + 1)
                    x = qkv[:, j, 0:384].rearrange("p (h s d) -> p h s d", s=4, d=16)
                    x1, x2 = x[:, :, 0::2, :], x[:, :, 1::2, :]
                    tab = lambda name: cst(name, 32, 32 * (j - 1)).rearrange("p (s d) -> p s d", s=2)[:, None, :, :] \
                        .broadcast_to([P, 6, 2, 16])
                    r = [rope[:, i] for i in range(4)]
                    chain.settle()
                    for t, xx, name in ((0, x1, "cos"), (1, x2, "sin"), (2, x2, "cos"), (3, x1, "sin")):
                        chain.did(g.tensor_tensor(r[t], xx, tab(name), ALU.mult))
                    chain.settle()
                    chain.did(g.tensor_tensor(x1, r[0], r[1], ALU.subtract))
                    g.tensor_tensor(x2, r[2], r[3], ALU.add).then_inc(s_rope, 1)
                    pool.wait_ge(s_rope, l * (NT - 1) + j)
                order.wait_filled(pool, ("f2", l, 1))
                pool.wait_ge(s_kv_out, 32 * (l + 1))
                for buf in (BP, KP, BM, BC, KC, s0_in):
                    chain.did(g.memset(buf, 0.0))
                chain.settle()
                pool.sem_inc(s_zero, 1)
                for d in range(2):
                    for h in range(4):
                        r = slice(HD * (h % 2), HD * (h % 2) + HD)
                        g.dma_start(s0_in[r, d, h // 2, r], a["state_wkv"][0, l, d, h]).then_inc(s_state, 16)
                pool.wait_ge(s_nkk, l + 1)
                for n, step in enumerate(STEPS):
                    kind, i, d = step
                    j = step_tile(step)
                    gn = l * len(STEPS) + n
                    cols = slice(P * j, P * j + P)
                    E = EX[n % 2]
                    pool.wait_ge(s_ex, gn + 1)
                    if n > 0:
                        order.wait_filled(pool, ("tb", l, STEPS[n - 1], 1))
                        if n > 1:
                            order.wait_emptied(pool, ("s1", l, STEPS[n - 2], 1))
                    e0 = CH - 1 if d == 0 else 0
                    chain.did(g.tensor_copy(LC[:, n % 2], E[:, :, 1, e0::CH]))
                    chain.did(g.tensor_tensor(BT, kkT[:, :, cols], aT[:, d, :, cols], ALU.mult))
                    for ct in range(2):
                        chain.did(g.tensor_scalar(KD[:, ct], aT[:, d, ct, cols], pc("k_a", ct), omka[:, ct:ct + 1],
                                                  ALU.mult, ALU.add))
                    chain.did(g.tensor_tensor(E[:, :, 0, :], E[:, :, 0, :], kkT[:, :, cols], ALU.mult))
                    chain.settle()
                    chain.did(g.tensor_tensor(E[:, :, 1, :], E[:, :, 1, :], rT[:, :, cols], ALU.mult))
                    chain.did(g.tensor_tensor(KD, KD, kT_[:, :, cols], ALU.mult))
                    chain.did(g.tensor_tensor(BT, BT, E[:, :, 2, :], ALU.mult))
                    chain.settle()
                    chain.did(g.tensor_tensor(KD, KD, E[:, :, 2, :], ALU.mult))
                    chain.settle()
                    for q in range(2):
                        r = slice(HD * q, HD * q + HD)
                        chain.did(g.tensor_copy(BP[r, :, q, :], BT[r, :, :]))
                        chain.did(g.tensor_copy(KP[r, :, q, :], KD[r, :, :]))
                    chain.settle()
                    pool.sem_inc(s_pad, 1)
                    for hp in range(2):
                        order.wait_emptied(pool, ("ab", l, step, hp))
                    z = lambda B: B[:, :, :, 0:P]
                    four = lambda B: B.rearrange("p a b c -> p (a b) c")
                    N = AB.rearrange("p a b c -> p (a b) c")[:, :, 0:P]
                    mask = lambda name: cst(name, P, P * d)[:, None, :].broadcast_to([P, 4, P])
                    g.tensor_tensor(four(ND), N, mask("m16"), ALU.mult).then_inc(s_tri, 1)
                    pool.wait_ge(s_tri, 2 * gn + 1)
                    chain.did(g.tensor_tensor(four(XA), four(ND), ident[:, None, :].broadcast_to([P, 4, P]), ALU.add))
                    chain.did(g.tensor_tensor(four(O32), N, mask("m32"), ALU.mult))
                    chain.did(g.tensor_tensor(four(O64), N, mask("m64"), ALU.mult))
                    chain.settle()
                    pool.sem_inc(s_tri, 1)
                    if n == 2:
                        for dd in range(2):
                            order.wait_emptied(pool, ("so", l, dd))
                            for h in range(4):
                                r = slice(HD * (h % 2), HD * (h % 2) + HD)
                                g.dma_start(new_s[0, l, dd, h], s_fin[r, dd, h // 2, r]).then_inc(s_state_out, 16)


def kernel(**inputs):
    from concourse import bacc
    from concourse.bass_utils import run_bass_kernel_spmd

    nc = bacc.Bacc("TRN2", target_bir_lowering=False, num_devices=1)
    const, dft = constants()
    arrays = {name: np.ascontiguousarray(x) for name, x in inputs.items()}
    arrays["const"], arrays["dft"] = const, dft
    aps = {name: nc.dram_tensor(f"in_{name}", x.shape, F32, kind="ExternalInput").ap() for name, x in arrays.items()}
    shapes = [(1, CTX, D), (1, LAT, D), (1, DEPTH, CTX, NKV, HD), (1, DEPTH, CTX, NKV, HD), (1, DEPTH, 2, 4, HD, HD)]
    outs = [nc.dram_tensor(f"out_{i}", s, F32, kind="ExternalOutput").ap() for i, s in enumerate(shapes)]
    build(nc, aps, outs)
    r = run_bass_kernel_spmd(nc, [{f"in_{name}": x for name, x in arrays.items()}], core_ids=[0])
    return tuple(r.results[0][f"out_{i}"] for i in range(len(shapes)))
```

```python
from contextlib import ExitStack

import numpy as np

import concourse.bass as bass
from concourse import mybir

F32 = mybir.dt.float32
F32R = mybir.dt.float32r
ACT = mybir.ActivationFunctionType
ALU = mybir.AluOpType
AXX = mybir.AxisListType.X

P = 128
D = 1024
KT = D // P
DEPTH = 2
CTX, LAT = 128, 512
TOK = CTX + LAT
NT = TOK // P
HALF = TOK // 2
SEGS = ((0, 0, CTX), (1, CTX, TOK))
HD = 64
NQ, NKV = 4, 2
CH = 64
GRID_W = 64
NE = 8
DFE = 1024
EPS = 1e-6
GN_EPS = 64e-5
LOG_DECAY = -float(np.exp(-0.5))
BANKS = 8

ROWS = [("mod_b", 48), ("norm1", 8), ("norm2", 8), ("conv", 6), ("w0", 4), ("a0", 4),
        ("k_k", 2), ("k_a", 2), ("r_k", 2), ("ln_w", 2), ("ln_b", 2), ("c_ctx", 8), ("c", 8)]
ROW = {}
_n = 0
for _name, _k in ROWS:
    ROW[_name] = _n
    _n += _k
NROWS = _n

CAP = 224
SLOTS = 2 * P

CONSTS = [("ident", 128), ("ones", 128), ("blk", 128), ("band", 512), ("mzr", 512), ("m16", 256),
          ("m32", 256), ("m64", 256), ("cos", 128), ("sin", 128), ("dft64", 256), ("dft128", 256),
          ("scan", 128), ("rank", 8), ("eps", 2), ("upper", 128), ("slots", CAP), ("slot", 2)]
CC = {}
_n = 0
for _name, _k in CONSTS:
    CC[_name] = _n
    _n += _k
NCONST = _n

IN_TILES = [
    (("r", 0), 0, 0), (("r", 1), 0, 128), (("k", 0), 0, 256), (("k", 1), 0, 384),
    (("v", 0), 1, 0), (("v", 1), 1, 128), (("wa", 0), 1, 256), (("gd", 0), 1, 384),
    (("bx", 0), 3, 0), (("bx", 1), 3, 128), (("bb", 0), 3, 256), (("bb", 1), 3, 384),
    (("bc", 0), 4, 0), (("bc", 1), 4, 128), (("f", 0), 4, 256), (("f", 1), 4, 384)]
RW_TILES, CF_TILES = IN_TILES[:8], IN_TILES[8:]

MOD_ITEMS = 12
MOD_FIRST = 4
SUBS, SUB_FIRST = 2 * MOD_ITEMS, 2 * MOD_FIRST
SLOT = KT * 512
CHUNK = KT * 256
MAX_ROUNDS = -(-TOK // CAP)
DENSE_PARTS = ((0, 8), (8, 8), (16, 6))
EXP_F = DFE // P
EXP_CHUNKS = EXP_F + 4
PAIR_ITEMS = 2 * EXP_CHUNKS // 2
EXP_UNITS = 2 * EXP_CHUNKS
UNIT = CHUNK // 2

STEPS = [("c", 0, d) for d in range(2)] + [("s", i, d) for d in range(2) for i in range(4)]


def step_tile(step):
    kind, i, d = step
    return 0 if kind == "c" else (1 + i if d == 0 else 4 - i)


def key_blocks(j):
    if j == 0:
        return [(1, 0)]
    return ([(0, j - 1)] if j > 1 else []) + [(1, j), (2, None)] + ([(3, j + 1)] if j < NT - 1 else [])


def on_tensor(l, n):
    return l == 0 and n < SUB_FIRST and n // 2 % 2 == 1


HT_TILES = [(j, q) for j in range(NT) for q in range(2)]
HT_EARLY, HT_LATE = HT_TILES[:BANKS - 1], HT_TILES[BANKS - 1:]

FIRST_SUBS = (2, 3, 0, 1, 6, 7, 4, 5)


def sums_done(l, n):
    return sum(not on_tensor(l2, n2) for l2 in range(l + 1) for n2 in range(SUBS if l2 < l else n + 1))


def fourier_groups(j):
    return [[("f1", 0), ("f1", 1)], [("f1", 2), ("f1", 3)], [("f1", 4), ("f2c", 0)], [("f2", 0)], [("f2", 1)]][j]


def constants():
    c = np.zeros((P, NCONST), np.float32)
    i = np.arange(P)[:, None]
    j = np.arange(P)[None, :]

    def put(name, a, at=0):
        c[:, CC[name] + at:CC[name] + at + a.shape[1]] = a

    put("ident", np.eye(P))
    put("ones", np.ones((P, P)))
    put("blk", (i // HD == j // HD).astype(np.float32))
    put("band", np.where(j >= i, 0.0, -1e30))
    put("band", np.where(j <= i, 0.0, -1e30), 384)
    for d in range(2):
        before = (i < j) if d == 0 else (i > j)
        same = lambda n: i // n == j // n
        put("mzr", (before & same(CH)).astype(np.float32), 256 * d)
        put("mzr", ((before | (i == j)) & same(CH)).astype(np.float32), 256 * d + 128)
        put("m16", (before & same(16)).astype(np.float32), 128 * d)
        put("m32", (before & same(32) & ~same(16)).astype(np.float32), 128 * d)
        put("m64", (before & same(64) & ~same(32)).astype(np.float32), 128 * d)
    inv = 10000.0 ** (-np.arange(16, dtype=np.float32) / 16)
    t = np.arange(LAT)
    ang = np.stack([(t // GRID_W)[:, None] * inv, (t % GRID_W)[:, None] * inv], 1).astype(np.float32)
    for name, fn in (("cos", np.cos), ("sin", np.sin)):
        put(name, fn(ang).reshape(4, P, 32).transpose(1, 0, 2).reshape(P, 128))
    e = np.arange(HD)
    a64 = 2 * np.pi * ((e[:, None] * e[None, :]) % HD) / HD
    for g in range(2):
        s = slice(g * HD, (g + 1) * HD)
        c[s, CC["dft64"] + g * HD:CC["dft64"] + (g + 1) * HD] = np.cos(a64) / 8
        c[s, CC["dft64"] + 128 + g * HD:CC["dft64"] + 128 + (g + 1) * HD] = -np.sin(a64) / 8
    a128 = 2 * np.pi * ((i * j) % P) / P
    put("dft128", np.cos(a128) / np.sqrt(P))
    put("dft128", np.sin(a128) / np.sqrt(P), 128)
    put("scan", np.broadcast_to((j % CH != 0), (P, P)).astype(np.float32))
    put("rank", np.broadcast_to(NE - np.arange(NE), (P, NE)).astype(np.float32))
    put("eps", np.full((P, 1), EPS), 0)
    put("eps", np.full((P, 1), GN_EPS), 1)
    put("upper", (i < j).astype(np.float32))
    put("slots", np.broadcast_to(np.arange(CAP), (P, CAP)).astype(np.float32))
    slot = i + P * np.arange(2)[None, :]
    put("slot", np.where(slot < CAP, slot, -2.0 * TOK))
    u = np.arange(LAT)
    a512 = 2 * np.pi * ((u[:, None] * u[None, :]) % LAT) / LAT
    dft = np.stack([np.cos(a512), np.sin(a512)]) / np.sqrt(LAT)
    return c, dft.astype(np.float32)


FINE = ("x4", "d8", "x8", "x8t", "g1", "y1", "y1t", "g2", "y2", "wp")


def streams(name):
    return [(hp, par) for hp in range(2) for par in range(2)] if name in FINE else [(hp,) for hp in range(2)]


class Order:

    def __init__(self, filled, emptied):
        self.filled, self.emptied = filled, emptied
        self.at, self.by, self.count = {}, [], {k: [] for k in emptied}
        self.next = 0

    def add(self, name, engine):
        self.at[name] = len(self.by)
        self.count[engine].append(len(self.by))
        self.by.append(engine)

    def bank(self, name):
        return self.at[name] % BANKS

    def wait_filled(self, eng, name):
        eng.wait_ge(self.filled, self.at[name] + 1)

    def wait_emptied(self, eng, name):
        n = self.at[name]
        e = self.by[n]
        eng.wait_ge(self.emptied[e], self.count[e].index(n) + 1)

    def open(self, pe, name):
        n = self.at[name]
        assert n == self.next, (name, n, self.next)
        self.next += 1
        if n >= BANKS:
            e = self.by[n - BANKS]
            pe.wait_ge(self.emptied[e], self.count[e].index(n - BANKS) + 1)
        return n % BANKS


class Chain:

    def __init__(self, eng, sem):
        self.eng, self.sem, self.n = eng, sem, 0

    def did(self, ins):
        ins.then_inc(self.sem, 1)
        self.n += 1

    def settle(self, behind=0):
        self.eng.wait_ge(self.sem, self.n - behind)


class PairOrder(Order):

    def wait_filled(self, eng, name, it, back=0):
        eng.wait_ge(self.filled, (it + 1 - back) * len(self.by) + self.at[name] + 1)

    def wait_emptied(self, eng, name, it):
        eng.wait_ge(self.emptied["V"], (it + 1) * len(self.by) + self.at[name] + 1)

    def open(self, pe, name, it):
        n = self.at[name]
        assert n == self.next % len(self.by), (name, n, self.next)
        self.next += 1
        pe.wait_ge(self.emptied["V"], (it + 1) * len(self.by) + n - BANKS + 1)
        return n % BANKS


def list_pair_groups(order):
    def gather(k):
        for b in range(4):
            order.add(("ga", k, b), "V")

    def scatter(k):
        for dt in range(KT):
            for h in range(2):
                order.add(("sc", k, dt, h), "V")

    for k in range(2):
        for b in range(4):
            order.add(("bc", k, b), "V")
        if k == 0:
            gather(0)
        for f in range(EXP_F):
            order.add(("up", k, f), "V")
        for i in range(2):
            for q in range(2):
                order.add(("dw", k, i, q), "V")
        if k == 0:
            gather(1)
        scatter(k)
    assert len(order.by) % BANKS == 0


def list_groups(order):
    for l in range(DEPTH):
        order.add(("params", l), "V")
        if l == 0:
            for s in FIRST_SUBS[:4]:
                order.add(("ms", 0, s), "V")
            for j in range(NT):
                for q in range(2):
                    order.add(("x", j, q), "AV"[q])
            for s in FIRST_SUBS[4:]:
                order.add(("ms", 0, s), "V")
        for h in range(2):
            order.add(("ss1", l, h), "A")
        for n, (name, _, _) in enumerate(RW_TILES):
            for h in range(2):
                order.add(("in", l, name, h), "A" if name[0] in ("wa", "gd") else "AV"[h])
            if n > 0:
                order.add(("ms", l, SUB_FIRST + n - 1), "V")
        for j in range(NT):
            order.add(("qkv", l, j), "AV"[j % 2])
            if j in (0, 3):
                order.add(("ms", l, SUB_FIRST + (7 if j == 0 else 8)), "V")
        for n, (name, _, _) in enumerate(CF_TILES):
            for h in range(2):
                order.add(("in", l, name, h), "AV"[h])
            if n > 0:
                order.add(("ms", l, SUB_FIRST + 9 + n - 1), "V")
        for j in range(NT):
            order.add(("vt", l, j), "A")
        for ct in range(2):
            for h in range(2):
                order.add(("bonus", l, ct, h), "V")
        for ct in range(2):
            for h in range(2):
                order.add(("kks", l, ct, h), "A")
        order.add(("ckt", l), "V")
        for j in range(NT):
            order.add(("qt", l, j), "V")
        for kind in range(2):
            for d in range(2):
                for ct in range(2):
                    for h in range(2):
                        order.add(("up", l, kind, d, ct, h), "A")
        for j in range(NT):
            for h in range(NQ):
                order.add(("qk", l, j, h), "V")
            for name, x in fourier_groups(j):
                order.add((name, l, x), "A" if name == "f2c" else "AV"[x % 2])
            for h in range(NQ):
                order.add(("pt", l, j, h), "AV"[h % 2])
            order.add(("pv", l, j), "V")
            order.add(("ot", l, j), "A")
        for step in STEPS:
            if step[:2] == ("s", 0):
                order.add(("si", l, step[2]), "V")
            for name, engine in (("ab", "V"), ("dd", "V"), ("ak", "V"), ("tz", "A"), ("tb", "A"),
                                 ("n2", "A"), ("d2", "A"), ("akv", "V"), ("x2", "V"), ("n4", "A"), ("d4", "A"),
                                 ("x4", "V"), ("d8", "A"), ("x8", "V"), ("x8t", "A"), ("g1", "A"),
                                 ("y1", "V"), ("y1t", "A"), ("g2", "A"), ("y2", "V"), ("wp", "A"),
                                 ("rh", "V"), ("mt", "V"), ("s0", "V"), ("s1", "V"), ("yy", "V")):
                for key in streams(name):
                    order.add((name, l, step, *key), engine)
            if step[0] == "c":
                order.add(("so", l, step[2]), "V")
        for ct in range(2):
            for h in range(2):
                order.add(("mu", l, ct, h), "V")
        for ct in range(2):
            for h in range(2):
                order.add(("var", l, ct, h), "A")
        for ct in range(2):
            for h in range(2):
                order.add(("gup", l, ct, h), "V")
        for dt in range(KT):
            for h in range(2):
                order.add(("out", l, dt, h), "V")
        for h in range(2):
            order.add(("ss2", l, h), "A")
        if l == 0:
            for p, (_, nf) in enumerate(DENSE_PARTS):
                for f in range(nf):
                    for q in range(2):
                        for h in range(2):
                            order.add(("du", p, f, q, h), "AV"[q])
                    if p == 0 and f > 0:
                        order.add(("ms", 1, f - 1), "V")
                for c in range(4):
                    for t in range(2):
                        for h in range(2):
                            order.add(("dn", p, c, t, h), "V")
                    if p == c == 0:
                        order.add(("ms", 1, SUB_FIRST - 1), "V")
        else:
            order.add(("router", l), "V")
            for j, q in HT_EARLY:
                order.add(("ht", j, q), "V")
            order.add(("pos", l), "V")
            for j, q in HT_LATE:
                order.add(("ht", j, q), "V")
    for j in range(NT):
        for q in range(2):
            order.add(("y", j, q), "AV"[q])


def build(nc, a, outs):
    y_prompt, y_sample, new_k, new_v, new_s = outs
    with ExitStack() as ctx:
        def sb(name, cols):
            return ctx.enter_context(nc.sbuf_tensor(name, [P, cols], F32))

        def sem(name):
            return ctx.enter_context(nc.semaphore(name))

        def view(t, at, *dims):
            n = int(np.prod(dims))
            v = t[:, at:at + n]
            if len(dims) == 1:
                return v
            names = "abcde"[:len(dims)]
            spec = f"p ({' '.join(names)}) -> p {' '.join(names)}"
            return v.rearrange(spec, **{x: int(s) for x, s in zip(names[:-1], dims[:-1])})

        const = sb("const", NCONST)
        xT = view(sb("x_resid", KT * TOK), 0, KT, TOK)
        ring = sb("ring", 2 * SLOT)
        rs = sb("rms", TOK)[:, :]
        par_rows = rs[:, 0:P]
        par_t = sb("params", NROWS + 96 + 16 + 16 + 132 + 256 + 64 + 280 + 58 + 96)
        at = [0]

        def small(*dims):
            v = view(par_t, at[0], *dims)
            at[0] += int(np.prod(dims))
            return v

        cst = lambda name, n, off=0: const[:, CC[name] + off:CC[name] + off + n]
        ident, ones, blk = cst("ident", P), cst("ones", P), cst("blk", P)

        par = small(NROWS)
        mod = small(48, 2)
        silu_c = small(KT, 2)
        amul = small(KT, 2)
        qnw = small(HD)
        knw = small(HD)
        sink = small(NQ)
        g_up = small(256)
        router_w = small(KT, NE)
        rt_l, rt_key, rt_first, rt_second, gates, rt_t, posm = (small(NT, NE) for _ in range(7))
        cur_pos, cur_gate = small(2, NT), small(2, NT)
        gs_part, gslot = small(2, 2, 2), small(2, 2)
        rt_cnt, rt_m = small(NE), small(4)
        small(96)

        HT, MIX = 0, KT * TOK
        T1 = MIX + KT * TOK
        T2 = T1 + 8960
        SPARE = T2 + 11264
        TAIL = SPARE + 3 * TOK
        guard = nc.sbuf_tensor("arena", [P, TAIL + 1792], F32)
        arena = guard.__enter__()
        guard.__exit__(None, None, None)
        hT = view(arena, HT, KT, TOK)
        x_tok = view(arena, HT, NT, D)

        mixT = view(arena, MIX, KT, TOK)
        rank_up = view(arena, TAIL, 4, 256)
        mod_w = [view(arena, MIX + KT * 256 * i, KT, 256) for i in range(2)]
        acc = [view(rs, P, 2, 256), view(arena, MIX + 2 * KT * 256, 2, 256)]
        yT = mixT[:, 4:6, :]
        T3 = HT
        rT = view(arena, T1, 2, TOK)
        kT_ = view(arena, T1 + 1280, 2, TOK)
        vT = view(arena, T1 + 2560, 2, TOK)
        kkT = view(arena, T1 + 3840, 2, TOK)
        v_tok = view(arena, T1 + 5120, NT, 4, HD)
        waT = view(arena, T1 + 6400, TOK)
        gdT = view(arena, T1 + 7040, TOK)
        tmp = view(arena, T1 + 7680, 2, TOK)
        bxT = view(arena, T2, 2, TOK)
        bbT = view(arena, T2 + 1280, 2, TOK)
        bcT = view(arena, T2 + 2560, 2, TOK)
        lw = view(arena, T2, 2, 2, TOK)
        aT = view(arena, T2 + 2560, 2, 2, TOK)
        T2b = T2 + 5120
        qkv = view(arena, T2b, NT, 512)
        fT = view(arena, T2b + 2560, 2, TOK)
        qT = view(arena, T3, 2, TOK)
        kT = view(arena, T3 + 1280, TOK)
        ck_tok = view(arena, T3 + 1920, P)
        cv_tok = view(arena, T3 + 2048, P)
        ckT = view(arena, T3 + 2176, P)
        sc = view(arena, T3 + 2304, NQ, 512)
        qk_sq = view(arena, T2b + 3840, NT, 384)
        qk_t = view(arena, MIX + 2 * KT * 256 + 256, 2, 6, HD)
        rope = view(arena, TAIL + 1024, 4, 6, 2, 16)
        rk = view(arena, T2b + 3840, 2, TOK)
        conv_u = view(arena, SPARE, 2, TOK + 4)
        o_tok = view(arena, T3 + 4352, 4, HD)
        v1 = [view(arena, MIX + 4 * TOK, 2, 256)] + [view(arena, T2b + 3840 + 512 * j, 2, 256) for j in range(4)]
        pT = [view(arena, SPARE + 512 * h, 4, P) for h in range(3)] + [view(arena, T3 + 4608, 4, P)]
        s0_in = view(arena, T1 + 7680, 2, 2, P)
        s_fin = view(arena, T1 + 7680 + 512, 2, 2, P)

        free = [(T2b, SPARE), (T3, T3 + 5120), (SPARE, SPARE + 1920)]

        def wk(*dims):
            n = int(np.prod(dims))
            for i, (lo, hi) in enumerate(free):
                if hi - lo >= n:
                    free[i] = (lo + n, hi)
                    return view(arena, lo, *dims)
            raise ValueError("no room")

        AB, AK = wk(2, 2, 256), wk(2, 2, 256)
        EX = [view(arena, TAIL, 2, 3, P), wk(2, 3, P)]
        ST = wk(2, 3, P)
        DD, ND, D2, N2, O32, O64, XA, XB = (wk(2, 2, P) for _ in range(8))
        RR, WP = wk(2, 2, P), wk(2, 2, P)
        BP, KP = view(arena, TAIL + 768, 2, 2, P), view(arena, TAIL + 1280, 2, 2, P)
        BM = wk(2, 2, P)
        BC, KC = wk(2, 2, P), wk(2, 2, P)
        BT, KD, RH = view(arena, T1 + 6400, 2, P), view(arena, T1 + 6400 + 256, 2, P), wk(2, P)
        att = view(par_t, at[0] - 96, 2, 24)
        qk_ss = view(par_t, at[0] - 48, NT * 6)
        LC = view(par_t, at[0] - 18, 2, 2, 2)
        omka = view(par_t, at[0] - 10, 2)

        def sbr(name, cols):
            return ctx.enter_context(nc.sbuf_tensor(name, [P, cols], F32R))

        GW = 6144
        g_hi, g_lo = sbr("g_hi", GW), sbr("g_lo", GW)
        h_hi, h_lo = sbr("h_hi", KT * TOK), sbr("h_lo", KT * TOK)
        w_hi, w_lo = sbr("w_hi", 2 * CHUNK), sbr("w_lo", 2 * CHUNK)
        sel_t = sbr("select", NT * CAP + 2 * TOK)
        silt = sb("silu", 2 * TOK)
        f32 = lambda x: x.bitcast(F32)
        sil = view(silt, 0, 2, TOK)
        sel = view(sel_t, 0, NT, CAP)
        selT = view(sel_t, NT * CAP, 2, TOK)
        e_sil = view(silt, 0, 2, CAP)
        junk = view(silt, 2 * CAP, 2, 3 * P)
        xg = [view(t, 0, KT, CAP) for t in (g_hi, g_lo)]
        eg = [view(t, KT * CAP, EXP_F, SLOTS) for t in (g_hi, g_lo)]
        yg = [view(t, KT * (CAP + SLOTS), 2, D) for t in (g_hi, g_lo)]
        dg = [view(t, 0, 8, TOK) for t in (g_hi, g_lo)]
        hc = [view(t, 0, KT, TOK) for t in (h_hi, h_lo)]
        ht = [view(t, 0, NT, D) for t in (h_hi, h_lo)]
        rounds_t = ctx.enter_context(nc.sbuf_tensor("rounds", [P, 2], mybir.dt.int32))

        psum = [ctx.enter_context(nc.psum_tensor(f"bank{i}", [P, 512], F32)) for i in range(BANKS)]

        filled = sem("bank_filled")
        emptied = {"A": sem("emptied_by_scalar"), "V": sem("emptied_by_vector")}
        order = Order(filled, emptied)
        list_groups(order)
        order2 = PairOrder(sem("pair_filled"), {"V": sem("pair_emptied")})
        list_pair_groups(order2)

        s_const, s_tables, s_x, s_par = sem("const_in"), sem("tables_in"), sem("x_in"), sem("params_in")
        s_ring = [sem(f"ring_in{i}") for i in range(2)]
        s_macc, s_mod_in = sem("mod_sums_ready"), [sem(f"mod_weights_in{i}") for i in range(2)]
        s_rank, s_gup_in, s_cache, s_state = sem("rank_weights_in"), sem("small_weights_in"), sem("cache_in"), sem("state_in")
        s_zero, s_zero2 = sem("buffers_zeroed"), sem("late_buffers_zeroed")
        s_silc, s_sq, s_hmul, s_h = sem("silu_c_ready"), sem("squares_ready"), sem("h_scaled"), sem("h_ready")
        s_kkr, s_kq, s_rk = sem("kk_raw"), sem("kk_squared"), sem("rk_ready")
        s_qsq, s_qss, s_qrt, s_qk, s_rope = (sem("qk_squares"), sem("qk_sumsq"), sem("qk_root"), sem("qk_normed"),
                                             sem("qk_roped"))
        s_max, s_exp = sem("row_max_ready"), sem("exp_done")
        s_cu, s_conv = sem("conv_gated"), sem("conv_done")
        s_sum, s_ex, s_pad, s_tri = sem("decay_sums"), sem("decay_exp"), sem("scaled_ready"), sem("triangles_ready")
        s_st0 = sem("state_zeroed")
        s_nkk = sem("kk_normed")
        s_gn, s_gsq = sem("y_centred"), sem("y_squared")
        s_kv_out, s_state_out, s_y_out = sem("kv_stored"), sem("states_stored"), sem("y_stored")
        s_hi, s_lo, s_sil, s_ghi = sem("weights_hi"), sem("weights_lo"), sem("silu_done"), sem("g_hi_done")
        s_glo = sem("g_lo_done")
        s_hhi, s_hlo = sem("h_hi_done"), sem("h_lo_done")
        s_rmax, s_rexp, s_rounds = sem("router_max"), sem("router_exp"), sem("rounds_ready")
        s_moe_done = sem("experts_done")
        s_ring2 = [sem(f"pair_ring_in{i}") for i in range(2)]
        s_hi2, s_lo2, s_sil2, s_ghi2, s_glo2 = (sem("pair_weights_hi"), sem("pair_weights_lo"), sem("pair_silu"),
                                               sem("pair_g_hi"), sem("pair_g_lo"))
        s_sel, s_xhi, s_gs, s_yhi, s_used2 = (sem("select_ready"), sem("gathered_hi"), sem("slot_gates"),
                                             sem("expert_out_hi"), sem("unit_used"))
        s_ca, s_cv, s_cp = sem("scalar_chain"), sem("vector_chain"), sem("pool_chain")

        USED_SIGNALS = EXP_F + 2 * 3

        block = ctx.enter_context(nc.Block())

        items = []
        for l in range(DEPTH):
            for i in range(MOD_FIRST if l == 0 else 0):
                items.append(("mod", l, i))
            for i in range(5):
                items.append(("win", l, i))
            items.append(("dft", l, 0))
            for i in range(2):
                items.append(("wout", l, i))
            if l == 0:
                for p, (_, nf) in enumerate(DENSE_PARTS):
                    for i in range(nf // 2):
                        items.append(("up", l, p, i))
                        if p == 0:
                            items.append(("mod", l + 1, i))
                    for i in range(2):
                        items.append(("down", l, p, i))
        number = {it: n for n, it in enumerate(items)}

        def load_count(name):
            return 32 * (number[name] // 2 + 1)

        chunks = [(p, kind, i) for p, (_, nf) in enumerate(DENSE_PARTS)
                  for kind, n in (("up", nf), ("down", 4)) for i in range(n)]
        chunk_no = {c: n for n, c in enumerate(chunks)}

        def mod_buffer(l, n):
            return n % 2 if l == 0 and n < SUB_FIRST else 0

        def item(name):
            return (number[name] % 2) * SLOT

        def wait_item(eng, name):
            eng.wait_ge(s_ring[number[name] % 2], load_count(name))

        def wait_used(sp, name):
            kind, l = name[:2]
            if kind == "mod":
                n = 2 * name[2] + 1
                if on_tensor(l, n):
                    order.wait_filled(sp, ("ms", l, n))
                else:
                    sp.wait_ge(s_macc, sums_done(l, n))
            elif kind == "win":
                i = name[2]
                if i == 2:
                    order.wait_filled(sp, ("qkv", l, NT - 1))
                else:
                    order.wait_filled(sp, ("in", l, [t for t in IN_TILES if t[1] == i][-1][0], 1))
            elif kind == "dft":
                order.wait_filled(sp, ("f2", l, 1))
            elif kind == "wout":
                order.wait_filled(sp, ("out", l, 4 * name[2] + 3, 1))
            else:
                sp.wait_ge(s_lo, chunk_no[(name[2], kind, 2 * name[3] + 1)] + 1)

        @block.sync
        def _(sp):
            first = 2 * P
            sp.dma_start(const[:, 0:first], a["const"][:, 0:first]).then_inc(s_const, 16)

            def load(name):
                n = number[name]
                if n >= 2:
                    wait_used(sp, items[n - 2])
                kind, l = name[:2]
                s, base = n % 2, item(name)
                if kind == "mod":
                    w = view(ring, base, KT, 512)
                    src = a["mod_w"][l].rearrange("(k p) n -> p k n", p=P)[:, :, 512 * name[2]:512 * (name[2] + 1)]
                    pieces = [(w[:, 4 * i:4 * i + 4, :], src[:, 4 * i:4 * i + 4, :]) for i in range(2)]
                elif kind == "win":
                    i = name[2]
                    src = a["w_in"][l].rearrange("(k p) n -> p k n", p=P)
                    if i < 4:
                        lo, n_ = [(1280, 512), (1792, 448), (0, 512), (512, 512)][i]
                        w = view(ring, base, KT, n_)
                        pieces = [(w[:, 4 * q:4 * q + 4, :], src[:, 4 * q:4 * q + 4, lo:lo + n_]) for q in range(2)]
                    else:
                        w = view(ring, base, KT, 512)
                        pieces = [(w[:, :, 0:256], src[:, :, 1024:1280]), (w[:, :, 256:512], src[:, :, 2240:2496])]
                elif kind == "dft":
                    w = view(ring, base, 2, 4, 512)
                    pieces = [(w[:, i], a["dft"][i].rearrange("(j p) n -> p j n", p=P)) for i in range(2)]
                elif kind == "wout":
                    i = name[2]
                    w = view(ring, base, KT, 512)
                    src = a["w_out"][l].rearrange("(k p) n -> p k n", p=P)[:, :, 512 * i:512 * (i + 1)]
                    pieces = [(w[:, 4 * q:4 * q + 4, :], src[:, 4 * q:4 * q + 4, :]) for q in range(2)]
                elif kind == "up":
                    _, _, p, i = name
                    w = view(ring, base, 2, KT, 256)
                    f0 = P * (DENSE_PARTS[p][0] + 2 * i)
                    pieces = [(w[:, q], a[nm][0].rearrange("(k p) n -> p k n", p=P)[:, :, f0:f0 + 256])
                              for q, nm in enumerate(("ffn_w1", "ffn_w3"))]
                else:
                    _, _, p, i = name
                    f0, nf = DENSE_PARTS[p]
                    w = view(ring, base, nf, 512)
                    src = a["ffn_w2"][0].rearrange("(k p) n -> p k n", p=P)[:, f0:f0 + nf, 512 * i:512 * (i + 1)]
                    pieces = [(w[:, :nf // 2], src[:, :nf // 2]), (w[:, nf // 2:], src[:, nf // 2:])]
                for dst, src in pieces:
                    sp.dma_start(dst, src).then_inc(s_ring[s], 16)

            for l in range(DEPTH):
                if l > 0:
                    sp.wait_ge(s_h, KT * 2 * l)
                vec = [("mod_b", a["mod_b"][l].rearrange("(r p) -> r p", p=P)),
                       ("norm1", a["norm1_w"][l].rearrange("(r p) -> r p", p=P)),
                       ("norm2", a["norm2_w"][l].rearrange("(r p) -> r p", p=P)),
                       ("conv", a["conv_w"][l].rearrange("t (r p) -> (t r) p", p=P)),
                       ("w0", a["rwkv_w0"][l].rearrange("d (r p) -> (d r) p", p=P)),
                       ("a0", a["rwkv_a0"][l].rearrange("d (r p) -> (d r) p", p=P)),
                       ("k_k", a["rwkv_k_k"][l].rearrange("(r p) -> r p", p=P)),
                       ("k_a", a["rwkv_k_a"][l].rearrange("(r p) -> r p", p=P)),
                       ("r_k", a["rwkv_r_k"][l].rearrange("(r q) p -> r (q p)", q=2)),
                       ("ln_w", a["rwkv_ln_w"][l].rearrange("(r p) -> r p", p=P)),
                       ("ln_b", a["rwkv_ln_b"][l].rearrange("(r p) -> r p", p=P)),
                       ("c_ctx", a["c_ctx"].rearrange("(r p) -> r p", p=P)),
                       ("c", a["c"][0].rearrange("(r p) -> r p", p=P))]
                for name, src in vec:
                    n = src.shape[0]
                    sp.dma_start(par_rows[ROW[name]:ROW[name] + n, :], src).then_inc(s_par, 16)
                if l == 0:
                    load(("mod", l, 0))
                    load(("mod", l, 1))
                    sp.dma_start(x_tok[:, 0, :], a["x_prompt"][0]).then_inc(s_x, 16)
                    sp.dma_start(x_tok[:, 1:NT, :], a["x_sample"][0].rearrange("(j p) n -> p j n", p=P)).then_inc(s_x, 16)
                    sp.dma_start(const[:, first:NCONST], a["const"][:, first:NCONST]).then_inc(s_tables, 16)
                    load(("mod", l, 2))
                    load(("mod", l, 3))
                sp.wait_ge(s_zero, l + 1)
                for d in range(2):
                    sp.dma_start(rank_up[32 * d:32 * d + 32, d, :], a["rwkv_w_up"][l, d]).then_inc(s_rank, 16)
                    sp.dma_start(rank_up[64 + 32 * d:96 + 32 * d, 2 + d, :], a["rwkv_a_up"][l, d]).then_inc(s_rank, 16)
                sp.dma_start(g_up[0:64, :], a["rwkv_g_up"][l]).then_inc(s_gup_in, 16)
                sp.dma_start(qnw, a["q_norm_w"][l][None, :].broadcast_to([P, HD])).then_inc(s_gup_in, 16)
                sp.dma_start(knw, a["k_norm_w"][l][None, :].broadcast_to([P, HD])).then_inc(s_gup_in, 16)
                sp.dma_start(sink, a["attn_sink"][l][None, :].broadcast_to([P, NQ])).then_inc(s_gup_in, 16)
                sp.dma_start(router_w, a["router_w"][0].rearrange("(k p) e -> p k e", p=P)).then_inc(s_gup_in, 16)
                def load_mod(*subs):
                    for n in subs:
                        m = n - SUB_FIRST + (SUBS - SUB_FIRST) * l
                        if n >= SUB_FIRST + 2:
                            sp.wait_ge(s_macc, sums_done(l, n - 2))
                        src = a["mod_w"][l].rearrange("(k p) n -> p k n", p=P)[:, :, 256 * n:256 * (n + 1)]
                        sp.dma_start(mod_w[m % 2], src).then_inc(s_mod_in[m % 2], 16)

                load(("win", l, 0))
                load_mod(*range(SUB_FIRST, SUB_FIRST + 2))
                load(("win", l, 1))
                load_mod(*range(SUB_FIRST + 2, SUB_FIRST + 6))
                load(("win", l, 2))
                load_mod(*range(SUB_FIRST + 6, SUB_FIRST + 10))
                load(("win", l, 3))
                load(("win", l, 4))
                load_mod(*range(SUB_FIRST + 10, SUBS))
                order.wait_filled(sp, ("in", l, CF_TILES[-1][0], 1))
                sp.dma_start(ck_tok, a["cache_k"][0, l].rearrange("t h d -> t (h d)")).then_inc(s_cache, 16)
                sp.dma_start(cv_tok, a["cache_v"][0, l].rearrange("t h d -> t (h d)")).then_inc(s_cache, 16)
                load(("dft", l, 0))
                load(("wout", l, 0))
                load(("wout", l, 1))
                for it in items:
                    if l == 0 and (it[0] in ("up", "down") or it[:2] == ("mod", 1)):
                        load(it)
            for it in items[-2:]:
                wait_used(sp, it)
            sp.wait_ge(s_rounds, 1)
            rounds = sp.value_load(rounds_t[0:1, 0:1], min_val=1, max_val=MAX_ROUNDS)
            with sp.Fori(0, rounds) as r:
                with sp.Fori(0, NE // 2) as pair:
                    it = r * (NE // 2) + pair
                    for n in range(PAIR_ITEMS):
                        k, i = n // (PAIR_ITEMS // 2), n % (PAIR_ITEMS // 2)
                        e = 2 * pair + k
                        sp.wait_ge(s_lo2, (it + 1) * 2 * EXP_UNITS + 4 * (n - 1))
                        if i < EXP_F // 2:
                            w = view(ring, ((n + len(items)) % 2) * SLOT, 2, KT, 256)
                            pieces = [(w[:, q], a[nm][0, bass.ds(e, 1)].rearrange("e (k p) n -> p (e k) n", p=P)
                                       [:, :, 256 * i:256 * (i + 1)]) for q, nm in enumerate(("moe_w1", "moe_w3"))]
                        else:
                            i -= EXP_F // 2
                            w = view(ring, ((n + len(items)) % 2) * SLOT, EXP_F, 512)
                            src = a["moe_w2"][0, bass.ds(e, 1)].rearrange("e (k p) n -> p (e k) n", p=P)
                            pieces = [(w[:, q:q + 4], src[:, q:q + 4, 512 * i:512 * (i + 1)]) for q in (0, 4)]
                        for dst, src in pieces:
                            sp.dma_start(dst, src).then_inc(s_ring2[n % 2], 16)
            for j in range(NT):
                for q in range(2):
                    order.wait_emptied(sp, ("y", j, q))
                dst = y_prompt[0] if j == 0 else y_sample[0, P * (j - 1):P * j, :]
                sp.dma_start(dst, x_tok[:, j, :]).then_inc(s_y_out, 16)
            sp.wait_ge(s_y_out, 16 * NT)
            sp.wait_ge(s_kv_out, DEPTH * 2 * 16)
            sp.wait_ge(s_state_out, DEPTH * 8 * 16)

        @block.tensor
        def _(pe):
            mm, tr = nc.tensor.matmul, nc.tensor.transpose

            def end(ins):
                ins.then_inc(filled, 1)

            pe.wait_ge(s_const, 16)

            def sum_squares(name, l, nth):
                for h in range(2):
                    b = psum[order.open(pe, (name, l, h))]
                    for k in range(KT):
                        if h == 0:
                            pe.wait_ge(s_sq, KT * (nth - 1) + k + 1)
                        ins = mm(b[:, 0:HALF], ones, hT[:, k, HALF * h:HALF * (h + 1)], start=(k == 0), stop=(k == KT - 1))
                    end(ins)

            def mod_sub(l, n):
                if on_tensor(l, n):
                    wait_item(pe, ("mod", l, n // 2))
                    w = view(ring, item(("mod", l, n // 2)), KT, 512)
                    b = psum[order.open(pe, ("ms", l, n))]
                    for t in range(2):
                        for k in range(KT):
                            c0 = 256 * (n % 2) + P * t
                            ins = mm(b[:, 2 * t:2 * t + 2], w[:, k, c0:c0 + P], silu_c[:, k, :],
                                     start=(k == 0), stop=(k == KT - 1))
                    end(ins)
                    return
                pe.wait_ge(s_macc, sums_done(l, n))
                b = psum[order.open(pe, ("ms", l, n))]
                sums = acc[mod_buffer(l, n)]
                for t in range(2):
                    for vec in range(2):
                        ins = mm(b[:, 2 * t + vec:2 * t + vec + 1], sums[:, vec, P * t:P * t + P], ones[:, 0:1],
                                 start=True, stop=True)
                end(ins)

            def in_tiles(l, tiles, sub):
                at_item = None
                for n, (name, it, col) in enumerate(tiles):
                    if it != at_item:
                        at_item = it
                        wait_item(pe, ("win", l, it))
                    width = {1: 448}.get(it, 512)
                    w = view(ring, item(("win", l, it)), KT, width)
                    m = 64 if name[0] == "gd" else P
                    for h in range(2):
                        b = psum[order.open(pe, ("in", l, name, h))]
                        for k in range(KT):
                            if (name, h) == (RW_TILES[0][0], 0):
                                pe.wait_ge(s_h, KT * 2 * l + k + 1)
                            ins = mm(b[0:m, 0:HALF], w[:, k, col:col + m], hT[:, k, HALF * h:HALF * (h + 1)],
                                     start=(k == 0), stop=(k == KT - 1))
                        end(ins)
                    if n > 0:
                        mod_sub(l, sub + n - 1)

            def split3(out, lhs, rhs, first, last):
                for i, (x, y) in enumerate(((0, 0), (0, 1), (1, 0))):
                    ins = mm(out, lhs[x], rhs[y], start=(first and i == 0), stop=(last and i == 2))
                return ins

            def weights(n, *dims):
                return [view(t, (n % 2) * CHUNK, *dims) for t in (w_hi, w_lo)]

            def dense():
                for p, (_, nf) in enumerate(DENSE_PARTS):
                    for f in range(nf):
                        n = chunk_no[(p, "up", f)]
                        pe.wait_ge(s_lo, n + 1)
                        w = weights(n, 2, KT, P)
                        for q in range(2):
                            for h in range(2):
                                b = psum[order.open(pe, ("du", p, f, q, h))]
                                cols = slice(HALF * h, HALF * (h + 1))
                                for k in range(KT):
                                    if (p, f, q, h) == (0, 0, 0, 0):
                                        pe.wait_ge(s_hlo, k + 1)
                                    ins = split3(b[:, 0:HALF], [x[:, q, k, :] for x in w], [x[:, k, cols] for x in hc],
                                                 k == 0, k == KT - 1)
                                end(ins)
                        if p == 0 and f > 0:
                            mod_sub(1, f - 1)
                    for c in range(4):
                        n = chunk_no[(p, "down", c)]
                        pe.wait_ge(s_lo, n + 1)
                        w = weights(n, nf, 256)
                        for t in range(2):
                            for h in range(2):
                                b = psum[order.open(pe, ("dn", p, c, t, h))]
                                cols = slice(HALF * h, HALF * (h + 1))
                                for f in range(nf):
                                    if (c, t, h) == (0, 0, 0):
                                        pe.wait_ge(s_glo, DENSE_PARTS[p][0] + f + 1)
                                    ins = split3(b[:, 0:HALF], [x[:, f, P * t:P * t + P] for x in w],
                                                 [x[:, f, cols] for x in dg], f == 0, f == nf - 1)
                                end(ins)
                        if p == c == 0:
                            mod_sub(1, SUB_FIRST - 1)

            def experts():
                o = order2
                pe.sem_inc(o.filled, len(o.by))
                pe.sem_inc(s_used2, 2 * USED_SIGNALS)
                pe.wait_ge(s_rounds, 1)
                rounds = pe.value_load(rounds_t[0:1, 0:1], min_val=1, max_val=MAX_ROUNDS)
                with pe.Fori(0, rounds) as r:
                    with pe.Fori(0, NE // 2) as pair:
                        it = r * (NE // 2) + pair

                        def end2(ins):
                            ins.then_inc(o.filled, 1)

                        def unit(u, *dims):
                            pe.wait_ge(s_lo2, (it + 1) * 2 * EXP_UNITS + u + 1)
                            return [view(t, (u % 4) * UNIT, *dims) for t in (w_hi, w_lo)]

                        def spread(k):
                            pe.wait_ge(s_sel, 2 * it + k + 1)
                            for b4 in range(4):
                                b = psum[o.open(pe, ("bc", k, b4), it)]
                                src = cur_pos if b4 < 2 else cur_gate
                                lo, n = ((0, 3), (3, 2))[b4 % 2]
                                for j in range(n):
                                    ins = mm(b[:, P * j:P * j + P], src[:, k, lo + j:lo + j + 1].broadcast_to([P, P]),
                                             ident, start=True, stop=True)
                                end2(ins)

                        def gather(k):
                            pe.wait_ge(s_sel, 2 * it + k + 1)
                            for b4 in range(4):
                                b = psum[o.open(pe, ("ga", k, b4), it)]
                                for t in range(2):
                                    d = 2 * b4 + t
                                    for j in range(NT):
                                        for x in range(2):
                                            ins = mm(b[:, CAP * t:CAP * t + CAP], ht[x][:, j, P * d:P * d + P], sel[:, j, :],
                                                     start=(j + x == 0), stop=(j == NT - 1 and x == 1))
                                end2(ins)

                        def scatter(k):
                            o.wait_emptied(pe, ("bc", k, 1), it)
                            for dt in range(KT):
                                if dt % 4 == 0:
                                    o.wait_emptied(pe, ("dw", k, dt // 4, 1), it)
                                for h in range(2):
                                    b = psum[o.open(pe, ("sc", k, dt, h), it)]
                                    for q in range(2):
                                        for x in range(2):
                                            ins = mm(b[:, 0:HALF], yg[x][:, q, P * dt:P * dt + P],
                                                     selT[:, q, HALF * h:HALF * (h + 1)],
                                                     start=(q + x == 0), stop=(q + x == 2))
                                    end2(ins)

                        for k in range(2):
                            spread(k)
                            if k == 0:
                                gather(0)
                            for f in range(EXP_F):
                                b = psum[o.open(pe, ("up", k, f), it)]
                                for q in range(2):
                                    w = unit(EXP_UNITS * k + 2 * f + q, KT, P)
                                    for kt in range(KT):
                                        if f == q == kt % 2 == 0:
                                            o.wait_emptied(pe, ("ga", k, kt // 2), it)
                                        ins = split3(b[:, CAP * q:CAP * q + CAP], [x[:, kt, :] for x in w],
                                                     [x[:, kt, :] for x in xg], kt == 0, kt == KT - 1)
                                    if q == 0:
                                        ins.then_inc(s_used2, 1)
                                end2(ins)
                            for i in range(2):
                                banks = [psum[o.open(pe, ("dw", k, i, q), it)] for q in range(2)]
                                for c in range(4):
                                    w = unit(EXP_UNITS * k + 2 * EXP_F + 4 * i + c, 2, 512)
                                    if i == 0:
                                        pe.wait_ge(s_glo2, (2 * it + k) * EXP_F + 2 * c + 2)
                                    for q in range(2):
                                        for f in range(2):
                                            ins = split3(banks[q][:, :], [x[:, 2 * c + f, P * q:P * q + P] for x in eg],
                                                         [x[:, f, :] for x in w], c + f == 0, c + f == 4)
                                        if c == 3:
                                            end2(ins)
                                    if c < 3:
                                        ins.then_inc(s_used2, 1)
                            if k == 0:
                                gather(1)
                            scatter(k)

            for l in range(DEPTH):
                pe.wait_ge(s_par, (l + 1) * 16 * len(ROWS))
                b = psum[order.open(pe, ("params", l))]
                end(tr(b[:, 0:NROWS], par_rows[0:NROWS, :], ident[0:NROWS, 0:NROWS]))
                if l == 0:
                    pe.wait_ge(s_silc, 1)
                    for n in FIRST_SUBS[:4]:
                        mod_sub(l, n)
                    pe.wait_ge(s_x, 32)
                    for j in range(NT):
                        for q in range(2):
                            b = psum[order.open(pe, ("x", j, q))]
                            for k in range(4):
                                ins = tr(b[:, P * k:P * k + P], x_tok[:, j, P * (4 * q + k):P * (4 * q + k) + P], ident)
                            end(ins)
                    for n in FIRST_SUBS[4:]:
                        mod_sub(l, n)
                if l == 0:
                    pe.wait_ge(s_tables, 16)
                sum_squares("ss1", l, 2 * l + 1)
                in_tiles(l, RW_TILES, SUB_FIRST)
                wait_item(pe, ("win", l, 2))
                w = view(ring, item(("win", l, 2)), KT, 512)
                for j in range(NT):
                    b = psum[order.open(pe, ("qkv", l, j))]
                    for k in range(KT):
                        ins = mm(b[:, :], hT[:, k, P * j:P * j + P], w[:, k, :], start=(k == 0), stop=(k == KT - 1))
                    end(ins)
                    if j in (0, 3):
                        mod_sub(l, SUB_FIRST + (7 if j == 0 else 8))
                in_tiles(l, CF_TILES, SUB_FIRST + 9)
                for ct in range(2):
                    for h in range(2):
                        order.wait_emptied(pe, ("in", l, ("v", ct), h))
                for j in range(NT):
                    b = psum[order.open(pe, ("vt", l, j))]
                    for ct in range(2):
                        ins = tr(b[:, P * ct:P * ct + P], vT[:, ct, P * j:P * j + P], ident)
                    end(ins)
                pe.wait_ge(s_rk, l + 1)
                for ct in range(2):
                    for h in range(2):
                        b = psum[order.open(pe, ("bonus", l, ct, h))]
                        end(mm(b[:, 0:HALF], blk, rk[:, ct, HALF * h:HALF * (h + 1)], start=True, stop=True))
                pe.wait_ge(s_kq, l + 1)
                for ct in range(2):
                    for h in range(2):
                        b = psum[order.open(pe, ("kks", l, ct, h))]
                        end(mm(b[:, 0:HALF], blk, tmp[:, ct, HALF * h:HALF * (h + 1)], start=True, stop=True))
                pe.wait_ge(s_cache, 32 * (l + 1))
                b = psum[order.open(pe, ("ckt", l))]
                end(tr(b[:, 0:P], ck_tok, ident))
                for j in range(NT):
                    if j == 0:
                        pe.wait_ge(s_qk, l * NT + 1)
                    else:
                        pe.wait_ge(s_rope, l * (NT - 1) + j)
                    b = psum[order.open(pe, ("qt", l, j))]
                    for t in range(3):
                        ins = tr(b[:, P * t:P * t + P], qkv[:, j, P * t:P * t + P], ident)
                    end(ins)
                pe.wait_ge(s_rank, 16 * 4 * (l + 1))
                for h in range(2):
                    order.wait_emptied(pe, ("in", l, ("wa", 0), h))
                for kind in range(2):
                    for d in range(2):
                        for ct in range(2):
                            for h in range(2):
                                b = psum[order.open(pe, ("up", l, kind, d, ct, h))]
                                end(mm(b[:, 0:HALF], rank_up[:, 2 * kind + d, P * ct:P * ct + P],
                                       waT[:, HALF * h:HALF * (h + 1)], start=True, stop=True))
                order.wait_emptied(pe, ("ckt", l))
                for j in range(NT):
                    order.wait_emptied(pe, ("qt", l, j))
                for ct in range(2):
                    for h in range(2):
                        order.wait_emptied(pe, ("in", l, ("f", ct), h))

                def fourier(name, x):
                    if name == "f1":
                        b = psum[order.open(pe, ("f1", l, x))]
                        for ct in range(2):
                            ins = mm(b[:, 256 * ct:256 * ct + 256], fT[:, ct, P * x:P * x + P], cst("dft64", 256),
                                     start=True, stop=True)
                    elif name == "f2c":
                        order.wait_emptied(pe, ("f1", l, 0))
                        b = psum[order.open(pe, ("f2c", l, 0))]
                        for ct in range(2):
                            for cs in range(2):
                                ins = mm(b[:, P * ct:P * ct + P], v1[0][:, ct, P * cs:P * cs + P],
                                         cst("dft128", P, P * cs), start=(cs == 0), stop=(cs == 1))
                    else:
                        for i in range(1, NT):
                            order.wait_emptied(pe, ("f1", l, i))
                        wait_item(pe, ("dft", l, 0))
                        w = view(ring, item(("dft", l, 0)), 2, 4, 512)
                        b = psum[order.open(pe, ("f2", l, x))]
                        for i in range(4):
                            for cs in range(2):
                                ins = mm(b[:, :], v1[1 + i][:, x, P * cs:P * cs + P], w[:, cs, i, :],
                                         start=(i + cs == 0), stop=(i + cs == 4))
                    end(ins)

                for j in range(NT):
                    blocks = key_blocks(j)
                    for h in range(NQ):
                        kv, g = h // 2, h % 2
                        r0 = HD * kv
                        b = psum[order.open(pe, ("qk", l, j, h))]
                        for pos, kb in blocks:
                            rhs = ckT[r0:r0 + HD, :] if kb is None else kT[r0:r0 + HD, P * kb:P * kb + P]
                            ins = mm(b[:, P * pos:P * pos + P], qT[r0:r0 + HD, g, P * j:P * j + P], rhs,
                                     start=True, stop=True)
                        end(ins)
                    for name, x in fourier_groups(j):
                        fourier(name, x)
                    pe.wait_ge(s_exp, l * NT + j + 1)
                    for h in range(NQ):
                        b = psum[order.open(pe, ("pt", l, j, h))]
                        for pos, kb in blocks:
                            ins = tr(b[:, P * pos:P * pos + P], sc[:, h, P * pos:P * pos + P], ident)
                        end(ins)
                    b = psum[order.open(pe, ("pv", l, j))]
                    for h in range(NQ):
                        order.wait_emptied(pe, ("pt", l, j, h))
                        kv = h // 2
                        for i, (pos, kb) in enumerate(blocks):
                            v = cv_tok if kb is None else qkv[:, kb, 384:512]
                            ins = mm(b[:, HD * h:HD * h + HD], pT[h][:, pos, :], v[:, HD * kv:HD * kv + HD],
                                     start=(i == 0), stop=(i == len(blocks) - 1))
                    end(ins)
                    order.wait_emptied(pe, ("pv", l, j))
                    b = psum[order.open(pe, ("ot", l, j))]
                    for t in range(2):
                        ins = tr(b[:, P * t:P * t + P], o_tok[:, 2 * t:2 * t + 2, :], ident)
                    end(ins)
                for j in range(NT):
                    order.wait_emptied(pe, ("vt", l, j))
                for n, step in enumerate(STEPS):
                    kind, i, d = step
                    j = step_tile(step)
                    T = lambda name, *key: (name, l, step, *key)
                    gn = l * len(STEPS) + n
                    if (kind, i) == ("s", 0):
                        pe.wait_ge(s_state, 16 * 8 * (l + 1))
                        b = psum[order.open(pe, ("si", l, d))]
                        for hp in range(2):
                            ins = tr(b[:, P * hp:P * hp + P], s0_in[:, d, hp, :], ident)
                        end(ins)
                    v0 = 2 * i if kind == "s" else 0
                    ver = lambda s: (v0 + s) % 3
                    pe.wait_ge(s_pad, gn + 1)
                    V = lambda hp, par: v_tok[:, j, 2 * hp + par, :]

                    def after(key, *names):
                        for name in names:
                            for x in streams(name):
                                if x[:len(key)] == key[:len(x)]:
                                    order.wait_emptied(pe, T(name, *x))

                    def products(name, make, cols=P, need=()):
                        for key in streams(name):
                            after(key, *need)
                            b = psum[order.open(pe, T(name, *key))]
                            for i, par in enumerate(key[1:] or range(2)):
                                ins = make(b[:, cols * i:cols * i + cols], key[0], par)
                            end(ins)

                    def four(name, lhs, rhs, cols=P, need=()):
                        products(name, lambda o, hp, par: mm(o, lhs(hp, par), rhs(hp, par), start=True, stop=True), cols, need)

                    def flip(name, B, need):
                        products(name, lambda o, hp, par: tr(o, B[:, hp, par, :], ident), P, (need,))

                    E = EX[n % 2]
                    zr = lambda hp, par: E[:, hp, 0:2, :]
                    four("ab", lambda hp, par: BP[:, hp, par, :], zr, 256)
                    four("dd", lambda hp, par: E[:, hp, 0, :], lambda hp, par: BP[:, hp, par, :])
                    four("ak", lambda hp, par: KP[:, hp, par, :], zr, 256)
                    for hp in range(2):
                        b = psum[order.open(pe, T("tz", hp))]
                        end(tr(b[:, 0:P], E[:, hp, 0, :], ident))
                    for hp in range(2):
                        b = psum[order.open(pe, T("tb", hp))]
                        tr(b[:, 0:P], BT[:, hp], ident)
                        end(tr(b[:, P:2 * P], KD[:, hp], ident))
                    pe.wait_ge(s_tri, 2 * gn + 1)
                    sq = lambda B: (lambda hp, par: B[:, hp, par, :])
                    four("n2", sq(DD), sq(ND), need=("dd",))
                    four("d2", sq(ND), sq(DD))
                    four("akv", lambda hp, par: AK[:, hp, par, 0:P], V, HD, need=("ak",))
                    pe.wait_ge(s_tri, 2 * gn + 2)
                    four("x2", sq(D2), sq(XA), need=("d2",))
                    four("n4", sq(D2), sq(N2), need=("n2",))
                    four("d4", sq(N2), sq(D2))
                    four("x4", sq(DD), sq(XB), need=("d4", "x2"))
                    four("d8", sq(ND), sq(DD), need=("n4",))
                    four("x8", sq(D2), sq(XA), need=("d8", "x4"))
                    flip("x8t", XB, "x8")
                    four("g1", sq(O32), sq(N2), need=("x8t",))
                    four("y1", sq(ND), sq(XB), need=("g1",))
                    flip("y1t", XA, "y1")
                    four("g2", sq(O64), sq(N2), need=("y1t",))
                    four("y2", sq(ND), sq(XA), need=("g2",))
                    four("wp", sq(XB), sq(RR), need=("y2", "akv", "tz"))
                    for hp in range(2):
                        after((hp,), "wp", "ab")
                        b = psum[order.open(pe, T("rh", hp))]
                        for par in range(2):
                            ins = mm(b[HD * par:HD * par + HD, 0:P], WP[:, hp, par, 0:HD], AB[:, hp, par, P:2 * P],
                                     start=True, stop=True)
                        end(ins)
                    for hp in range(2):
                        after((hp,), "tb")
                        b = psum[order.open(pe, T("mt", hp))]
                        for par in range(2):
                            ins = mm(b[HD * par:HD * par + HD, 0:P], WP[:, hp, par, 0:HD],
                                     BC[:, hp, :, HD * par:HD * par + HD], start=True, stop=True)
                        end(ins)
                    for s in range(2):
                        c = s if d == 0 else 1 - s
                        if s == 0 and kind == "c":
                            pe.wait_ge(s_st0, 2 * l + d + 1)
                        elif s == 0 and i == 0:
                            order.wait_emptied(pe, ("si", l, d))
                        for hp in range(2):
                            if s == 1:
                                after((hp,), "s0")
                            else:
                                after((hp,), "mt")
                                if i > 0:
                                    order.wait_emptied(pe, ("s1", l, STEPS[n - 1], hp))
                            b = psum[order.open(pe, T(f"s{s}", hp))]
                            mm(b[:, 0:P], BM[:, hp, c, :], ST[:, hp, ver(s), :], start=True, stop=False, skip_group_check=True)
                            for par in range(2):
                                o = b[HD * par:HD * par + HD, HD * par:HD * par + HD]
                                cols = slice(HD * par, HD * par + HD)
                                mm(o, BC[:, hp, c, cols], WP[:, hp, par, HD:P], start=False, stop=False, skip_group_check=True)
                                ins = mm(o, KC[:, hp, c, cols], V(hp, par), start=False, stop=(par == 1), skip_group_check=True)
                            end(ins)
                    for hp in range(2):
                        after((hp,), "rh")
                        b = psum[order.open(pe, T("yy", hp))]
                        for s in range(2):
                            c = s if d == 0 else 1 - s
                            mm(b[:, CH * c:CH * c + CH], ST[:, hp, ver(s), :], RH[:, hp, CH * c:CH * c + CH],
                               start=(s == 0), stop=False, skip_group_check=True)
                        for par in range(2):
                            o = b[HD * par:HD * par + HD, 0:P]
                            mm(o, WP[:, hp, par, HD:P], AB[:, hp, par, P:2 * P], start=False, stop=False, skip_group_check=True)
                            ins = mm(o, V(hp, par), AK[:, hp, par, P:2 * P], start=False, stop=(par == 1), skip_group_check=True)
                        end(ins)

                    if kind == "c":
                        for hp in range(2):
                            after((hp,), "s1")
                        b = psum[order.open(pe, ("so", l, d))]
                        for hp in range(2):
                            ins = tr(b[:, P * hp:P * hp + P], ST[:, hp, ver(2), :], ident)
                        end(ins)

                for name in ("mu", "var"):
                    if name == "mu":
                        for hp in range(2):
                            order.wait_emptied(pe, ("yy", l, STEPS[-1], hp))
                    else:
                        pe.wait_ge(s_gsq, l + 1)
                    src = yT if name == "mu" else tmp
                    for ct in range(2):
                        for h in range(2):
                            b = psum[order.open(pe, (name, l, ct, h))]
                            end(mm(b[:, 0:HALF], blk, src[:, ct, HALF * h:HALF * (h + 1)], start=True, stop=True))
                pe.wait_ge(s_gup_in, 16 * 5 * (l + 1))
                for ct in range(2):
                    for h in range(2):
                        b = psum[order.open(pe, ("gup", l, ct, h))]
                        end(mm(b[:, 0:HALF], g_up[0:64, P * ct:P * ct + P], gdT[0:64, HALF * h:HALF * (h + 1)],
                               start=True, stop=True))
                pe.wait_ge(s_conv, l + 1)
                for j in range(NT):
                    order.wait_emptied(pe, ("ot", l, j))
                order.wait_emptied(pe, ("f2c", l, 0))
                for ct in range(2):
                    order.wait_emptied(pe, ("f2", l, ct))
                early = [(t, h) for t in range(2) for h in range(2)]
                banks = {}

                def project(g, i, ks):
                    t, h = g
                    w = view(ring, item(("wout", l, i)), KT, 512)
                    for k in ks:
                        ins = mm(banks[g][:, 0:HALF], w[:, k, P * t:P * t + P], mixT[:, k, HALF * h:HALF * (h + 1)],
                                 start=(k == 0), stop=(k == 5), skip_group_check=True)
                    return ins

                for i in range(2):
                    wait_item(pe, ("wout", l, i))
                    if i == 0:
                        for g in early:
                            banks[g] = psum[order.open(pe, ("out", l, g[0], g[1]))]
                            project(g, i, (0, 1, 2, 3, 6, 7))
                        for ct in range(2):
                            for h in range(2):
                                order.wait_emptied(pe, ("gup", l, ct, h))
                    for t in range(4):
                        for h in range(2):
                            g = (t, h)
                            if i == 0 and g in early:
                                end(project(g, i, (4, 5)))
                            else:
                                banks[g] = psum[order.open(pe, ("out", l, 4 * i + t, h))]
                                end(project(g, i, (0, 1, 2, 3, 6, 7, 4, 5)))
                sum_squares("ss2", l, 2 * l + 2)
                if l == 1:
                    pe.wait_ge(s_h, KT * (2 * l + 2))
                    b = psum[order.open(pe, ("router", l))]
                    for j in range(NT):
                        for k in range(KT):
                            ins = mm(b[:, NE * j:NE * j + NE], hT[:, k, P * j:P * j + P], router_w[:, k, :],
                                     start=(k == 0), stop=(k == KT - 1))
                    end(ins)
                    def token_major(tiles):
                        for j, q in tiles:
                            b = psum[order.open(pe, ("ht", j, q))]
                            for k in range(4):
                                ins = tr(b[:, P * k:P * k + P], hT[:, 4 * q + k, P * j:P * j + P], ident)
                            end(ins)

                    token_major(HT_EARLY)
                    pe.wait_ge(s_rmax, 1)
                    b = psum[order.open(pe, ("pos", l))]
                    for j in range(NT + 1):
                        for i in range(min(j + 1, NT)):
                            ins = mm(b[:, NE * j:NE * j + NE], cst("upper", P) if i == j else ones, rt_first[:, i, :],
                                     start=(i == 0), stop=(i == min(j, NT - 1)))
                    end(ins)
                    token_major(HT_LATE)
                    for j in range(NT):
                        for q in range(2):
                            order.wait_emptied(pe, ("ht", j, q))
                for h in range(2):
                    order.wait_emptied(pe, ("ss2", l, h))
                if l == 0:
                    dense()
                else:
                    experts()
                    pe.wait_ge(s_moe_done, 1)
            for j in range(NT):
                for q in range(2):
                    b = psum[order.open(pe, ("y", j, q))]
                    for k in range(4):
                        ins = tr(b[:, P * k:P * k + P], xT[:, 4 * q + k, P * j:P * j + P], ident)
                    end(ins)

        pc = lambda name, i: par[:, ROW[name] + i:ROW[name] + i + 1]
        def chunk_item(n):
            p, kind, i = chunks[n]
            return (kind, 0, p, i // 2)

        def dense_chunk(n):
            p, kind, i = chunks[n]
            base = item(chunk_item(n))
            if kind == "up":
                dims, src = (2, KT, P), view(ring, base, 2, KT, 256)[:, :, :, P * (i % 2):P * (i % 2) + P]
            else:
                nf = DENSE_PARTS[p][1]
                dims, src = (nf, 256), view(ring, base, nf, 512)[:, :, 256 * (i % 2):256 * (i % 2) + 256]
            return [view(t, (n % 2) * CHUNK, *dims) for t in (w_hi, w_lo)], src

        def wait_chunk_used(eng, n):
            if n < 2:
                return
            p, kind, i = chunks[n - 2]
            order.wait_filled(eng, ("du", p, i, 1, 1) if kind == "up" else ("dn", p, i, 1, 1))

        def pair_unit(u):
            n, half = divmod(u, 2)
            c = n % EXP_CHUNKS
            base = ((n // 2 + len(items)) % 2) * SLOT
            if c < EXP_F:
                dims, src = (KT, P), view(ring, base, 2, KT, 256)[:, half, :, P * (c % 2):P * (c % 2) + P]
            else:
                f = 4 * (c % 2) + 2 * half
                dims, src = (2, 512), view(ring, base, EXP_F, 512)[:, f:f + 2, :]
            return [view(t, (u % 4) * UNIT, *dims) for t in (w_hi, w_lo)], src

        def wait_unit_used(eng, u, it):
            back = 1 if u < 4 else 0
            k, x = divmod((u - 4) % (2 * EXP_UNITS), EXP_UNITS)
            if x < 2 * EXP_F and x % 2 == 1:
                order2.wait_filled(eng, ("up", k, x // 2), it, back)
            elif x >= 2 * EXP_F and x % 4 == 3:
                order2.wait_filled(eng, ("dw", k, (x - 2 * EXP_F) // 4, 1), it, back)
            else:
                before = x // 2 if x < 2 * EXP_F else EXP_F + (x - 2 * EXP_F) - (x - 2 * EXP_F) // 4
                eng.wait_ge(s_used2, (it + 1 - back) * 2 * USED_SIGNALS + k * USED_SIGNALS + before + 1)

        def pair_splits(c):
            return [u for u in ((0, 1, 2) if c < 0 else (2 * c + 3, 2 * c + 4)) if u < EXP_UNITS]

        IN_DEST = {"r": rT, "k": kT_, "v": vT, "bx": bxT, "bb": bbT, "bc": bcT, "f": fT}

        @block.scalar
        def _(act):
            chain = Chain(act, s_ca)
            ac = nc.scalar.activation

            def end(ins):
                ins.then_inc(emptied["A"], 1)

            def take(name):
                order.wait_filled(act, name)
                return psum[order.bank(name)]

            def norm(l, which, then=None):
                if l == 0 and which == 1:
                    for j in range(NT):
                        for q in range(2):
                            order.wait_emptied(act, ("x", j, q))
                elif which == 1:
                    order.wait_emptied(act, ("dn", len(DENSE_PARTS) - 1, 3, 1, 1))
                for k in range(KT):
                    if which == 2:
                        order.wait_emptied(act, ("out", l, k, 1))
                    ac(hT[:, k, :], xT[:, k, :], ACT.Square).then_inc(s_sq, 1)
                for h in range(2):
                    b = take((f"ss{which}", l, h))
                    end(ac(rs[:, HALF * h:HALF * (h + 1)], b[:, 0:HALF], ACT.Sqrt, scale=1.0 / D, bias=cst("eps", 1)))
                nth = 2 * l + which - 1
                for k in range(KT):
                    act.wait_ge(s_hmul, KT * nth + k + 1)
                    for vec, lo, hi in SEGS:
                        ins = ac(hT[:, k, lo:hi], hT[:, k, lo:hi], ACT.Identity,
                                 bias=mod[:, 24 * (which - 1) + k, vec:vec + 1])
                    ins.then_inc(s_h, 1)
                    if then:
                        then(k)

            def in_evac(l, tiles):
                for name, _, _ in tiles:
                    for h in range(2):
                        key = ("in", l, name, h)
                        if order.by[order.at[key]] != "A":
                            continue
                        b = take(key)
                        cols = slice(HALF * h, HALF * (h + 1))
                        if name[0] == "wa":
                            chain.did(ac(waT[0:64, cols], b[0:64, 0:HALF], ACT.Tanh))
                            end(ac(waT[64:P, cols], b[64:P, 0:HALF], ACT.Copy))
                        elif name[0] == "gd":
                            end(ac(gdT[0:64, cols], b[0:64, 0:HALF], ACT.Sigmoid))
                        else:
                            end(ac(IN_DEST[name[0]][:, name[1], cols], b[:, 0:HALF], ACT.Copy))

            def dense_split(n):
                wait_item(act, chunk_item(n))
                wait_chunk_used(act, n)
                dst, src = dense_chunk(n)
                ac(dst[0], src, ACT.Copy).then_inc(s_hi, 1)

            for l in range(DEPTH):
                if l == 0:
                    order.wait_emptied(act, ("params", l))
                    chain.did(ac(silu_c[:, :, 0], par[:, ROW["c_ctx"]:ROW["c_ctx"] + KT], ACT.Silu))
                    ac(silu_c[:, :, 1], par[:, ROW["c"]:ROW["c"] + KT], ACT.Silu).then_inc(s_silc, 1)
                    for j in range(NT):
                        b = take(("x", j, 0))
                        end(ac(xT[:, 0:4, P * j:P * j + P], b[:, :].rearrange("p (k t) -> p k t", k=4), ACT.Copy))
                    act.wait_ge(s_tables, 16)
                norm(l, 1)
                in_evac(l, RW_TILES)
                for j in range(0, NT, 2):
                    b = take(("qkv", l, j))
                    end(ac(qkv[:, j, :], b[:, :], ACT.Copy))
                act.wait_ge(s_kkr, l + 1)
                for ct in range(2):
                    ins = ac(tmp[:, ct, :], kkT[:, ct, :], ACT.Square)
                ins.then_inc(s_kq, 1)
                for j in range(NT):
                    order.wait_emptied(act, ("qkv", l, j))
                    ins = ac(qk_sq[:, j, :], qkv[:, j, 0:384], ACT.Square)
                ins.then_inc(s_qsq, 1)
                in_evac(l, CF_TILES[:2])
                act.wait_ge(s_qss, l + 1)
                ac(qk_ss, qk_ss, ACT.Sqrt, scale=1.0 / HD, bias=cst("eps", 1)).then_inc(s_qrt, 1)
                in_evac(l, CF_TILES[2:])
                for j in range(NT):
                    b = take(("vt", l, j))
                    end(ac(v_tok[:, j].rearrange("p h d -> p (h d)"), b[:, 0:256], ACT.Copy))
                for ct in range(2):
                    for h in range(2):
                        b = take(("kks", l, ct, h))
                        end(ac(tmp[:, ct, HALF * h:HALF * (h + 1)], b[:, 0:HALF], ACT.Sqrt))
                act.wait_ge(s_conv, l + 1)
                for kind in range(2):
                    for d in range(2):
                        for ct in range(2):
                            for h in range(2):
                                b = take(("up", l, kind, d, ct, h))
                                row = ROW["w0" if kind == 0 else "a0"] + 2 * d + ct
                                dst = (lw if kind == 0 else aT)[:, d, ct, HALF * h:HALF * (h + 1)]
                                end(ac(dst, b[:, 0:HALF], ACT.Sigmoid, bias=par[:, row:row + 1]))
                def decays(n):
                    gn = l * len(STEPS) + n
                    E = EX[n % 2]
                    act.wait_ge(s_sum, gn + 1)
                    chain.did(ac(E[:, :, 2, :], E[:, :, 1, :], ACT.Exp, scale=-1.0))
                    chain.settle()
                    ac(E[:, :, 0:2, :], E[:, :, 0:2, :], ACT.Exp).then_inc(s_ex, 1)

                for j in range(NT):
                    pos = [p for p, _ in key_blocks(j)]
                    lo, hi = P * pos[0], P * (pos[-1] + 1)
                    act.wait_ge(s_max, l * NT + j + 1)
                    A = att[:, j % 2]
                    for h in range(NQ):
                        chain.did(ac(sc[:, h, lo:hi], sc[:, h, lo:hi], ACT.Exp, scale=HD ** -0.5,
                                     bias=A[:, 4 + h:5 + h], accum_out=A[:, 8 + h:9 + h]))
                    chain.settle()
                    ac(A[:, 12:16], A[:, 12:16], ACT.Exp).then_inc(s_exp, 1)
                    if j == 1:
                        decays(0)
                    for name, x in fourier_groups(j):
                        if name == "f1" and x % 2 == 0:
                            b = take(("f1", l, x))
                            end(ac(v1[x].rearrange("p a b -> p (a b)"), b[:, :], ACT.Copy))
                        elif name == "f2c":
                            b = take(("f2c", l, 0))
                            end(ac(mixT[:, 6:8, 0:CTX], b[:, 0:256].rearrange("p (t n) -> p t n", t=2), ACT.Copy))
                        elif name == "f2" and x == 0:
                            b = take(("f2", l, 0))
                            end(ac(mixT[:, 6, CTX:TOK], b[:, :], ACT.Copy))
                    for h in (0, 2):
                        b = take(("pt", l, j, h))
                        end(ac(pT[h].rearrange("p a b -> p (a b)")[:, lo:hi], b[:, lo:hi], ACT.Copy))
                    b = take(("ot", l, j))
                    end(ac(mixT[:, 0:2, P * j:P * j + P], b[:, 0:256].rearrange("p (t n) -> p t n", t=2), ACT.Copy))
                for n, step in enumerate(STEPS):
                    T = lambda name, *key: (name, l, step, *key)

                    def copies(name, dst):
                        for key in streams(name):
                            b = take(T(name, *key))
                            if len(key) == 2:
                                end(ac(dst[:, key[0], key[1]], b[:, 0:P], ACT.Copy))
                            else:
                                end(ac(dst[:, key[0]], b[:, 0:256].rearrange("p (a b) -> p a b", a=2), ACT.Copy))

                    for hp in range(2):
                        b = take(T("tz", hp))
                        end(ac(RR[:, hp, :, 0:HD], b[:, 0:P].rearrange("p (a b) -> p a b", a=2), ACT.Copy))
                    if n == 0:
                        act.wait_ge(s_zero2, l + 1)
                    for hp in range(2):
                        b = take(T("tb", hp))
                        for c in range(2):
                            rows = slice(CH * c, CH * c + CH)
                            chain.did(ac(BC[rows, hp, c, :], b[rows, 0:P], ACT.Copy, scale=-1.0))
                            ins = ac(KC[rows, hp, c, :], b[rows, P:2 * P], ACT.Copy)
                            if c == 0:
                                chain.did(ins)
                            else:
                                end(ins)
                    copies("n2", N2)
                    copies("d2", D2)
                    copies("n4", ND)
                    copies("d4", DD)
                    if n + 1 < len(STEPS):
                        decays(n + 1)
                    copies("d8", D2)
                    copies("x8t", N2)
                    copies("g1", ND)
                    copies("y1t", N2)
                    copies("g2", ND)
                    copies("wp", WP)

                act.wait_ge(s_gn, l + 1)
                act.wait_ge(s_state_out, 16 * 8 * (l + 1))
                for ct in range(2):
                    ins = ac(tmp[:, ct, :], yT[:, ct, :], ACT.Square)
                ins.then_inc(s_gsq, 1)
                for ct in range(2):
                    for h in range(2):
                        b = take(("var", l, ct, h))
                        end(ac(tmp[:, ct, HALF * h:HALF * (h + 1)], b[:, 0:HALF], ACT.Sqrt, scale=1.0 / HD,
                               bias=cst("eps", 1, 1)))
                def high(k):
                    act.wait_ge(s_h, KT + k + 1)
                    ac(hc[0][:, k, :], hT[:, k, :], ACT.Copy).then_inc(s_hhi, 1)

                if l == 0:
                    dense_split(0)
                    norm(l, 2, high)
                    for n, (p, kind, i) in enumerate(chunks):
                        if n + 1 < len(chunks):
                            dense_split(n + 1)
                        if kind == "up":
                            u = DENSE_PARTS[p][0] + i
                            if u >= 2:
                                act.wait_ge(s_glo, u - 1)
                            for h in range(2):
                                b = take(("du", p, i, 0, h))
                                end(ac(sil[:, u % 2, HALF * h:HALF * (h + 1)], b[:, 0:HALF], ACT.Silu))
                            if i == 0 and p > 0:
                                order.wait_filled(act, ("dn", p - 1, 3, 1, 1))
                            order.wait_emptied(act, ("du", p, i, 1, 1))
                            ac(dg[0][:, i, :], sil[:, u % 2, :], ACT.Copy).then_inc(s_ghi, 1)
                else:
                    norm(l, 2)
                    def high_parts(tiles):
                        for j, q in tiles:
                            b = take(("ht", j, q))
                            ac(ht[0][:, j, 512 * q:512 * (q + 1)], b[:, :], ACT.Copy).then_inc(s_hhi, 1)

                    high_parts(HT_EARLY)
                    act.wait_ge(s_rmax, 1)
                    ac(rt_l, rt_l, ACT.Exp).then_inc(s_rexp, 1)
                    high_parts(HT_LATE)
                    o = order2
                    act.sem_inc(s_hi2, 2 * EXP_UNITS)
                    act.wait_ge(s_rounds, 1)
                    rounds = act.value_load(rounds_t[0:1, 0:1], min_val=1, max_val=MAX_ROUNDS)
                    with act.Fori(0, rounds) as r:
                        with act.Fori(0, NE // 2) as pair:
                            it = r * (NE // 2) + pair
                            take2 = lambda name: (o.wait_filled(act, name, it), psum[o.bank(name)])[1]

                            def split(u):
                                n = u // 4
                                act.wait_ge(s_ring2[n % 2], it * 32 * (PAIR_ITEMS // 2) + 32 * (n // 2 + 1))
                                wait_unit_used(act, u, it)
                                dst, src = pair_unit(u)
                                ac(dst[0], src, ACT.Copy).then_inc(s_hi2, 1)

                            for k in range(2):
                                for u in pair_splits(-1):
                                    split(EXP_UNITS * k + u)
                                for b4 in range(4):
                                    b = take2(("ga", k, b4))
                                    ac(xg[0][:, 2 * b4:2 * b4 + 2, :], b[:, 0:2 * CAP].rearrange("p (t n) -> p t n", t=2),
                                       ACT.Copy).then_inc(s_xhi, 1)
                                for c in range(EXP_CHUNKS):
                                    for u in pair_splits(c):
                                        split(EXP_UNITS * k + u)
                                    if c < EXP_F:
                                        u = (2 * it + k) * EXP_F + c
                                        b = take2(("up", k, c))
                                        if c >= 2:
                                            act.wait_ge(s_glo2, u - 1)
                                        ac(e_sil[:, c % 2, :], b[:, 0:CAP], ACT.Silu).then_inc(s_sil2, 1)
                                        o.wait_emptied(act, ("up", k, c), it)
                                        ac(eg[0][:, c, 0:CAP], e_sil[:, c % 2, :], ACT.Copy).then_inc(s_ghi2, 1)
                                    elif (c - EXP_F) % 2 == 1:
                                        i = (c - EXP_F) // 2
                                        act.wait_ge(s_gs, 2 * it + k + 1)
                                        for q in range(2):
                                            b = take2(("dw", k, i, q))
                                            ac(yg[0][:, q, 512 * i:512 * (i + 1)], b[:, :], ACT.Copy,
                                               scale=gslot[:, k, q:q + 1]).then_inc(s_yhi, 1)
            for j in range(NT):
                b = take(("y", j, 0))
                end(ac(x_tok[:, j, 0:512], b[:, :], ACT.Copy))

        @block.vector
        def _(ve):
            chain = Chain(ve, s_cv)
            v = nc.vector

            def end(ins):
                ins.then_inc(emptied["V"], 1)

            def take(name):
                order.wait_filled(ve, name)
                return psum[order.bank(name)]

            def norm(l, which, then=None):
                t = 24 * (which - 1) + 8
                w = par[:, ROW[f"norm{which}"]:ROW[f"norm{which}"] + KT]
                chain.did(v.scalar_tensor_tensor(out=amul, in0=mod[:, t:t + KT, :], scalar=1.0,
                                                 in1=w[:, :, None].broadcast_to([P, KT, 2]), op0=ALU.add, op1=ALU.mult))
                for h in range(2):
                    order.wait_emptied(ve, (f"ss{which}", l, h))
                    chain.did(v.reciprocal(rs[:, HALF * h:HALF * (h + 1)], rs[:, HALF * h:HALF * (h + 1)]))
                chain.settle()
                for k in range(KT):
                    for vec, lo, hi in SEGS:
                        ins = v.scalar_tensor_tensor(out=hT[:, k, lo:hi], in0=xT[:, k, lo:hi], scalar=amul[:, k, vec:vec + 1],
                                                     in1=rs[:, lo:hi], op0=ALU.mult, op1=ALU.mult)
                        if vec == 0:
                            chain.did(ins)
                    ins.then_inc(s_hmul, 1)
                    if then and k >= 2:
                        then(k - 2)
                if then:
                    then(KT - 2)
                    then(KT - 1)

            def mod_sums(l, n):
                if n < SUB_FIRST:
                    wait_item(ve, ("mod", l, n // 2))
                    w = view(ring, item(("mod", l, n // 2)), KT, 512)[:, :, 256 * (n % 2):256 * (n % 2) + 256]
                else:
                    m = n - SUB_FIRST + (SUBS - SUB_FIRST) * l
                    ve.wait_ge(s_mod_in[m % 2], 16 * (m // 2 + 1))
                    w = mod_w[m % 2]
                sums = acc[mod_buffer(l, n)]
                for k in range(KT):
                    for vec in range(2):
                        if k == 0:
                            chain.did(v.tensor_scalar(sums[:, vec], w[:, k], silu_c[:, k, vec:vec + 1], None, ALU.mult))
                            continue
                        chain.settle(1)
                        ins = v.scalar_tensor_tensor(out=sums[:, vec], in0=w[:, k], scalar=silu_c[:, k, vec:vec + 1],
                                                     in1=sums[:, vec], op0=ALU.mult, op1=ALU.add)
                        if (k, vec) != (KT - 1, 1):
                            chain.did(ins)
                ins.then_inc(s_macc, 1)

            def mod_take(l, n):
                b = take(("ms", l, n))
                dst, src = mod[:, 2 * n:2 * n + 2, :], b[:, 0:4].rearrange("p (t v) -> p t v", v=2)
                if n < SUB_FIRST:
                    end(v.tensor_copy(dst, src))
                else:
                    end(v.tensor_tensor(dst, src, par[:, 2 * n:2 * n + 2][:, :, None].broadcast_to([P, 2, 2]), ALU.add))

            def in_evac(l, tiles, sub, then=None):
                for n, (name, _, _) in enumerate(tiles):
                    for h in range(2):
                        key = ("in", l, name, h)
                        if order.by[order.at[key]] != "V":
                            continue
                        b = take(key)
                        end(v.tensor_copy(IN_DEST[name[0]][:, name[1], HALF * h:HALF * (h + 1)], b[:, 0:HALF]))
                    if n > 0:
                        mod_take(l, sub + n - 1)
                    if sub + n < SUBS:
                        mod_sums(l, sub + n)
                    if then:
                        then(n)

            def residual(b, h, dt, gate, drain=False):
                parts = ((0, 0, CTX), (1, CTX, HALF)) if h == 0 else ((1, HALF, TOK),)
                for vec, lo, hi in parts:
                    off = HALF * h
                    ins = v.scalar_tensor_tensor(out=xT[:, dt, lo:hi], in0=b[:, lo - off:hi - off],
                                                 scalar=mod[:, gate + dt, vec:vec + 1], in1=xT[:, dt, lo:hi],
                                                 op0=ALU.mult, op1=ALU.add)
                    if hi < TOK and vec == 0 and not drain:
                        chain.did(ins)
                return ins

            def dense_split(n):
                ve.wait_ge(s_hi, n + 1)
                dst, src = dense_chunk(n)
                v.tensor_tensor(dst[1], src, f32(dst[0]), ALU.subtract).then_inc(s_lo, 1)

            def experts():
                o = order2
                ve.sem_inc(o.emptied["V"], len(o.by))
                ve.sem_inc(s_lo2, 2 * EXP_UNITS)
                for x in eg:
                    v.tensor_scalar(x[:, :, CAP:SLOTS], ones[:, 0:SLOTS - CAP][:, None, :].broadcast_to([P, EXP_F, SLOTS - CAP]),
                                    0.0, None, ALU.mult)
                ve.wait_ge(s_rounds, 1)
                rounds = ve.value_load(rounds_t[0:1, 0:1], min_val=1, max_val=MAX_ROUNDS)
                with ve.Fori(0, rounds) as r:
                    with ve.Fori(0, NE // 2) as pair:
                        it = r * (NE // 2) + pair

                        def end2(ins):
                            ins.then_inc(o.emptied["V"], 1)

                        def take2(name):
                            o.wait_filled(ve, name, it)
                            return psum[o.bank(name)]

                        def settle():
                            ve.drain()

                        def split(u):
                            ve.wait_ge(s_hi2, (it + 1) * 2 * EXP_UNITS + u + 1)
                            dst, src = pair_unit(u)
                            v.tensor_tensor(dst[1], src, f32(dst[0]), ALU.subtract).then_inc(s_lo2, 1)

                        def select(k):
                            e = 2 * pair + k
                            settle()
                            if k == 1:
                                o.wait_filled(ve, ("ga", 0, 3), it)
                            v.tensor_copy(cur_pos[:, k, :], posm[:, :, bass.ds(e, 1)].rearrange("p j e -> p (j e)"))
                            v.tensor_copy(cur_gate[:, k, :], gates[:, :, bass.ds(e, 1)].rearrange("p j e -> p (j e)"))
                            settle()
                            for j in range(NT):
                                ins = v.tensor_scalar(sel[:, j, :], cst("slots", CAP), cur_pos[:, k, j:j + 1], None, ALU.is_equal)
                            ins.then_inc(s_sel, 1)

                        def spread(k):
                            for b2 in range(2):
                                b = take2(("bc", k, b2))
                                lo, n = ((0, 384), (384, 256))[b2]
                                for q in range(2):
                                    ins = v.tensor_scalar(selT[:, q, lo:lo + n], b[:, 0:n], cst("slot", 1, q), None, ALU.is_equal)
                                end2(ins)
                            settle()
                            for b2 in range(2):
                                b = take2(("bc", k, 2 + b2))
                                lo, n = ((0, 384), (384, 256))[b2]
                                for q in range(2):
                                    v.tensor_tensor(junk[:, q, 0:n], b[:, 0:n], f32(selT[:, q, lo:lo + n]), ALU.mult)
                                settle()
                                for q in range(2):
                                    ins = v.tensor_reduce(out=gs_part[:, k, q, b2:b2 + 1], in_=junk[:, q, 0:n], axis=AXX, op=ALU.add)
                                end2(ins)
                                settle()
                            v.tensor_tensor(gslot[:, k, :], gs_part[:, k, :, 0], gs_part[:, k, :, 1], ALU.add).then_inc(s_gs, 1)
                            ve.wait_ge(s_gs, 2 * it + k + 1)

                        def gathered(k):
                            for b4 in range(4):
                                b = take2(("ga", k, b4))
                                ve.wait_ge(s_xhi, 4 * (2 * it + k) + b4 + 1)
                                end2(v.tensor_tensor(xg[1][:, 2 * b4:2 * b4 + 2, :], b[:, 0:2 * CAP].rearrange("p (t n) -> p t n", t=2),
                                                     f32(xg[0][:, 2 * b4:2 * b4 + 2, :]), ALU.subtract))

                        def scattered(k):
                            for dt in range(KT):
                                for h in range(2):
                                    end2(residual(take2(("sc", k, dt, h)), h, dt, 40, drain=True))

                        select(0)
                        for k in range(2):
                            if k == 0:
                                spread(0)
                                for u in pair_splits(-1):
                                    split(u)
                                gathered(0)
                            for c in range(EXP_CHUNKS):
                                for u in pair_splits(c):
                                    split(EXP_UNITS * k + u)
                                if c < EXP_F:
                                    u = (2 * it + k) * EXP_F + c
                                    b = take2(("up", k, c))
                                    ve.wait_ge(s_sil2, u + 1)
                                    end2(v.tensor_tensor(e_sil[:, c % 2, :], b[:, CAP:2 * CAP], e_sil[:, c % 2, :], ALU.mult))
                                    ve.wait_ge(s_ghi2, u + 1)
                                    v.tensor_tensor(eg[1][:, c, 0:CAP], e_sil[:, c % 2, :], f32(eg[0][:, c, 0:CAP]),
                                                    ALU.subtract).then_inc(s_glo2, 1)
                                elif (c - EXP_F) % 2 == 1:
                                    i = (c - EXP_F) // 2
                                    cols = slice(512 * i, 512 * (i + 1))
                                    for q in range(2):
                                        b = take2(("dw", k, i, q))
                                        ve.wait_ge(s_yhi, 4 * (2 * it + k) + 2 * i + q + 1)
                                        end2(v.scalar_tensor_tensor(out=yg[1][:, q, cols], in0=b[:, :], scalar=gslot[:, k, q:q + 1],
                                                                    in1=f32(yg[0][:, q, cols]), op0=ALU.mult, op1=ALU.subtract))
                                if k == 0 and c == EXP_F:
                                    select(1)
                            if k == 0:
                                for u in pair_splits(-1):
                                    split(EXP_UNITS + u)
                                gathered(1)
                            scattered(k)
                            if k == 0:
                                spread(1)
                    ve.drain()
                    v.tensor_scalar(posm, posm, -float(CAP), None, ALU.add)
                    ve.drain()
                ve.sem_inc(s_moe_done, 1)

            for l in range(DEPTH):
                b = take(("params", l))
                end(v.tensor_copy(par, b[:, 0:NROWS]))
                order.wait_emptied(ve, ("params", l))
                if l == 0:
                    ve.wait_ge(s_silc, 1)
                    for i in range(0, SUB_FIRST, 4):
                        mod_sums(0, i)
                        mod_sums(0, i + 1)
                        for n in FIRST_SUBS[i:i + 4]:
                            mod_take(0, n)
                        if i == 0:
                            for j in range(NT):
                                b = take(("x", j, 1))
                                end(v.tensor_copy(xT[:, 4:8, P * j:P * j + P], b[:, :].rearrange("p (k t) -> p k t", k=4)))
                    ve.wait_ge(s_tables, 16)
                m = 2 * SUB_FIRST
                order.wait_emptied(ve, ("ms", l, FIRST_SUBS[-1] if l == 0 else SUB_FIRST - 1))
                chain.did(v.tensor_tensor(mod[:, 0:m, :], mod[:, 0:m, :], par[:, 0:m][:, :, None].broadcast_to([P, m, 2]),
                                          ALU.add))
                chain.settle()
                norm(l, 1)
                in_evac(l, RW_TILES, SUB_FIRST)
                for ct in range(2):
                    order.wait_emptied(ve, ("in", l, ("k", ct), 0))
                    order.wait_emptied(ve, ("in", l, ("k", ct), 1))
                    chain.did(v.tensor_scalar(omka[:, ct:ct + 1], pc("k_a", ct), -1.0, 1.0, ALU.mult, ALU.add))
                    ins = v.tensor_scalar(kkT[:, ct, :], kT_[:, ct, :], pc("k_k", ct), None, ALU.mult)
                ins.then_inc(s_kkr, 1)
                mod_take(l, SUB_FIRST + 7)
                mod_sums(l, SUB_FIRST + 8)
                for j in range(1, NT, 2):
                    b = take(("qkv", l, j))
                    end(v.tensor_copy(qkv[:, j, :], b[:, :]))
                def qk_norm(n):
                    if n == 1:
                        for jj in range(NT):
                            order.wait_emptied(ve, ("qkv", l, jj))
                        ve.wait_ge(s_qsq, l + 1)
                        v.tensor_reduce(out=qk_ss, in_=qk_sq.rearrange("p j (h d) -> p (j h) d", d=HD), axis=AXX,
                                        op=ALU.add).then_inc(s_qss, 1)
                    elif n == 2:
                        ve.wait_ge(s_qrt, l + 1)
                        ve.wait_ge(s_gup_in, 16 * 5 * (l + 1))
                        chain.did(v.reciprocal(qk_ss, qk_ss))
                        for ct in range(2):
                            for h in range(2):
                                order.wait_emptied(ve, ("in", l, ("r", ct), h))
                            ins = v.scalar_tensor_tensor(out=rk[:, ct, :], in0=rT[:, ct, :], scalar=pc("r_k", ct), in1=kT_[:, ct, :],
                                                         op0=ALU.mult, op1=ALU.mult)
                            if ct == 0:
                                chain.did(ins)
                        ins.then_inc(s_rk, 1)
                    if 3 <= n:
                        j = n - 3
                        q_in = qkv[:, j, 0:384].rearrange("p (h d) -> p h d", d=HD)
                        t = qk_t[:, j % 2]
                        chain.settle()
                        chain.did(v.tensor_tensor(t, q_in, qk_ss[:, 6 * j:6 * j + 6][:, :, None].broadcast_to([P, 6, HD]), ALU.mult))
                        chain.settle()
                        chain.did(v.tensor_tensor(
                            qkv[:, j, 0:256].rearrange("p (g k d) -> p k g d", g=2, k=2),
                            t[:, 0:4, :].rearrange("p (k g) d -> p k g d", k=2),
                            qnw[:, None, None, :].broadcast_to([P, 2, 2, HD]), ALU.mult))
                        v.tensor_tensor(qkv[:, j, 256:384].rearrange("p (k d) -> p k d", k=2), t[:, 4:6, :],
                                        knw[:, None, :].broadcast_to([P, 2, HD]), ALU.mult).then_inc(s_qk, 1)

                mod_take(l, SUB_FIRST + 8)
                in_evac(l, CF_TILES, SUB_FIRST + 9, qk_norm)
                for ct in range(2):
                    for h in range(2):
                        b = take(("bonus", l, ct, h))
                        for c2 in range(2):
                            order.wait_emptied(ve, ("in", l, ("v", ct), c2))
                        cols = slice(HALF * h, HALF * (h + 1))
                        end(v.tensor_tensor(vT[:, ct, cols], b[:, 0:HALF], vT[:, ct, cols], ALU.mult))
                b = take(("ckt", l))
                end(v.tensor_copy(ckT, b[:, 0:P]))
                for j in range(NT):
                    b = take(("qt", l, j))
                    chain.did(v.tensor_copy(qT[:, :, P * j:P * j + P], b[:, 0:256].rearrange("p (t n) -> p t n", t=2)))
                    end(v.tensor_copy(kT[:, P * j:P * j + P], b[:, 256:384]))
                ve.wait_ge(s_cu, l + 1)
                for h in range(2):
                    for ct in range(2):
                        order.wait_emptied(ve, ("in", l, ("bb", ct), h))
                for ct in range(2):
                    for at0, (_, lo, hi) in ((0, SEGS[0]), (2, SEGS[1])):
                        n = hi - lo
                        u = lambda s: conv_u[:, ct, at0 + lo + s:at0 + hi + s]
                        o = mixT[:, 2 + ct, lo:hi]
                        chain.did(v.tensor_scalar(o, u(0), pc("conv", ct), None, ALU.mult))
                        for s in (1, 2):
                            chain.settle()
                            chain.did(v.scalar_tensor_tensor(out=o, in0=u(s), scalar=pc("conv", 2 * s + ct), in1=o,
                                                             op0=ALU.mult, op1=ALU.add))
                        chain.settle()
                        ins = v.tensor_tensor(o, o, bbT[:, ct, lo:hi], ALU.mult)
                        if (ct, lo) != (1, CTX):
                            chain.did(ins)
                        else:
                            ins.then_inc(s_conv, 1)

                def sums(n):
                    _, _, d = STEPS[n]
                    j = step_tile(STEPS[n])
                    E = EX[n % 2]
                    x = lw[:, d, :, P * j:P * j + P]
                    if n >= 2:
                        for hp in range(2):
                            order.wait_emptied(ve, ("rh", l, STEPS[n - 2], hp))
                    for hp in range(2):
                        chain.did(v.tensor_tensor_scan(out=E[:, hp, 1, :], data0=cst("scan", P), data1=x[:, hp, :],
                                                       initial=0.0, op0=ALU.mult, op1=ALU.add))
                    chain.settle()
                    if d == 0:
                        chain.did(v.tensor_tensor(E[:, :, 0, :], E[:, :, 1, :], x, ALU.subtract))
                        chain.settle()
                    else:
                        for c in range(2):
                            tot = E[:, :, 1, CH * c + CH - 1:CH * c + CH].broadcast_to([P, 2, CH])
                            chain.did(v.tensor_tensor(E[:, :, 0, CH * c:CH * c + CH], tot, E[:, :, 1, CH * c:CH * c + CH],
                                                      ALU.subtract))
                        chain.settle()
                        chain.did(v.tensor_tensor(E[:, :, 1, :], E[:, :, 0, :], x, ALU.add))
                        chain.settle()
                    v.tensor_scalar(E[:, :, 0:2, :], E[:, :, 0:2, :], LOG_DECAY, None, ALU.mult).then_inc(s_sum, 1)

                for j in range(NT):
                    pos = [p for p, _ in key_blocks(j)]
                    lo, hi = P * pos[0], P * (pos[-1] + 1)
                    A = att[:, j % 2]
                    for h in range(NQ):
                        b = take(("qk", l, j, h))
                        if j == 0:
                            end(v.tensor_copy(sc[:, h, lo:hi], b[:, lo:hi]))
                        else:
                            end(v.tensor_tensor(sc[:, h, lo:hi], b[:, lo:hi], cst("band", 512)[:, lo:hi], ALU.add))
                    order.wait_emptied(ve, ("qk", l, j, NQ - 1))
                    chain.did(v.tensor_reduce(out=A[:, 0:4], in_=sc[:, :, lo:hi], axis=AXX, op=ALU.max))
                    chain.settle()
                    chain.did(v.scalar_tensor_tensor(out=A[:, 0:4], in0=A[:, 0:4], scalar=HD ** -0.5, in1=sink,
                                                     op0=ALU.mult, op1=ALU.max))
                    chain.settle()
                    chain.did(v.tensor_scalar(A[:, 4:8], A[:, 0:4], -1.0, None, ALU.mult))
                    v.tensor_tensor(A[:, 12:16], sink, A[:, 0:4], ALU.subtract).then_inc(s_max, 1)
                    if j < 4:
                        ct, h = divmod(j, 2)
                        order.wait_emptied(ve, ("kks", l, ct, h))
                        part = tmp[:, ct, HALF * h:HALF * (h + 1)]
                        chain.did(v.tensor_scalar(part, part, 1e-12, None, ALU.max))
                        chain.settle()
                        chain.did(v.reciprocal(part, part))
                    if j == 1:
                        sums(0)
                    if j == 3:
                        chain.settle()
                        v.scalar_tensor_tensor(out=kkT, in0=kkT, scalar=-1.0, in1=tmp, op0=ALU.mult,
                                               op1=ALU.mult).then_inc(s_nkk, 1)
                    for name, x in fourier_groups(j):
                        if name == "f1" and x % 2 == 1:
                            b = take(("f1", l, x))
                            end(v.tensor_copy(v1[x].rearrange("p a b -> p (a b)"), b[:, :]))
                        elif name == "f2" and x == 1:
                            b = take(("f2", l, 1))
                            end(v.tensor_copy(mixT[:, 7, CTX:TOK], b[:, :]))
                    for h in (1, 3):
                        b = take(("pt", l, j, h))
                        end(v.tensor_copy(pT[h].rearrange("p a b -> p (a b)")[:, lo:hi], b[:, lo:hi]))
                    ve.wait_ge(s_exp, l * NT + j + 1)
                    chain.did(v.tensor_tensor(A[:, 16:20], A[:, 8:12], A[:, 12:16], ALU.add))
                    chain.settle()
                    chain.did(v.reciprocal(A[:, 16:20], A[:, 16:20]))
                    chain.settle()
                    b = take(("pv", l, j))
                    end(v.tensor_tensor(o_tok, b[:, 0:256].rearrange("p (h d) -> p h d", h=NQ),
                                        A[:, 16:20][:, :, None].broadcast_to([P, NQ, HD]), ALU.mult))
                ve.wait_ge(s_zero2, l + 1)
                for n, step in enumerate(STEPS):
                    kind, i, d = step
                    j = step_tile(step)
                    gn = l * len(STEPS) + n
                    T = lambda name, *key: (name, l, step, *key)
                    E = EX[n % 2]
                    v0 = 2 * i if kind == "s" else 0
                    if (kind, i) == ("s", 0):
                        b = take(("si", l, d))
                        end(v.tensor_copy(ST[:, :, 0, :], b[:, 0:256].rearrange("p (a b) -> p a b", a=2)))
                    elif kind == "c":
                        if d == 1:
                            order.wait_emptied(ve, ("so", l, 0))
                        v.memset(ST[:, :, 0, :], 0.0).then_inc(s_st0, 1)
                    pair = lambda b: b[:, 0:256].rearrange("p (a b) -> p a b", a=2)
                    for hp in range(2):
                        b = take(T("ab", hp))
                        end(v.scalar_tensor_tensor(out=AB[:, hp], in0=b[:, :].rearrange("p (a b) -> p a b", a=2), scalar=-1.0,
                                                   in1=cst("mzr", 256, 256 * d)[:, None, :].broadcast_to([P, 2, 256]),
                                                   op0=ALU.mult, op1=ALU.mult))
                    for hp in range(2):
                        b = take(T("dd", hp))
                        end(v.scalar_tensor_tensor(out=DD[:, hp], in0=pair(b), scalar=-1.0,
                                                   in1=cst("m16", P, P * (1 - d))[:, None, :].broadcast_to([P, 2, P]),
                                                   op0=ALU.mult, op1=ALU.mult))
                    for hp in range(2):
                        b = take(T("ak", hp))
                        end(v.tensor_tensor(AK[:, hp], b[:, :].rearrange("p (a b) -> p a b", a=2),
                                            cst("mzr", 256, 256 * d)[:, None, :].broadcast_to([P, 2, 256]), ALU.mult))
                    for hp in range(2):
                        b = take(T("akv", hp))
                        end(v.tensor_copy(RR[:, hp, :, HD:P], b[:, 0:P].rearrange("p (a b) -> p a b", a=2)))

                    def plus(name, dst, src, made=None):
                        for key in streams(name):
                            for x in streams(made) if made else ():
                                if x[:len(key)] == key[:len(x)]:
                                    order.wait_emptied(ve, T(made, *x))
                            b = take(T(name, *key))
                            if len(key) == 2:
                                hp, par_ = key
                                end(v.tensor_tensor(dst[:, hp, par_], b[:, 0:P], src[:, hp, par_], ALU.add))
                            else:
                                end(v.tensor_tensor(dst[:, key[0]], pair(b), src[:, key[0]], ALU.add))

                    plus("x2", XB, XA)
                    if n + 1 < len(STEPS):
                        sums(n + 1)
                    plus("x4", XA, XB, "x2")
                    plus("x8", XB, XA, "x4")
                    plus("y1", XA, XB, "x8")
                    plus("y2", XB, XA, "y1")
                    for hp in range(2):
                        b = take(T("rh", hp))
                        end(v.tensor_tensor(RH[:, hp], b[:, 0:P], E[:, hp, 1, :], ALU.add))
                    for hp in range(2):
                        b = take(T("mt", hp))
                        for par_ in range(2):
                            r = slice(HD * par_, HD * par_ + HD)
                            ins = v.tensor_tensor(BM[r, hp, :, r], b[r, 0:P].rearrange("p (c k) -> p c k", c=2),
                                                  ident[r, r][:, None, :].broadcast_to([HD, 2, HD]), ALU.add)
                            if par_ == 0:
                                chain.did(ins)
                        end(ins)
                    for s in range(2):
                        c = s if d == 0 else 1 - s
                        for hp in range(2):
                            b = take(T(f"s{s}", hp))
                            end(v.tensor_scalar(ST[:, hp, (v0 + s + 1) % 3, :], b[:, 0:P], LC[:, n % 2, hp, c:c + 1], None,
                                                ALU.mult))
                    for hp in range(2):
                        b = take(T("yy", hp))
                        o = yT[:, hp, P * j:P * j + P]
                        if d == 0:
                            end(v.tensor_copy(o, b[:, 0:P]))
                        else:
                            end(v.tensor_tensor(o, b[:, 0:P], o, ALU.add))
                    if kind == "c":
                        b = take(("so", l, d))
                        end(v.tensor_copy(s_fin[:, d], pair(b)))

                order.wait_emptied(ve, ("yy", l, STEPS[-1], 1))
                for ct in range(2):
                    for h in range(2):
                        b = take(("mu", l, ct, h))
                        cols = slice(HALF * h, HALF * (h + 1))
                        end(v.scalar_tensor_tensor(out=yT[:, ct, cols], in0=b[:, 0:HALF], scalar=-1.0 / HD, in1=yT[:, ct, cols],
                                                   op0=ALU.mult, op1=ALU.add))
                order.wait_emptied(ve, ("mu", l, 1, 1))
                ve.sem_inc(s_gn, 1)
                for ct in range(2):
                    for h in range(2):
                        order.wait_emptied(ve, ("var", l, ct, h))
                        part = tmp[:, ct, HALF * h:HALF * (h + 1)]
                        chain.did(v.reciprocal(part, part))
                    chain.settle()
                    chain.did(v.scalar_tensor_tensor(out=yT[:, ct, :], in0=yT[:, ct, :], scalar=pc("ln_w", ct),
                                                     in1=tmp[:, ct, :], op0=ALU.mult, op1=ALU.mult))
                    chain.settle()
                    chain.did(v.scalar_tensor_tensor(out=yT[:, ct, :], in0=yT[:, ct, :], scalar=pc("ln_b", ct),
                                                     in1=vT[:, ct, :], op0=ALU.add, op1=ALU.add))
                chain.settle()
                for ct in range(2):
                    for h in range(2):
                        b = take(("gup", l, ct, h))
                        cols = slice(HALF * h, HALF * (h + 1))
                        end(v.tensor_tensor(yT[:, ct, cols], b[:, 0:HALF], yT[:, ct, cols], ALU.mult))
                for dt in range(KT):
                    for h in range(2):
                        end(residual(take(("out", l, dt, h)), h, dt, 16))
                def low(k):
                    ve.wait_ge(s_hhi, k + 1)
                    v.tensor_tensor(hc[1][:, k, :], hT[:, k, :], f32(hc[0][:, k, :]), ALU.subtract).then_inc(s_hlo, 1)

                if l == 0:
                    dense_split(0)
                    norm(l, 2, low)
                else:
                    norm(l, 2)
                if l == 1:
                    three = lambda x: x[:, :, None].broadcast_to([P, NT, NE])
                    b = take(("router", l))
                    m = view(par_t, at[0] - 96, 3, NT)
                    end(v.tensor_copy(rt_t, b[:, 0:NT * NE].rearrange("p (j e) -> p j e", e=NE)))
                    order.wait_emptied(ve, ("router", l))
                    rank = cst("rank", NE)[:, None, :].broadcast_to([P, NT, NE])

                    def pick(dst, mx):
                        chain.did(v.tensor_reduce(out=mx, in_=rt_t, axis=AXX, op=ALU.max))
                        chain.settle()
                        chain.did(v.tensor_tensor(rt_key, rt_t, three(mx), ALU.is_equal))
                        chain.settle()
                        chain.did(v.tensor_tensor(rt_key, rt_key, rank, ALU.mult))
                        chain.settle()
                        chain.did(v.tensor_reduce(out=m[:, 2], in_=rt_key, axis=AXX, op=ALU.max))
                        chain.settle()
                        chain.did(v.tensor_tensor(dst, rt_key, three(m[:, 2]), ALU.is_equal))
                        chain.settle()

                    pick(rt_first, m[:, 0])
                    chain.did(v.tensor_tensor(rt_l, rt_t, three(m[:, 0]), ALU.subtract))
                    chain.did(v.scalar_tensor_tensor(out=rt_t, in0=rt_first, scalar=-3e38, in1=rt_t, op0=ALU.mult, op1=ALU.add))
                    chain.settle()
                    pick(rt_second, m[:, 1])
                    v.tensor_tensor(rt_first, rt_first, rt_second, ALU.add).then_inc(s_rmax, 1)

                    def low_parts(tiles):
                        for j, q in tiles:
                            b = take(("ht", j, q))
                            cols = slice(512 * q, 512 * (q + 1))
                            ve.wait_ge(s_hhi, KT + 2 * j + q + 1)
                            end(v.tensor_tensor(ht[1][:, j, cols], b[:, :], f32(ht[0][:, j, cols]), ALU.subtract))

                    low_parts(HT_EARLY)
                    ve.wait_ge(s_rmax, 1)
                    ve.wait_ge(s_rexp, 1)
                    chain.did(v.tensor_tensor(gates, rt_l, rt_first, ALU.mult))
                    chain.settle()
                    chain.did(v.tensor_reduce(out=m[:, 0], in_=gates, axis=AXX, op=ALU.add))
                    chain.settle()
                    chain.did(v.reciprocal(m[:, 0], m[:, 0]))
                    chain.settle()
                    chain.did(v.tensor_tensor(gates, gates, three(m[:, 0]), ALU.mult))
                    b = take(("pos", l))
                    chain.did(v.scalar_tensor_tensor(out=posm, in0=b[:, 0:NT * NE].rearrange("p (j e) -> p j e", e=NE),
                                                     scalar=1.0, in1=rt_first, op0=ALU.add, op1=ALU.mult))
                    end(v.tensor_reduce(out=rt_m[:, 0:1], in_=b[:, NT * NE:(NT + 1) * NE], axis=AXX, op=ALU.max))
                    order.wait_emptied(ve, ("pos", l))
                    chain.did(v.tensor_scalar(posm, posm, -1.0, None, ALU.add))
                    for i in range(1, MAX_ROUNDS):
                        chain.did(v.tensor_scalar(rt_m[:, i:i + 1], rt_m[:, 0:1], float(CAP * i), 1.0 if i == 1 else 0.0,
                                                  ALU.is_gt, ALU.add))
                    for i in range(2, MAX_ROUNDS):
                        chain.settle()
                        chain.did(v.tensor_tensor(rt_m[:, 1:2], rt_m[:, 1:2], rt_m[:, i:i + 1], ALU.add))
                    chain.settle()
                    v.tensor_copy(rounds_t[:, 0:1], rt_m[:, 1:2]).then_inc(s_rounds, 1)
                    low_parts(HT_LATE)
                    experts()
                else:
                    for n, (p, kind, i) in enumerate(chunks):
                        if n + 1 < len(chunks):
                            dense_split(n + 1)
                        if kind == "up":
                            u = DENSE_PARTS[p][0] + i
                            for h in range(2):
                                cols = slice(HALF * h, HALF * (h + 1))
                                order.wait_emptied(ve, ("du", p, i, 0, h))
                                b = take(("du", p, i, 1, h))
                                end(v.tensor_tensor(sil[:, u % 2, cols], b[:, 0:HALF], sil[:, u % 2, cols], ALU.mult))
                            ve.wait_ge(s_ghi, u + 1)
                            v.tensor_tensor(dg[1][:, i, :], sil[:, u % 2, :], f32(dg[0][:, i, :]), ALU.subtract).then_inc(s_glo, 1)
                        else:
                            for t in range(2):
                                for h in range(2):
                                    end(residual(take(("dn", p, i, t, h)), h, 2 * i + t, 40))
                        if 0 < n <= SUB_FIRST:
                            mod_take(1, n - 1)
                        if n < SUB_FIRST:
                            mod_sums(1, n)
            for j in range(NT):
                b = take(("y", j, 1))
                end(v.tensor_copy(x_tok[:, j, 512:1024], b[:, :]))

        @block.gpsimd
        def _(pool):
            chain = Chain(pool, s_cp)
            g = nc.gpsimd
            pool.wait_ge(s_tables, 16)
            for l in range(DEPTH):
                if l > 0:
                    order.wait_emptied(pool, ("dn", len(DENSE_PARTS) - 1, 3, 1, 1))
                g.memset(rank_up, 0.0).then_inc(s_zero, 1)
                pool.wait_ge(s_qk, l * NT + 1)
                g.dma_start(new_k[0, l].rearrange("t h d -> t (h d)"), qkv[:, 0, 256:384]).then_inc(s_kv_out, 16)
                g.dma_start(new_v[0, l].rearrange("t h d -> t (h d)"), qkv[:, 0, 384:512]).then_inc(s_kv_out, 16)
                for j in range(1, NT):
                    pool.wait_ge(s_qk, l * NT + j + 1)
                    x = qkv[:, j, 0:384].rearrange("p (h s d) -> p h s d", s=4, d=16)
                    x1, x2 = x[:, :, 0::2, :], x[:, :, 1::2, :]
                    tab = lambda name: cst(name, 32, 32 * (j - 1)).rearrange("p (s d) -> p s d", s=2)[:, None, :, :] \
                        .broadcast_to([P, 6, 2, 16])
                    r = [rope[:, i] for i in range(4)]
                    chain.settle()
                    for t, xx, name in ((0, x1, "cos"), (1, x2, "sin"), (2, x2, "cos"), (3, x1, "sin")):
                        chain.did(g.tensor_tensor(r[t], xx, tab(name), ALU.mult))
                    chain.settle()
                    chain.did(g.tensor_tensor(x1, r[0], r[1], ALU.subtract))
                    g.tensor_tensor(x2, r[2], r[3], ALU.add).then_inc(s_rope, 1)
                    pool.wait_ge(s_rope, l * (NT - 1) + j)
                for name in ("bx", "bc"):
                    for ct in range(2):
                        for h in range(2):
                            order.wait_emptied(pool, ("in", l, (name, ct), h))
                chain.did(g.memset(conv_u, 0.0))
                chain.settle()
                chain.did(g.tensor_tensor(conv_u[:, :, 1:1 + CTX], bcT[:, :, 0:CTX], bxT[:, :, 0:CTX], ALU.mult))
                g.tensor_tensor(conv_u[:, :, 3 + CTX:3 + TOK], bcT[:, :, CTX:TOK], bxT[:, :, CTX:TOK], ALU.mult).then_inc(s_cu, 1)
                order.wait_filled(pool, ("up", l, 1, 1, 1, 1))
                pool.wait_ge(s_nkk, l + 1)
                for buf in (BP, KP, s0_in):
                    chain.did(g.memset(buf, 0.0))
                chain.settle()
                for d in range(2):
                    for h in range(4):
                        r = slice(HD * (h % 2), HD * (h % 2) + HD)
                        g.dma_start(s0_in[r, d, h // 2, r], a["state_wkv"][0, l, d, h]).then_inc(s_state, 16)
                pool.wait_ge(s_nkk, l + 1)
                for n, step in enumerate(STEPS):
                    kind, i, d = step
                    j = step_tile(step)
                    gn = l * len(STEPS) + n
                    cols = slice(P * j, P * j + P)
                    E = EX[n % 2]
                    pool.wait_ge(s_ex, gn + 1)
                    if n > 0:
                        order.wait_filled(pool, ("tb", l, STEPS[n - 1], 1))
                        if n > 1:
                            order.wait_emptied(pool, ("s1", l, STEPS[n - 2], 1))
                    e0 = CH - 1 if d == 0 else 0
                    chain.did(g.tensor_copy(LC[:, n % 2], E[:, :, 1, e0::CH]))
                    chain.did(g.tensor_tensor(BT, kkT[:, :, cols], aT[:, d, :, cols], ALU.mult))
                    for ct in range(2):
                        chain.did(g.tensor_scalar(KD[:, ct], aT[:, d, ct, cols], pc("k_a", ct), omka[:, ct:ct + 1],
                                                  ALU.mult, ALU.add))
                    chain.did(g.tensor_tensor(E[:, :, 0, :], E[:, :, 0, :], kkT[:, :, cols], ALU.mult))
                    chain.settle()
                    chain.did(g.tensor_tensor(E[:, :, 1, :], E[:, :, 1, :], rT[:, :, cols], ALU.mult))
                    chain.did(g.tensor_tensor(KD, KD, kT_[:, :, cols], ALU.mult))
                    chain.did(g.tensor_tensor(BT, BT, E[:, :, 2, :], ALU.mult))
                    chain.settle()
                    chain.did(g.tensor_tensor(KD, KD, E[:, :, 2, :], ALU.mult))
                    chain.settle()
                    for q in range(2):
                        r = slice(HD * q, HD * q + HD)
                        chain.did(g.tensor_copy(BP[r, :, q, :], BT[r, :, :]))
                        chain.did(g.tensor_copy(KP[r, :, q, :], KD[r, :, :]))
                    chain.settle()
                    pool.sem_inc(s_pad, 1)
                    if n == 0:
                        order.wait_filled(pool, ("ot", l, NT - 1))
                        pool.wait_ge(s_kv_out, 32 * (l + 1))
                        for buf in (BM, BC, KC):
                            chain.did(g.memset(buf, 0.0))
                        chain.settle()
                        pool.sem_inc(s_zero2, 1)
                    for hp in range(2):
                        order.wait_emptied(pool, ("ab", l, step, hp))
                    four = lambda B: B.rearrange("p a b c -> p (a b) c")
                    N = AB.rearrange("p a b c -> p (a b) c")[:, :, 0:P]
                    mask = lambda name: cst(name, P, P * d)[:, None, :].broadcast_to([P, 4, P])
                    g.tensor_tensor(four(ND), N, mask("m16"), ALU.mult).then_inc(s_tri, 1)
                    pool.wait_ge(s_tri, 2 * gn + 1)
                    chain.did(g.tensor_tensor(four(XA), four(ND), ident[:, None, :].broadcast_to([P, 4, P]), ALU.add))
                    chain.did(g.tensor_tensor(four(O32), N, mask("m32"), ALU.mult))
                    chain.did(g.tensor_tensor(four(O64), N, mask("m64"), ALU.mult))
                    chain.settle()
                    pool.sem_inc(s_tri, 1)
                    if n == 2:
                        for dd in range(2):
                            order.wait_emptied(pool, ("so", l, dd))
                            for h in range(4):
                                r = slice(HD * (h % 2), HD * (h % 2) + HD)
                                g.dma_start(new_s[0, l, dd, h], s_fin[r, dd, h // 2, r]).then_inc(s_state_out, 16)


def kernel(**inputs):
    from concourse import bacc
    from concourse.bass_utils import run_bass_kernel_spmd

    nc = bacc.Bacc("TRN2", target_bir_lowering=False, num_devices=1)
    const, dft = constants()
    arrays = {name: np.ascontiguousarray(x) for name, x in inputs.items()}
    arrays["const"], arrays["dft"] = const, dft
    aps = {name: nc.dram_tensor(f"in_{name}", x.shape, F32, kind="ExternalInput").ap() for name, x in arrays.items()}
    shapes = [(1, CTX, D), (1, LAT, D), (1, DEPTH, CTX, NKV, HD), (1, DEPTH, CTX, NKV, HD), (1, DEPTH, 2, 4, HD, HD)]
    outs = [nc.dram_tensor(f"out_{i}", s, F32, kind="ExternalOutput").ap() for i, s in enumerate(shapes)]
    build(nc, aps, outs)
    r = run_bass_kernel_spmd(nc, [{f"in_{name}": x for name, x in arrays.items()}], core_ids=[0])
    return tuple(r.results[0][f"out_{i}"] for i in range(len(shapes)))
```
